# Optimizing a Trainium2 kernel written in Bass

```python
import math
import jax, jax.numpy as jnp
from jax import lax
import numpy as np

D_MODEL = 1024
BATCH = 1
SEQ = 1024
DEPTH = 1
DEC_BATCH = 8
DEC_SEQ = 8
PAST_LEN = 2048
PAGE_SIZE = 128

HEAD_DIM = 64
A_GROUPS = ((128, 1), (512, 4), (2048, 16))
A_HEADS = 8
A_WIDTH = A_HEADS * HEAD_DIM
A_QKV = len(A_GROUPS) * A_WIDTH
B_HEADS = 4
B_QK = 2 * HEAD_DIM
B_VD = 2 * HEAD_DIM
B_WIDTH = B_HEADS * B_VD
IN_WIDTH = 3 * A_QKV + A_WIDTH + 3 * B_WIDTH + B_WIDTH + 2 * D_MODEL
Q_BLOCK = 128
EPS = 1e-6

kernel_name = "dilated_diff_attention_hybrid_step"

def alibi_slopes(n):
    return jnp.asarray(2.0 ** (-8.0 * np.arange(1, n + 1) / n), dtype=jnp.float32)

def rms_norm(x, g):
    xf = x.astype(jnp.float32)
    y = xf * lax.rsqrt(jnp.mean(xf * xf, axis=-1, keepdims=True) + EPS)
    return y * g.astype(jnp.float32)

def softmax_with_lse(scores, valid):
    scores = jnp.where(valid, scores, -jnp.inf)
    m = jnp.max(scores, axis=-1, keepdims=True)
    p = jnp.exp(scores - m)
    l = jnp.sum(p, axis=-1, keepdims=True)
    return p / l, (m + jnp.log(l))[..., 0]

def mixer_inputs(x, norm_g, w_in, q_norm_a, k_norm_a, q_norm_b, k_norm_b):
    b, s, _ = x.shape
    G = len(A_GROUPS)
    h = rms_norm(x, norm_g).astype(x.dtype)
    z = jnp.einsum('bsd,de->bse', h, w_in)
    sizes = [A_QKV, A_QKV, A_QKV, A_WIDTH, B_WIDTH, B_WIDTH, B_WIDTH, B_WIDTH, D_MODEL, D_MODEL]
    offs = [int(o) for o in np.cumsum(sizes)[:-1]]
    qa, ka, va, ga, qb, kb, vb, gb, ma, mb = jnp.split(z, offs, axis=-1)
    qa = rms_norm(qa.reshape(b, s, G, A_HEADS, HEAD_DIM), q_norm_a)
    ka = rms_norm(ka.reshape(b, s, G, A_HEADS, HEAD_DIM), k_norm_a)
    va = va.reshape(b, s, G, A_HEADS, HEAD_DIM).astype(jnp.float32)
    qb = rms_norm(qb.reshape(b, s, B_HEADS, 2, HEAD_DIM), q_norm_b)
    kb = rms_norm(kb.reshape(b, s, B_HEADS, 2, HEAD_DIM), k_norm_b)
    vb = vb.reshape(b, s, B_HEADS, B_VD).astype(jnp.float32)
    return qa, ka, va, ga, qb, kb, vb, gb, ma, mb

def dilated_window_prompt(q, k, v, window, dilation, slopes):
    bsz, s, h, d = q.shape
    n = window // dilation
    unit = dilation * n
    sp = -(-s // unit) * unit
    nb = sp // unit

    def to_sub(t):
        t = jnp.pad(t, ((0, 0), (0, sp - s), (0, 0), (0, 0)))
        t = t.reshape(bsz, sp // dilation, dilation, h, d).transpose(0, 2, 1, 3, 4)
        return t.reshape(bsz, dilation, nb, n, h, d)

    def prev_block(t):
        return jnp.pad(t, ((0, 0), (0, 0), (1, 0), (0, 0), (0, 0), (0, 0)))[:, :, :-1]

    qs, ks, vs = to_sub(q), to_sub(k), to_sub(v)
    kk = jnp.concatenate([prev_block(ks), ks], axis=3)
    vv = jnp.concatenate([prev_block(vs), vs], axis=3)
    scores = jnp.einsum('brnihd,brnjhd->brnhij', qs, kk) * (d ** -0.5)
    i = jnp.arange(n)[:, None]
    j = jnp.arange(2 * n)[None, :]
    dist = i + n - j
    band = (dist >= 0) & (dist <= n)
    exists = (jnp.arange(nb)[:, None, None] > 0) | (j[None] >= n)
    valid = band[None] & exists
    bias = -slopes[:, None, None] * (dist * dilation).astype(jnp.float32)[None]
    p, lse = softmax_with_lse(scores + bias, valid[None, None, :, None])
    out = jnp.einsum('brnhij,brnjhd->brnihd', p, vv)
    out = out.reshape(bsz, dilation, nb * n, h, d).transpose(0, 2, 1, 3, 4).reshape(bsz, sp, h, d)[:, :s]
    lse = lse.transpose(0, 1, 2, 4, 3).reshape(bsz, dilation, nb * n, h)
    lse = lse.transpose(0, 2, 1, 3).reshape(bsz, sp, h)[:, :s]
    return out, lse

def dilated_window_sample(q, k_ext, v_ext, window, dilation, slopes):
    bsz, t, h, d = q.shape
    L = k_ext.shape[1] - t
    n = window // dilation
    steps = jnp.arange(n + 1)
    idx = L + jnp.arange(t)[:, None] - steps[None, :] * dilation
    valid = idx >= 0
    idxc = jnp.maximum(idx, 0)
    kg = k_ext[:, idxc]
    vg = v_ext[:, idxc]
    scores = jnp.einsum('bthd,btshd->bhts', q, kg) * (d ** -0.5)
    bias = -slopes[:, None, None] * (steps * dilation).astype(jnp.float32)[None, None, :]
    p, lse = softmax_with_lse(scores + bias[None], valid[None, None])
    out = jnp.einsum('bhts,btshd->bthd', p, vg)
    return out, lse.transpose(0, 2, 1)

def combine_groups(outs, lses):
    w = jax.nn.softmax(jnp.stack(lses, axis=0), axis=0)
    return jnp.sum(w[..., None] * jnp.stack(outs, axis=0), axis=0)

def diff_attention(q, k, v, q_pos, k_pos, lam, slopes):
    d = q.shape[-1]
    scores = jnp.einsum('bqhcd,bkhcd->bhcqk', q, k) * (d ** -0.5)
    rel = q_pos[:, None] - k_pos[None, :]
    scores = scores - slopes[:, None, None, None] * rel.astype(jnp.float32)
    p, _ = softmax_with_lse(scores, rel >= 0)
    a = p[:, :, 0] - lam * p[:, :, 1]
    return jnp.einsum('bhqk,bkhe->bqhe', a, v)

def diff_attention_prompt(q, k, v, lam, slopes):
    bsz, s = q.shape[:2]
    nqb = s // Q_BLOCK
    qb = q.reshape((bsz, nqb, Q_BLOCK) + q.shape[2:]).swapaxes(0, 1)
    k_pos = jnp.arange(s)

    def block(args):
        qi, bi = args
        q_pos = bi * Q_BLOCK + jnp.arange(Q_BLOCK)
        return diff_attention(qi, k, v, q_pos, k_pos, lam, slopes)

    out = lax.map(block, (qb, jnp.arange(nqb)))
    return out.swapaxes(0, 1).reshape(bsz, s, B_HEADS, B_VD)

def merge_branches(x, o_a, ga, o_b, gb, ma, mb, subln_g, lam_init, w_proj_a, w_proj_b, w_out):
    b, s, _ = x.shape
    f32 = jnp.float32
    o_b = rms_norm(o_b, subln_g) * (1.0 - lam_init)
    ya = (o_a.reshape(b, s, A_WIDTH) * jax.nn.silu(ga.astype(f32))).astype(x.dtype)
    yb = (o_b.reshape(b, s, B_WIDTH) * jax.nn.silu(gb.astype(f32))).astype(x.dtype)
    pa = jnp.einsum('bse,ed->bsd', ya, w_proj_a)
    pb = jnp.einsum('bse,ed->bsd', yb, w_proj_b)
    m = jax.nn.sigmoid(ma.astype(f32)) * pa + jax.nn.sigmoid(mb.astype(f32)) * pb
    return x + jnp.einsum('bsd,de->bse', m.astype(x.dtype), w_out).astype(x.dtype)

def setup_inputs(seed: int = 0) -> dict:
    key = jax.random.key(seed)
    ks = jax.random.split(key, 24)
    f32 = jnp.float32
    n_pages = PAST_LEN // PAGE_SIZE
    n_used = DEC_BATCH * n_pages
    n_phys = n_used + max(1, n_used // 4)

    def nrm(k, shape, scale):
        return scale * jax.random.normal(k, shape, f32)

    return {
        "x_prompt": nrm(ks[0], (BATCH, SEQ, D_MODEL), 1.0),
        "x_sample": nrm(ks[1], (DEC_BATCH, DEC_SEQ, D_MODEL), 1.0),
        "cache_a0_kv": nrm(ks[2], (DEPTH, DEC_BATCH, min(A_GROUPS[0][0], PAST_LEN), 2, A_HEADS, HEAD_DIM), 1.0),
        "cache_a1_kv": nrm(ks[3], (DEPTH, DEC_BATCH, min(A_GROUPS[1][0], PAST_LEN), 2, A_HEADS, HEAD_DIM), 1.0),
        "cache_a2_kv": nrm(ks[4], (DEPTH, DEC_BATCH, min(A_GROUPS[2][0], PAST_LEN), 2, A_HEADS, HEAD_DIM), 1.0),
        "cache_b_kv": nrm(ks[5], (DEPTH, n_phys, PAGE_SIZE, 2, B_HEADS, B_VD), 1.0),
        "page_table": jax.random.permutation(ks[6], n_phys)[:n_used].reshape(DEC_BATCH, n_pages).astype(jnp.int32),
        "norm_g": 1.0 + nrm(ks[7], (DEPTH, D_MODEL), 0.02),
        "w_in": nrm(ks[8], (DEPTH, D_MODEL, IN_WIDTH), D_MODEL ** -0.5),
        "q_norm_a": 1.0 + nrm(ks[9], (DEPTH, HEAD_DIM), 0.02),
        "k_norm_a": 1.0 + nrm(ks[10], (DEPTH, HEAD_DIM), 0.02),
        "q_norm_b": 1.0 + nrm(ks[11], (DEPTH, HEAD_DIM), 0.02),
        "k_norm_b": 1.0 + nrm(ks[12], (DEPTH, HEAD_DIM), 0.02),
        "lambda_q1": nrm(ks[13], (DEPTH, HEAD_DIM), 0.1),
        "lambda_k1": nrm(ks[14], (DEPTH, HEAD_DIM), 0.1),
        "lambda_q2": nrm(ks[15], (DEPTH, HEAD_DIM), 0.1),
        "lambda_k2": nrm(ks[16], (DEPTH, HEAD_DIM), 0.1),
        "subln_g": 1.0 + nrm(ks[17], (DEPTH, B_VD), 0.02),
        "w_proj_a": nrm(ks[18], (DEPTH, A_WIDTH, D_MODEL), A_WIDTH ** -0.5),
        "w_proj_b": nrm(ks[19], (DEPTH, B_WIDTH, D_MODEL), B_WIDTH ** -0.5),
        "w_out": nrm(ks[20], (DEPTH, D_MODEL, D_MODEL), D_MODEL ** -0.5),
    }

def reference(x_prompt, x_sample, cache_a0_kv, cache_a1_kv, cache_a2_kv, cache_b_kv, page_table,
              norm_g, w_in, q_norm_a, k_norm_a, q_norm_b, k_norm_b,
              lambda_q1, lambda_k1, lambda_q2, lambda_k2, subln_g, w_proj_a, w_proj_b, w_out):
    f32 = jnp.float32
    G = len(A_GROUPS)
    slopes_a = alibi_slopes(G * A_HEADS).reshape(G, A_HEADS)
    slopes_b = alibi_slopes(B_HEADS)
    a_caches = (cache_a0_kv, cache_a1_kv, cache_a2_kv)
    new_p = [[] for _ in range(G + 1)]
    new_s = [[] for _ in range(G + 1)]
    xp, xs = x_prompt, x_sample
    for l in range(DEPTH):
        lam_init = 0.8 - 0.6 * math.exp(-0.3 * l)
        lam = (jnp.exp(jnp.sum(lambda_q1[l].astype(f32) * lambda_k1[l].astype(f32)))
               - jnp.exp(jnp.sum(lambda_q2[l].astype(f32) * lambda_k2[l].astype(f32))) + lam_init)
        norm_args = (norm_g[l], w_in[l], q_norm_a[l], k_norm_a[l], q_norm_b[l], k_norm_b[l])
        out_args = (subln_g[l], lam_init, w_proj_a[l], w_proj_b[l], w_out[l])

        b, s, _ = xp.shape
        qa, ka, va, ga, qb, kb, vb, gb, ma, mb = mixer_inputs(xp, *norm_args)
        outs, lses = [], []
        for g, (win, dil) in enumerate(A_GROUPS):
            o, lse = dilated_window_prompt(qa[:, :, g], ka[:, :, g], va[:, :, g], win, dil, slopes_a[g])
            outs.append(o)
            lses.append(lse)
            keep = min(win, s)
            new_p[g].append(jnp.stack([ka[:, s - keep:, g], va[:, s - keep:, g]], axis=2).astype(xp.dtype))
        o_a = combine_groups(outs, lses)
        o_b = diff_attention_prompt(qb, kb, vb, lam, slopes_b)
        new_p[G].append(jnp.stack([kb.reshape(b, s, B_HEADS, B_QK), vb], axis=2).astype(xp.dtype))
        yp = merge_branches(xp, o_a, ga, o_b, gb, ma, mb, *out_args)

        db, t, _ = xs.shape
        qa, ka, va, ga, qb, kb, vb, gb, ma, mb = mixer_inputs(xs, *norm_args)
        outs, lses = [], []
        for g, (win, dil) in enumerate(A_GROUPS):
            buf = a_caches[g][l].astype(f32)
            k_ext = jnp.concatenate([buf[:, :, 0], ka[:, :, g]], axis=1)
            v_ext = jnp.concatenate([buf[:, :, 1], va[:, :, g]], axis=1)
            o, lse = dilated_window_sample(qa[:, :, g], k_ext, v_ext, win, dil, slopes_a[g])
            outs.append(o)
            lses.append(lse)
            total = k_ext.shape[1]
            keep = min(win, total)
            new_s[g].append(jnp.stack([k_ext[:, total - keep:], v_ext[:, total - keep:]], axis=2).astype(a_caches[g].dtype))
        o_a = combine_groups(outs, lses)
        pages = cache_b_kv[l][page_table]
        n_pages, page = pages.shape[1], pages.shape[2]
        past_len = n_pages * page
        past = pages.reshape(db, past_len, 2, B_HEADS, B_VD).astype(f32)
        k_all = jnp.concatenate([past[:, :, 0].reshape(db, past_len, B_HEADS, 2, HEAD_DIM), kb], axis=1)
        v_all = jnp.concatenate([past[:, :, 1], vb], axis=1)
        o_b = diff_attention(qb, k_all, v_all, past_len + jnp.arange(t), jnp.arange(past_len + t), lam, slopes_b)
        new_s[G].append(jnp.stack([kb.reshape(db, t, B_HEADS, B_QK), vb], axis=2).astype(cache_b_kv.dtype))
        ys = merge_branches(xs, o_a, ga, o_b, gb, ma, mb, *out_args)

        xp, xs = yp, ys

    new_a0_prompt = jnp.stack(new_p[0], axis=0)
    new_a1_prompt = jnp.stack(new_p[1], axis=0)
    new_a2_prompt = jnp.stack(new_p[2], axis=0)
    new_b_prompt = jnp.stack(new_p[3], axis=0)
    new_a0_sample = jnp.stack(new_s[0], axis=0)
    new_a1_sample = jnp.stack(new_s[1], axis=0)
    new_a2_sample = jnp.stack(new_s[2], axis=0)
    new_b_sample = jnp.stack(new_s[3], axis=0)
    return (xp, xs, new_a0_prompt, new_a1_prompt, new_a2_prompt, new_b_prompt,
            new_a0_sample, new_a1_sample, new_a2_sample, new_b_sample)


_drawn_inputs = setup_inputs


def setup_inputs(seed=0):
    import zlib

    import numpy as np

    out = dict(_drawn_inputs(seed))
    spreads = {}
    factors = {'norm_g': 2.835,
     'q_norm_a': 8.0,
     'k_norm_a': 3.612,
     'q_norm_b': 8.0,
     'k_norm_b': 4.374,
     'lambda_q1': 4.039,
     'lambda_k1': 6.134,
     'lambda_q2': 3.978,
     'lambda_k2': 5.519,
     'subln_g': 8.0}
    for name, (base, spread) in spreads.items():
        noise = np.random.default_rng([zlib.crc32(name.encode()), seed]).standard_normal(out[name].shape)
        drawn = base * np.exp(spread * noise) if base else spread * noise
        out[name] = __import__('jax').numpy.asarray(drawn.astype(out[name].dtype))
    for name, factor in factors.items():
        out[name] = (out[name] * factor).astype(out[name].dtype)
    return out
```

```python
from contextlib import ExitStack

import numpy as np

import concourse.bass as bass
from concourse import mybir

ALU = mybir.AluOpType
ACT = mybir.ActivationFunctionType
AX_X = mybir.AxisListType.X
F32 = mybir.dt.float32
F32R = mybir.dt.float32r
I32 = mybir.dt.int32

P = 128
D_MODEL = 1024
SEQ = 1024
DEC_B = 8
DEC_T = 8
NS = DEC_B * DEC_T
ROWS = SEQ + NS
HD = 64
WINDOWS = ((128, 1), (512, 4), (2048, 16))
PAST = 2048
PAGE = 128
N_PAGES = PAST // PAGE
A_HEADS = 8
B_HEADS = 4
CW = 512
EPS = 1e-6
LAM_INIT = 0.2
MASKED = 1e30
NT = SEQ // P
TILES = NT + 1
NC = CW // P
KC = D_MODEL // P
NEW_A = 3 * (P + DEC_T)
KEYS_B = PAST + DEC_T

A_QKV = len(WINDOWS) * CW
COL = dict(qa=0, ka=A_QKV, va=2 * A_QKV, ga=3 * A_QKV, qb=3 * A_QKV + CW, kb=3 * A_QKV + 2 * CW,
           vb=3 * A_QKV + 3 * CW, gb=3 * A_QKV + 4 * CW, ma=3 * A_QKV + 5 * CW,
           mb=3 * A_QKV + 5 * CW + D_MODEL)


def weight_blocks():
    blocks = []
    for part, kind in (("qb", "q"), ("kb", "k"), ("vb", "v")):
        blocks.append((kind, 0, "in", COL[part], KC))
    for g in range(3):
        for part, kind in (("qa", "q"), ("ka", "k"), ("va", "v")):
            blocks.append((kind, g + 1, "in", COL[part] + g * CW, KC))
    for br in ("a", "b"):
        blocks.append(("g" + br, 0, "in", COL["g" + br], KC))
        for half in range(2):
            blocks.append(("m" + br, half, "in", COL["m" + br] + half * CW, KC))
            blocks.append(("p" + br, half, "proj_" + br, half * CW, NC))
    for half in range(2):
        blocks.append(("out", half, "out", half * CW, KC))
    return blocks


def width_a(G, i):
    if G == 1:
        return P if i == 0 else 2 * P
    if G == 2:
        return 2 * P if i % 2 else P
    return P


def pieces_of(i):
    if i < 4:
        return [(i, 0, i + 1)]
    return [(2 * i - 4, 0, 4), (2 * i - 3, 4, i - 3)]


def pieces_before(i):
    return i if i <= 4 else 2 * i - 4


def build_step(nc, x_p, x_s, ca, cb, page_table, norm_g, w_in, qna, kna, qnb, knb, lq1, lk1, lq2, lk2,
               subln, w_pa, w_pb, w_o, c_ident, c_bias_a, c_bias_b, c_bias_sa, c_bias_sb, c_mask, c_sel,
               c_coef, y_p, y_s, na_p, nb_p, na_s, nb_s):
    ds = bass.ds
    U = weight_blocks()
    w_dram = {"in": w_in[0], "proj_a": w_pa[0], "proj_b": w_pb[0], "out": w_o[0]}
    first_chunk = [0]
    for blk in U:
        first_chunk.append(first_chunk[-1] + blk[4])
    n_phys = cb.shape[1]
    FIRST_GATE = 12
    U_OUT = 22

    def nrows(i):
        return P if i < NT else NS

    with ExitStack() as ctx:
        def sem(name):
            return ctx.enter_context(nc.semaphore(name))

        def dram(name, shape):
            return nc.dram_tensor(name, shape, F32, kind="Internal").ap()

        top = [(nc.sbuf_base + 63) // 64 * 64]

        def place(name, shape, dt=F32, at=None):
            size = 4 * int(np.prod(shape[1:]))
            off = top[0] if at is None else at[0]
            t = nc.alloc_sbuf_tensor_at(name, list(shape), dt, offset=off)
            (top if at is None else at)[0] = off + (size + 31) // 32 * 32
            return t

        hT_hi = place("hT_hi", [P, KC, ROWS], F32R)
        hT_lo = place("hT_lo", [P, KC, ROWS], F32R)
        ident = place("ident", [P, P])
        gcol = place("gcol", [P, KC])
        qcol = place("qcol", [P, 2])
        krow = place("krow", [P, 2, HD])
        lamv = place("lamv", [P, 4, HD])
        lam = place("lam", [P, 8])
        subrow = place("subrow", [P, P])
        half_pow = place("half_pow", [P, 8])
        ss = place("ss", [P, 2, 8])
        rs = place("rs", [P, 2, 8])
        qTs = place("qTs", [P, 4, NC, NS])
        coef = place("coef", [NS, 2])
        st_sum = place("st_sum", [P, 2, 2, 16])
        st = place("st", [P, NT, 16])
        rlB = place("rlB", [P, 2, NT, 2])
        wB = place("wB", [P, 2, NT])
        sc_s = place("sc_s", [NS, 16])
        w_base = top[0]
        raw = place("raw", [P, 4, CW])
        w_hi, w_lo, set_at = [], [], []
        for s in range(2):
            set_at.append(top[0])
            w_hi.append(place(f"w_hi{s}", [P, KC, CW], F32R))
            w_lo.append(place(f"w_lo{s}", [P, KC, CW], F32R))
        q_base = top[0]
        qT = place("qT", [P, NC * SEQ])
        kT = place("kT", [P, NC * SEQ])
        v_sb = place("v_sb", [P, TILES, CW])
        work = top[0]
        zn = place("zn", [P, 2, CW])
        kn = place("kn", [P, 3, CW])
        end = top[0]
        assert end <= nc.sbuf_usable_end, end
        at = [q_base]
        xt = place("xt", [P, 2, D_MODEL], at=at)
        xn = place("xn", [P, 2, D_MODEL], at=at)
        hn = place("hn", [P, 2, CW], at=at)
        at = [work]
        qz = place("qz", [P, 2, SEQ], at=at)
        att = []
        for s in range(2):
            at = [set_at[s]]
            a = dict(sB=place(f"sB{s}", [P, 4, SEQ], at=at), tB=place(f"tB{s}", [P, 2, SEQ], at=at),
                     ptB=place(f"ptB{s}", [P, 2, CW], at=at))
            at = [set_at[s]]
            a |= dict(sA=place(f"sA{s}", [P, 4, 256], at=at), tA=place(f"tA{s}", [P, 2, 2, 256], at=at),
                      ptA=place(f"ptA{s}", [P, 3, 256], at=at))
            att.append(a)
        NKS, NVS = 8, 20
        at = [w_base]
        k_in = place("k_in", [P, NKS, CW], at=at)
        v_in = place("v_in", [P, NVS, CW], at=at)
        new_and_out = place("new_and_out", [P, 2, 4, CW], at=at)
        kv_new = new_and_out[0:DEC_T]
        os_ = new_and_out[HD:HD + DEC_T, 0, 0:2, :]
        q_all = place("q_all", [P, 4, NC, NS], at=at)
        q_g1 = place("q_g1", [P, 4, NC, NS], at=at)
        q_g2 = place("q_g2", [P, 8, NC, NS], at=at)
        kTs = place("kTs", [P, 2, NC, P], at=at)
        kTn = place("kTn", [P, 16, DEC_T], at=at)
        s_a = place("s_a", [NS, NEW_A], at=at)
        bias_sa = place("bias_sa", [NS, NEW_A], at=at)
        s_b = place("s_b", [NS, KEYS_B], at=at)
        bias_sb = place("bias_sb", [NS, KEYS_B], at=at)
        pT0 = place("pT0", [P, NS], at=at)
        pT1 = place("pT1", [P, 4, NS], at=at)
        pT2 = place("pT2", [P, 8, NS], at=at)
        pTn = place("pTn", [DEC_T, 4, NS], at=at)
        pTb = place("pTb", [P, N_PAGES, NS], at=at)
        mask = place("mask", [NS, 2, CW], at=at)
        om = place("om", [NS, 2, CW], at=at)
        sel = place("sel", [NS, DEC_T], at=at)
        pids = place("pids", [1, DEC_B * N_PAGES], I32, at=at)
        assert at[0] <= end, (at[0], end)
        at = [q_base]
        yT_hi = place("yT_hi", [P, NC, ROWS], F32R, at=at)
        yT_lo = place("yT_lo", [P, NC, ROWS], F32R, at=at)
        sig_at = at[0]
        sig = place("sig", [P, TILES, CW], at=at)
        zy = place("zy", [P, 2, CW], at=at)
        stc = place("stc", [P, NT, 3, 16], at=at)
        ew = place("ew", [P, NT, 3, 8], at=at)
        el = place("el", [P, NT, 3, 8], at=at)
        nmin = place("nmin", [P, NT, 8], at=at)
        den = place("den", [P, NT, 8], at=at)
        assert at[0] <= end, (at[0], end)
        at = [sig_at]
        og = place("og", [P, 2, 3, CW], at=at)
        sg = place("sg", [P, 2, CW], at=at)
        at = [q_base]
        mt = place("mt", [P, 2, D_MODEL], at=at)
        xl = place("xl", [P, 2, CW], at=at)
        yo = place("yo", [P, 3, CW], at=at)

        ps = ctx.enter_context(nc.psum_tensor("ps", [P, 8 * CW], F32))

        def bank(b, n=1):
            return ps[:, b * CW:(b + n) * CW]

        o_scr = [dram(f"o_scr{g}", [SEQ, CW]) for g in range(4)]
        st_scr = [dram(f"st_scr{g}", [SEQ, 16]) for g in range(3)]
        os_scr = dram("os_scr", [2, NS, CW])
        ma_scr = dram("ma_scr", [ROWS, D_MODEL])
        m_scr = dram("m_scr", [ROWS, D_MODEL])

        const_in = sem("const_in")
        setup = sem("setup")
        x_in = [sem(f"x_in{s}") for s in range(2)]
        h_ss, h_rs, h_xn, h_t, h_hn, h_hi, h_lo = (sem(n) for n in (
            "h_ss", "h_rs", "h_xn", "h_t", "h_hn", "h_hi", "h_lo"))
        pool_step = sem("pool_step")
        dve_step = sem("dve_step")
        raw_in = [sem(f"raw_in{s}") for s in range(4)]
        hi_done, lo_done = sem("hi_done"), sem("lo_done")
        z_ready = sem("z_ready")
        sq_ready, ss_ready, rs_ready = sem("sq_ready"), sem("ss_ready"), sem("rs_ready")
        zn_ready, kn_ready, v_ready = sem("zn_ready"), sem("kn_ready"), sem("v_ready")
        t_ready, t_moved = sem("t_ready"), sem("t_moved")
        k_out = [sem(f"k_out{s}") for s in range(3)]
        v_out, o_out = sem("v_out"), sem("o_out")
        copies = sem("copies")
        bq, bs, be, ba, bt, bm, bp, bo, bw, btab = (sem(n) for n in (
            "b_scores", "b_biased", "b_exp", "b_diff", "b_probsT", "b_probsT_moved", "b_piece_used",
            "b_stored", "b_weight", "b_table"))
        aq, as_, ae, atp, am, av, ao, ast, atab = (sem(n) for n in (
            "a_scores", "a_biased", "a_exp", "a_probsT", "a_probsT_moved", "a_values", "a_stored",
            "a_stats", "a_table"))
        btab2, atab2 = sem("b_table1"), sem("a_table1")
        qz_ready = sem("qz_ready")
        s_const = sem("s_const")
        sk_in = [sem(f"sk_in{s}") for s in range(NKS)]
        sv_in = [sem(f"sv_in{s}") for s in range(NVS)]
        sn_in, sq_b = sem("sn_in"), sem("s_queries")
        s_kt, s_km, s_qk, s_nt, s_nm = (sem(n) for n in (
            "s_keysT", "s_keysT_moved", "s_scored", "s_newT", "s_newT_moved"))
        s_ta, s_tb, s_min, s_ea, s_eb = (sem(n) for n in (
            "s_biased_a", "s_biased_b", "s_min_b", "s_exp_a", "s_exp_b"))
        s_pa, s_pam, s_pb, s_pbm = (sem(n) for n in (
            "s_probsT_a", "s_probsT_a_moved", "s_probsT_b", "s_probsT_b_moved"))
        s_pv, s_va, s_vb, s_om, s_sel, s_oc, s_out, s_rec = (sem(n) for n in (
            "s_tile_used", "s_values_a", "s_values_b", "s_masked", "s_summed", "s_o_copied", "s_o_out",
            "s_recip"))
        s_zero = sem("s_zero")
        st_in, ew_ready, ew_exp = sem("st_in"), sem("ew_ready"), sem("ew_exp")
        og_in = [sem(f"og_in{s}") for s in range(2)]
        sg_ready, silu_ready, og_pool, y_ready, y_t, y_hi, y_lo = (sem(n) for n in (
            "sg_ready", "silu_ready", "og_pool", "y_ready", "y_t", "y_hi", "y_lo"))
        osq, oss, ors = sem("o_square"), sem("o_sum"), sem("o_rstd")
        sig_ready, m_ready = sem("sig_ready"), sem("m_ready")
        m_out = sem("m_out")
        ml_in = [sem(f"ml_in{s}") for s in range(2)]
        mt_in = [sem(f"mt_in{s}") for s in range(2)]
        m_t, m_hi, m_lo = sem("m_t"), sem("m_hi"), sem("m_lo")
        xl_in = [sem(f"xl_in{s}") for s in range(2)]
        yo_ready = sem("yo_ready")
        yo_out = [sem(f"yo_out{s}") for s in range(3)]

        N_CONST = 16 * 14

        def mi(G, kind, i):
            return 18 * G + (9 if kind == "k" else 0) + i

        def ti(G, kind, i):
            return 17 * G + (9 if kind == "k" else 0) + i

        def z_freed(n):
            u, i = divmod(n, TILES)
            kind, G = U[u][0], U[u][1]
            br = 9 if kind[-1] == "b" else 0
            if kind in "qk":
                return zn_ready, mi(G, kind, i) + 1
            if kind == "v":
                return v_ready, 9 * G + i + 1
            if kind in ("ga", "gb"):
                return silu_ready, br + i + 1
            if kind in ("ma", "mb"):
                return sig_ready, 2 * br + 9 * G + i + 1
            if kind in ("pa", "pb"):
                return m_ready, 2 * br + 9 * G + i + 1
            return yo_ready, 9 * G + i + 1

        def row_start_step(G, i):
            if G <= 1:
                return i * P, 1
            if G == 2:
                return (i // 2) + (i % 2) * 512, 4
            return i, 8

        def rows_of(ap, G, i):
            a, s = row_start_step(G, i)
            return ap[a:a + s * (P - 1) + 1:s] if s > 1 else ap[a:a + P]

        def hT_of(h, G, k, i):
            if i == NT:
                return h[:, k, SEQ:ROWS]
            a, s = row_start_step(G, i)
            return h[:, k, a:a + s * (P - 1) + 1:s]

        def kept(G, i, kv):
            if G == 0:
                return nb_p[0, 0, i * P:(i + 1) * P, kv].rearrange("s h e -> s (h e)")
            out = na_p[G - 1][0, 0, :, kv].rearrange("s h e -> s (h e)")
            if G == 1:
                return out if i == NT - 1 else None
            if G == 2:
                return out[i // 2::4] if i % 2 else None
            return out[i::8]

        def kept_new(G, kv):
            if G == 0:
                return nb_s[0, :, :, kv].rearrange("b t h e -> b t (h e)")
            length = WINDOWS[G - 1][0]
            return na_s[G - 1][0, :, length - DEC_T:length, kv].rearrange("b t h e -> b t (h e)")

        k_sent = {s: [0] * (4 * TILES) for s in range(3)}
        v_sent = []
        for s in range(3):
            c = 0
            for kk in range(4 * TILES):
                G, i = divmod(kk, TILES)
                if kk % 3 == s and (i == NT or kept(G, i, 0) is not None):
                    c += 16
                k_sent[s][kk] = c
        c = 0
        for G in range(4):
            for i in range(TILES):
                c += 16 if (i == NT or kept(G, i, 1) is not None) else 0
            v_sent.append(c)

        def og_total(y):
            return sum(48 if yy < NT else 16 for yy in range(y % 2, y + 1, 2))

        def wait_reg(eng, s, value):
            eng.wait_ge(s, value)
            eng.nop(nofuse=True)

        block = ctx.enter_context(nc.Block())

        @block.sync
        def _(sp):
            sp.dma_start(ident[:, :], c_ident).then_inc(const_in, 16)
            sp.dma_start(gcol[:, :], norm_g[0].rearrange("(c p) -> p c", p=P), allow_slow_non_contiguous=True).then_inc(const_in, 16)

            def load_x(i):
                if i >= 2:
                    sp.wait_ge(h_xn, i - 1)
                src = x_p[0, i * P:(i + 1) * P, :] if i < NT else x_s.rearrange("b t d -> (b t) d")
                sp.dma_start(xt[0:nrows(i), i % 2, :], src).then_inc(x_in[i % 2], 16)

            load_x(0)
            load_x(1)
            for col, vec in ((0, qna), (1, qnb)):
                for h in range(2):
                    sp.dma_start(qcol[h * HD:(h + 1) * HD, col:col + 1],
                                 vec[0].rearrange("(d o) -> d o", o=1)).then_inc(const_in, 16)
            for col, vec in ((0, kna), (1, knb)):
                sp.dma_start(krow[:, col, :], vec[0].partition_broadcast(P)).then_inc(const_in, 16)
            for col, vec in enumerate((lq1, lk1, lq2, lk2)):
                sp.dma_start(lamv[:, col, :], vec[0].partition_broadcast(P)).then_inc(const_in, 16)
            sp.dma_start(coef[:, :], c_coef).then_inc(const_in, 16)
            sp.dma_start(subrow[:, :], subln[0].partition_broadcast(P)).then_inc(const_in, 16)

            def load_chunk(u, k):
                q = first_chunk[u] + k
                if q >= 4:
                    sp.wait_ge(lo_done, q - 3)
                _, _, name, col, _ = U[u]
                sp.dma_start(raw[:, q % 4, :], w_dram[name][k * P:(k + 1) * P, col:col + CW])\
                    .then_inc(raw_in[q % 4], 16)

            for i in range(2, TILES):
                load_x(i)
                if i == 2:
                    for k in range(4):
                        load_chunk(0, k)
                elif i + 1 < KC:
                    load_chunk(0, i + 1)

            def block_io(u):
                kind, G = U[u][0], U[u][1]
                prefetch = u + 1 < len(U) and u + 1 != FIRST_GATE
                for i in range(TILES):
                    if prefetch and i < U[u + 1][4]:
                        load_chunk(u + 1, i)
                    if kind == "k":
                        kk = TILES * G + i
                        dst = kept(G, i, 0) if i < NT else kept_new(G, 0)
                        if dst is not None:
                            sp.wait_ge(kn_ready, kk + 1)
                            sp.dma_start(dst, kn[0:nrows(i), kk % 3, :])\
                                .then_inc(k_out[kk % 3], 16)
                    if kind == "v":
                        dst = kept(G, i, 1) if i < NT else kept_new(G, 1)
                        if dst is not None:
                            sp.wait_ge(v_ready, TILES * G + i + 1)
                            sp.dma_start(dst, v_sb[0:nrows(i), i, :]).then_inc(v_out, 16)

            def tables(G):
                set_ = (3 * G + 2) % 2
                if G == 0:
                    for h in range(B_HEADS):
                        sp.wait_ge(z_ready, 27) if h < 2 else sp.wait_ge(bs, 16 + 16 * (h - 1))
                        sp.dma_start(att[set_]["tB"][:, h % 2, :], c_bias_b[h])\
                            .then_inc(btab if h % 2 == 0 else btab2, 16)
                else:
                    for c in range(NC):
                        base = 16 + 64 * (G - 1)
                        sp.wait_ge(z_ready, 27 * (G + 1)) if c < 2 else sp.wait_ge(as_, base + 16 * (c - 1))
                        sp.dma_start(att[set_]["tA"][:, c % 2, :, :],
                                     c_bias_a[G - 1, 2 * c:2 * c + 2].rearrange("h p x -> p h x"))\
                            .then_inc(atab if c % 2 == 0 else atab2, 16)

            def attention_out(G):
                if G == 0:
                    sp.wait_ge(bo, 8 + 32)
                else:
                    sp.wait_ge(ao, 8 + 32 * G)
                    sp.wait_ge(ast, 4 * G)
                for i in range(NT):
                    sp.dma_start(rows_of(o_scr[G], G, i).rearrange("s (c e) -> s c e", c=NC),
                                 qT[:, :].rearrange("p (c s) -> p c s", c=NC)[:, :, i * P:(i + 1) * P])\
                        .then_inc(o_out, 16)
                    if G:
                        sp.dma_start(rows_of(st_scr[G - 1], G, i), st[:, i, :]).then_inc(o_out, 16)

            for G in range(4):
                for kind in range(3):
                    block_io(3 * G + kind)
                tables(G)
                attention_out(G)

            sp.wait_ge(o_out, 16 * 8 * 7)
            sp.dma_start(pids[0:1, :], page_table.rearrange("b n -> (b n)").rearrange("(o n) -> o n", o=1))\
                .then_inc(s_const, 16)
            sp.dma_start(bias_sa[:, :], c_bias_sa).then_inc(s_const, 16)
            sp.dma_start(bias_sb[:, :], c_bias_sb).then_inc(s_const, 16)
            sp.dma_start(mask[:, :, :], c_mask.rearrange("g q e -> q g e")).then_inc(s_const, 16)
            sp.dma_start(sel[:, :], c_sel).then_inc(s_const, 16)
            sp.wait_ge(s_const, 80)
            for s in range(3):
                sp.wait_ge(k_out[s], k_sent[s][-1])
            sp.wait_ge(v_out, v_sent[-1])

            with sp.Fori(0, DEC_B) as b:
                wait_reg(sp, s_vb, b + 1)
                for kv in range(2):
                    for g in range(3):
                        ln = WINDOWS[g][0]
                        sp.dma_start(kv_new[:, kv, g, :],
                                     na_s[g][0, ds(b, 1), ln - DEC_T:ln, kv].rearrange("o t h e -> (o t) (h e)"))\
                            .then_inc(sn_in, 16)
                    sp.dma_start(kv_new[:, kv, 3, :],
                                 nb_s[0, ds(b, 1), :, kv].rearrange("o t h e -> (o t) (h e)"))\
                        .then_inc(sn_in, 16)

                def rows_a(T, kv):
                    g, r = (0, 0) if T == 0 else ((1, T - 1) if T < 5 else (2, T - 5))
                    dil = WINDOWS[g][1]
                    return ca[g][0, ds(b, 1), r::dil, kv].rearrange("o m h e -> (o m) (h e)")

                def load_k(T, src):
                    if T >= NKS:
                        wait_reg(sp, s_kt, 29 * b + 29 + T - 7)
                    else:
                        wait_reg(sp, s_kt, 29 * b + (T + 24 if T + 24 <= 28 else T + 16) + 1)
                    sp.dma_start(k_in[:, T % NKS, :], src).then_inc(sk_in[T % NKS], 16)

                def load_v(T, src):
                    if T < 13:
                        slot, last = T, (29 * b + 20 + T + 1 if T < 9 else 29 * b + T + 1)
                    elif T < 20:
                        slot, last = T, 29 * b + T + 1
                    else:
                        slot, last = T - 20, 29 * b + 29 + T - 20 + 1
                    wait_reg(sp, s_pv, last)
                    sp.dma_start(v_in[:, slot, :], src).then_inc(sv_in[slot], 16)

                for T in range(13):
                    load_k(T, rows_a(T, 0))
                    load_v(T, rows_a(T, 1))
                pages = []
                for j in range(N_PAGES):
                    pid = sp.value_load(pids[0:1, ds(b * N_PAGES + j, 1)], min_val=0, max_val=n_phys - 1)
                    load_k(13 + j, cb[0, ds(pid, 1), :, 0].rearrange("o s h e -> (o s) (h e)"))
                    if j < 7:
                        load_v(13 + j, cb[0, ds(pid, 1), :, 1].rearrange("o s h e -> (o s) (h e)"))
                for j in range(7, N_PAGES):
                    pid = sp.value_load(pids[0:1, ds(b * N_PAGES + j, 1)], min_val=0, max_val=n_phys - 1)
                    load_v(13 + j, cb[0, ds(pid, 1), :, 1].rearrange("o s h e -> (o s) (h e)"))

            sp.wait_ge(s_out, 32 + 32 * DEC_B)
            for k in range(KC):
                load_chunk(FIRST_GATE, k)
            for g in range(3):
                sp.dma_start(stc[:, :, g, :], st_scr[g].rearrange("(i p) s -> p i s", p=P)).then_inc(st_in, 16)

            def load_og(y):
                br, i = divmod(y, TILES)
                if y >= 2:
                    sp.wait_ge(y_ready, y - 1)
                if i == NT:
                    sp.dma_start(og[0:NS, y % 2, 0, :], os_scr[br]).then_inc(og_in[y % 2], 16)
                else:
                    for g in range(3 if br == 0 else 1):
                        src = o_scr[g + 1 if br == 0 else 0]
                        sp.dma_start(og[:, y % 2, g, :], src[i * P:(i + 1) * P, :]).then_inc(og_in[y % 2], 16)

            def rows_m(scr, i, half):
                return scr[i * P:i * P + nrows(i), half * CW:(half + 1) * CW]

            for u in range(FIRST_GATE, len(U)):
                kind, half = U[u][0], U[u][1]
                br = 1 if kind[-1] == "b" else 0
                if kind in ("ga", "gb"):
                    if br:
                        sp.wait_ge(m_out, 16 * 18)
                    load_og(9 * br)
                    load_og(9 * br + 1)
                if kind == "pb" and half == 0:
                    sp.wait_ge(y_t, 18)
                    for i in range(2):
                        sp.dma_start(zy[:, i, :], rows_m(ma_scr, i, 0)).then_inc(ml_in[i], 16)
                for i in range(TILES):
                    if u + 1 < len(U) and i < U[u + 1][4]:
                        load_chunk(u + 1, i)
                    if kind in ("ga", "gb") and i + 2 < TILES:
                        load_og(9 * br + i + 2)
                    if kind in ("pa", "pb"):
                        idx = 18 * br + 9 * half + i
                        sp.wait_ge(m_ready, idx + 1)
                        sp.dma_start(rows_m(m_scr if br else ma_scr, i, half), sig[0:nrows(i), i, :])\
                            .then_inc(m_out, 16)
                        nxt = 9 * half + i + 2
                        if br and nxt < 18:
                            hn_, in_ = divmod(nxt, 9)
                            sp.dma_start(zy[0:nrows(in_), nxt % 2, :], rows_m(ma_scr, in_, hn_))\
                                .then_inc(ml_in[nxt % 2], 16)
                    if kind == "out":
                        idx = 9 * half + i
                        if half == 0 and i == 0:
                            sp.wait_ge(m_out, 16 * 36)
                            for ii in range(2):
                                sp.dma_start(mt[0:nrows(ii), ii % 2, :], m_scr[ii * P:ii * P + nrows(ii), :])\
                                    .then_inc(mt_in[ii % 2], 16)
                            for ii in range(2):
                                sp.dma_start(xl[:, ii % 2, :], x_p[0, ii * P:(ii + 1) * P, 0:CW])\
                                    .then_inc(xl_in[ii % 2], 16)
                        if half == 0 and i + 2 < TILES:
                            ii = i + 2
                            sp.wait_ge(m_t, 2 * i + 2)
                            sp.dma_start(mt[0:nrows(ii), ii % 2, :], m_scr[ii * P:ii * P + nrows(ii), :])\
                                .then_inc(mt_in[ii % 2], 16)
                        sp.wait_ge(yo_ready, idx + 1)
                        dst = (y_p[0, i * P:(i + 1) * P, :] if i < NT else y_s.rearrange("b t d -> (b t) d"))
                        sp.dma_start(dst[:, half * CW:(half + 1) * CW], yo[0:nrows(i), idx % 3, :])\
                            .then_inc(yo_out[idx % 3], 16)
                        nxt = idx + 2
                        if nxt < 18:
                            hn_, in_ = divmod(nxt, 9)
                            src = (x_p[0, in_ * P:(in_ + 1) * P, :] if in_ < NT else
                                   x_s.rearrange("b t d -> (b t) d"))
                            sp.dma_start(xl[0:nrows(in_), nxt % 2, :], src[:, hn_ * CW:(hn_ + 1) * CW])\
                                .then_inc(xl_in[nxt % 2], 16)
            for s in range(3):
                sp.wait_ge(yo_out[s], 16 * 6)
            sp.wait_ge(copies, 16 * 3 * DEC_B)
            for s in range(3):
                sp.wait_ge(k_out[s], k_sent[s][-1])
            sp.wait_ge(v_out, v_sent[-1])

        @block.gpsimd
        def _(pool):
            steps = [0]

            def link(ins):
                steps[0] += 1
                ins.then_inc(pool_step, 1)
                pool.wait_ge(pool_step, steps[0])

            link(pool.memset(half_pow[:, :], -0.5))

            def rstd(out, in_, n, heads):
                r = in_.shape[0]
                link(pool.tensor_scalar(in_, in_, 1.0 / n, EPS, ALU.mult, ALU.add))
                return pool.tensor_tensor(out, in_, half_pow[0:r, 0:heads], ALU.pow)

            def input_lo(i):
                for half in range(2):
                    j = 2 * i + half
                    pool.wait_ge(h_hi, j + 1)
                    c0 = i * P
                    pool.tensor_tensor(hT_lo[:, 4 * half:4 * half + 4, c0:c0 + nrows(i)],
                                       hn[:, half, :].rearrange("p (k r) -> p k r", k=4)[:, :, 0:nrows(i)],
                                       hT_hi[:, 4 * half:4 * half + 4, c0:c0 + nrows(i)].bitcast(F32),
                                       ALU.subtract).then_inc(h_lo, 1)

            def split_lo(u, k):
                q = first_chunk[u] + k
                pool.wait_ge(hi_done, q + 1)
                pool.tensor_tensor(w_lo[u % 2][:, k, :], raw[:, q % 4, :],
                                   w_hi[u % 2][:, k, :].bitcast(F32), ALU.subtract).then_inc(lo_done, 1)

            for i in range(TILES):
                pool.wait_ge(h_ss, i + 1)
                rstd(rs[0:nrows(i), i % 2, 0:1], ss[0:nrows(i), i % 2, 0:1], D_MODEL, 1).then_inc(h_rs, 1)
                if i >= 1:
                    input_lo(i - 1)
                if i < KC:
                    split_lo(0, i)
            input_lo(TILES - 1)

            def block_(u):
                kind, G = U[u][0], U[u][1]
                prefetch = u + 1 < len(U) and u + 1 != FIRST_GATE
                for i in range(TILES):
                    r = nrows(i)
                    if kind in "qk":
                        m = mi(G, kind, i)
                        pool.wait_ge(ss_ready, m + 1)
                        rstd(rs[0:r, m % 2, :], ss[0:r, m % 2, :], HD, 8).then_inc(rs_ready, 1)
                    if prefetch and i < U[u + 1][4]:
                        split_lo(u + 1, i)
                    if kind == "k":
                        kk = TILES * G + i
                        pool.wait_ge(zn_ready, m + 1)
                        if kk >= 3:
                            G3, i3 = divmod(kk - 3, TILES)
                            pool.wait_ge(t_ready, ti(G3, "k", min(i3, NT - 1)) + 1)
                            if k_sent[kk % 3][kk - 3]:
                                pool.wait_ge(k_out[kk % 3], k_sent[kk % 3][kk - 3])
                        pool.tensor_tensor(kn[0:r, kk % 3, :].rearrange("p (h d) -> p h d", h=8),
                                           zn[0:r, m % 2, :].rearrange("p (h d) -> p h d", h=8),
                                           krow[0:r, 0 if G else 1, :].unsqueeze(1).to_broadcast([r, 8, HD]),
                                           ALU.mult).then_inc(kn_ready, 1)
                    if kind == "ga" and i < NT:
                        y = i
                        pool.wait_ge(ew_ready, 1)
                        pool.wait_ge(og_in[y % 2], 48 * (y // 2 + 1))
                        for g in (1, 2):
                            ins = pool.tensor_tensor(
                                og[:, y % 2, g, :].rearrange("p (h d) -> p h d", h=8),
                                og[:, y % 2, g, :].rearrange("p (h d) -> p h d", h=8),
                                ew[:, i, g, :].unsqueeze(2).to_broadcast([P, 8, HD]), ALU.mult)
                        ins.then_inc(og_pool, 1)
                    if kind == "gb":
                        pool.wait_ge(oss, i + 1)
                        rstd(rs[0:r, i % 2, 0:4], ss[0:r, i % 2, 0:4], P, 4).then_inc(ors, 1)

            def pad_queries(G):
                pool.wait_ge(t_ready, 17 * G + 17)
                for s in range(3):
                    pool.wait_ge(k_out[s], k_sent[s][TILES * G + NT])
                link(pool.memset(qz[0:HD, 1, :], 0.0))
                link(pool.memset(qz[HD:P, 0, :], 0.0))
                pool.wait_ge(t_moved, 17 * G + 9)
                with pool.Fori(0, NC) as c:
                    if G:
                        wait_reg(pool, aq, 16 * c + 16 + 64 * (G - 1))
                    else:
                        wait_reg(pool, bq, 16 * c + 16)
                    pool.tensor_copy(qz[0:HD, 0, :], qT[0:HD, ds(c * SEQ, SEQ)])
                    pool.tensor_copy(qz[HD:P, 1, :], qT[HD:P, ds(c * SEQ, SEQ)]).then_inc(qz_ready, 1)

            for G in range(4):
                for kind in range(3):
                    block_(3 * G + kind)
                pad_queries(G)
                if G:
                    pool.wait_ge(aq, 16 + 64 * G)
                else:
                    pool.wait_ge(bq, 16 + 64)

            pool.wait_ge(o_out, 16 * 8 * 7)
            link(pool.memset(q_all[:, :, :, :], 0.0))
            link(pool.memset(q_g1[:, :, :, :], 0.0))
            link(pool.memset(q_g2[:, :, :, :], 0.0))
            link(pool.memset(pT1[:, :, :], 0.0))
            link(pool.memset(pT2[:, :, :], 0.0))
            pool.sem_inc(s_zero, 1)

            def spread(t, off, dims, hh):
                base = t[hh * HD:(hh + 1) * HD, 0, 0, 0:1]
                return bass.AP(base.tensor, base.offset + off, [list(base.ap[0])] + dims)

            with pool.Fori(0, DEC_B) as b:
                wait_reg(pool, s_qk, 29 * b + 29)
                for hh in range(2):
                    src = qTs[hh * HD:(hh + 1) * HD, :, :, ds(b * DEC_T, DEC_T)]
                    pool.tensor_copy(spread(q_all, hh, [[NC * NS, 4], [NS + 16, NC], [2, DEC_T]], hh), src)
                    pool.tensor_copy(
                        spread(q_g1, hh, [[NC * NS + 2, 4], [NS + 16, NC], [8, 2]], hh),
                        qTs[hh * HD:(hh + 1) * HD, 2, :, ds(b * DEC_T, DEC_T)].rearrange("p c (u r) -> p r c u", u=2))
                    ins = pool.tensor_copy(
                        spread(q_g2, hh, [[NC * NS + 2, 8], [NS + 16, NC]], hh),
                        qTs[hh * HD:(hh + 1) * HD, 3, :, ds(b * DEC_T, DEC_T)].rearrange("p c r -> p r c"))
                ins.then_inc(sq_b, 1)

            for k in range(KC):
                split_lo(FIRST_GATE, k)
            for u in range(FIRST_GATE, len(U)):
                block_(u)

        @block.scalar
        def _(act):
            def copy_cache(b):
                for g, piece in ((0, 1536), (1, 1536), (2, 2560)):
                    keep = WINDOWS[g][0] - DEC_T
                    dst = na_s[g][0, b, 0:keep].rearrange("s v h e -> (s v h e)")
                    src = ca[g][0, b, DEC_T:keep + DEC_T].rearrange("s v h e -> (s v h e)")
                    act.dma_start(dst.rearrange("(a m x) -> a m x", a=16, x=piece),
                                  src.rearrange("(a m x) -> a m x", a=16, x=piece)).then_inc(copies, 16)

            def input_hi(i):
                for half in range(2):
                    j = 2 * i + half
                    act.wait_ge(h_hn, j + 1)
                    act.activation(hT_hi[:, 4 * half:4 * half + 4, i * P:i * P + nrows(i)],
                                   hn[:, half, :].rearrange("p (k r) -> p k r", k=4)[:, :, 0:nrows(i)],
                                   ACT.Copy).then_inc(h_hi, 1)

            def split_hi(u, k):
                q = first_chunk[u] + k
                act.wait_ge(raw_in[q % 4], 16 * (q // 4 + 1))
                if u >= 2:
                    act.wait_ge(z_ready, TILES * (u - 1))
                act.activation(w_hi[u % 2][:, k, :], raw[:, q % 4, :], ACT.Copy).then_inc(hi_done, 1)

            for i in range(TILES):
                r = nrows(i)
                act.wait_ge(x_in[i % 2], 16 * (i // 2 + 1))
                if i >= 2:
                    act.wait_ge(h_t, 2 * i - 2)
                    act.wait_ge(h_rs, i - 1)
                act.activation(xn[0:r, i % 2, :], xt[0:r, i % 2, :], ACT.Square,
                               accum_out=ss[0:r, i % 2, 0:1]).then_inc(h_ss, 1)
                if i >= 1:
                    input_hi(i - 1)
                if i < KC:
                    split_hi(0, i)
            input_hi(TILES - 1)
            act.wait_ge(setup, 2)
            act.activation(lam[:, 2:4], lam[:, 0:2], ACT.Exp).then_inc(setup, 1)

            def move(G, kind, i):
                t = ti(G, kind, i)
                act.wait_ge(t_ready, t + 1)
                src = bank(3 + t % 2).rearrange("p (c r) -> p c r", c=NC)
                if kind == "k":
                    act.activation(kT[:, :].rearrange("p (c s) -> p c s", c=NC)[:, :, i * P:(i + 1) * P], src, ACT.Copy).then_inc(t_moved, 1)
                    return
                if i == 0:
                    act.wait_ge(setup, 4)
                    if G:
                        act.wait_ge(o_out, 16 * 8 * (2 * G - 1))
                scale = qcol[:, (0 if G else 1):(0 if G else 1) + 1]
                if i < NT:
                    act.activation(qT[:, :].rearrange("p (c s) -> p c s", c=NC)[:, :, i * P:(i + 1) * P],
                                   src, ACT.Copy, scale=scale).then_inc(t_moved, 1)
                else:
                    act.activation(qTs[:, G, :, :],
                                   src[:, :, 0:NS], ACT.Copy, scale=scale).then_inc(t_moved, 1)

            def block_(u):
                kind, G = U[u][0], U[u][1]
                prefetch = u + 1 < len(U) and u + 1 != FIRST_GATE
                br = 1 if kind[-1] == "b" else 0
                if u < DEC_B:
                    copy_cache(u)
                for i in range(TILES):
                    n, r = TILES * u + i, nrows(i)
                    z = bank(n % 3)[0:r]
                    if kind in "qk":
                        m = mi(G, kind, i)
                        act.wait_ge(z_ready, n + 1)
                        if m >= 2:
                            act.wait_ge(ss_ready, m - 1)
                        act.activation(bank(5 + m % 2)[0:r], z, ACT.Square).then_inc(sq_ready, 1)
                    if kind == "q" and i:
                        move(G, "q", i - 1)
                    if kind == "k":
                        move(G, "q", NT) if i == 0 else move(G, "k", i - 1)
                    if kind in ("ga", "gb"):
                        y = 9 * br + i
                        if y == TILES:
                            act.wait_ge(m_out, 16 * 18)
                        act.wait_ge(z_ready, n + 1)
                        if y >= 2:
                            act.wait_ge(y_ready, y - 1)
                        act.activation(sg[0:r, y % 2, :], z, ACT.Sigmoid).then_inc(sg_ready, 1)
                        if br:
                            act.wait_ge(og_in[y % 2], og_total(y))
                            act.activation(og[0:r, y % 2, 1, :], og[0:r, y % 2, 0, :], ACT.Square)\
                                .then_inc(osq, 1)
                        if i:
                            move_y(y - 1)
                    if kind in ("ma", "mb"):
                        idx = 18 * br + 9 * G + i
                        if i == 0 and G == 0:
                            move_y(9 * br + NT)
                        if i == 0 and G == 1:
                            act.wait_ge(m_out, 16 * (18 * br + 9))
                        act.wait_ge(z_ready, n + 1)
                        act.activation(sig[0:r, i, :], z, ACT.Sigmoid).then_inc(sig_ready, 1)
                    if kind == "out" and G == 0:
                        if i == 0:
                            m_hi_move(0)
                        if i + 1 < TILES:
                            m_hi_move(i + 1)
                    if prefetch and i < U[u + 1][4]:
                        split_hi(u + 1, i)

            def move_y(y):
                i = y % TILES
                act.wait_ge(y_t, y + 1)
                act.activation(yT_hi[:, :, i * P:i * P + nrows(i)],
                               bank(3 + y % 2).rearrange("p (c r) -> p c r", c=NC)[:, :, 0:nrows(i)],
                               ACT.Copy).then_inc(y_hi, 1)

            def m_hi_move(i):
                for half in range(2):
                    act.wait_ge(m_t, 2 * i + half + 1)
                    act.activation(hT_hi[:, 4 * half:4 * half + 4, i * P:i * P + nrows(i)],
                                   bank(3 + 2 * (i % 2) + half).rearrange("p (c r) -> p c r", c=4)[:, :, 0:nrows(i)],
                                   ACT.Copy).then_inc(m_hi, 1)

            def attention_b():
                A = att[0]
                act.sem_inc(be, 16)
                act.sem_inc(bm, 12)
                act.sem_inc(bo, 8)
                with act.Fori(0, 2) as I:
                    for par in range(2):
                        def piece_move(i):
                            for p in pieces_of(i):
                                NP = 12 + 24 * I + 12 * par + p[0]
                                wait_reg(act, bt, NP + 1)
                                wait_reg(act, bp, NP - 1)
                                act.activation(A["ptB"][:, p[0] % 2, 0:p[2] * P], bank(4 + p[0] % 2)[:, 0:p[2] * P],
                                               ACT.Copy).then_inc(bm, 1)

                        def out_move(i):
                            wait_reg(act, bp, 12 + 24 * I + 12 * par + pieces_before(i + 1))
                            act.activation(qT[:, ds((2 * I + par) * SEQ + i * P, P)],
                                           bank(6 + i % 2)[:, 0:P], ACT.Copy,
                                           scale=rlB[:, par, i, 0:1]).then_inc(bo, 1)

                        for s in range(NT + 2):
                            if s < NT:
                                for mp in range(2):
                                    n = 2 * s + mp
                                    N = 16 + 32 * I + 16 * par + n
                                    wait_reg(act, bs, N + 1)
                                    sb = A["sB"][:, n % 4, 0:P * (s + 1)]
                                    act.activation(sb, sb, ACT.Exp, bias=st_sum[:, par, 0, n:n + 1],
                                                   scale=-1.0, accum_out=st_sum[:, par, 1, n:n + 1])\
                                        .then_inc(be, 1)
                            if 1 <= s <= NT:
                                piece_move(s - 1)
                            if s >= 2:
                                out_move(s - 2)

            def attention_a(G):
                A = att[(3 * G + 2) % 2]
                base, tbase = 16 + 64 * (G - 1), 8 + 32 * (G - 1)
                if G == 1:
                    act.sem_inc(ae, 16)
                    act.sem_inc(ao, 8)
                with act.Fori(0, 2) as I:
                    for par in range(2):
                        for s in range(16 + 3):
                            if s < 16:
                                N = base + 32 * I + 16 * par + s
                                wait_reg(act, as_, N + 1)
                                W = width_a(G, s // 2)
                                sb = A["sA"][:, s % 4, 0:W]
                                act.activation(sb, sb, ACT.Exp, bias=st_sum[:, par, 0, s:s + 1], scale=-1.0,
                                               accum_out=st_sum[:, par, 1, s:s + 1]).then_inc(ae, 1)
                            if s >= 3 and (s - 3) % 2 == 1:
                                i = (s - 3) // 2
                                N = base + 32 * I + 16 * par + 2 * i + 1
                                wait_reg(act, av, N + 1)
                                act.activation(qT[:, ds((2 * I + par) * SEQ + i * P, P)],
                                               bank(6 + i % 2)[:, 0:P], ACT.Copy).then_inc(ao, 1)

            for G in range(4):
                for kind in range(3):
                    u = 3 * G + kind
                    block_(u)
                attention_a(G) if G else attention_b()

            act.sem_inc(s_km, 29)
            act.sem_inc(s_oc, 2)
            act.sem_inc(s_out, 32)
            act.wait_ge(s_const, 80)
            act.wait_ge(s_zero, 1)
            with act.Fori(0, DEC_B) as b:
                def keys_move(T):
                    wait_reg(act, s_kt, 29 * b + 29 + T + 1)
                    wait_reg(act, s_qk, 29 * b + 29 + T - 1 if T >= 2 else 29 * b + 29 - (1 if T else 0))
                    act.activation(kTs[:, T % 2, :, :], bank(T % 2).rearrange("p (c r) -> p c r", c=NC),
                                   ACT.Copy).then_inc(s_km, 1)

                wait_reg(act, s_nt, b + 1)
                act.activation(kTn[:, :, :], bank(5)[:, 384:512].rearrange("p (c r) -> p c r", c=16),
                               ACT.Copy).then_inc(s_nm, 1)
                for T in range(29):
                    keys_move(T)
                    if T == 17:
                        wait_reg(act, s_ta, 2 * b + 1)
                        act.activation(s_a[:, :], s_a[:, :], ACT.Exp, bias=sc_s[:, 0:1], scale=-1.0,
                                       accum_out=sc_s[:, 1:2]).then_inc(s_ea, 1)
                wait_reg(act, s_min, b + 1)
                act.activation(s_b[:, :], s_b[:, :], ACT.Exp, bias=sc_s[:, 8:9], scale=-1.0,
                               accum_out=sc_s[:, 9:10]).then_inc(s_eb, 1)
                wait_reg(act, s_sel, 2 * b + 1)
                wait_reg(act, s_out, 32 * b + 32)
                act.activation(os_[:, 0, :], bank(2)[0:DEC_T], ACT.Copy).then_inc(s_oc, 1)
                wait_reg(act, s_oc, 2 * b + 3)
                act.dma_start(os_scr[0, ds(b * DEC_T, DEC_T), :], os_[:, 0, :]).then_inc(s_out, 16)
                wait_reg(act, s_sel, 2 * b + 2)
                act.activation(os_[:, 1, :], bank(2)[0:DEC_T], ACT.Copy).then_inc(s_oc, 1)
                wait_reg(act, s_oc, 2 * b + 4)
                act.dma_start(os_scr[1, ds(b * DEC_T, DEC_T), :], os_[:, 1, :]).then_inc(s_out, 16)

            for k in range(KC):
                split_hi(FIRST_GATE, k)
            act.wait_ge(ew_exp, 1)
            act.activation(ew[:, :, :, :], ew[:, :, :, :], ACT.Exp).then_inc(ew_exp, 1)
            for u in range(FIRST_GATE, len(U)):
                block_(u)

        @block.vector
        def _(dve):
            steps = [0]

            def link(ins):
                steps[0] += 1
                ins.then_inc(dve_step, 1)
                dve.wait_ge(dve_step, steps[0])

            def rows_scale(i):
                r = nrows(i)
                dve.wait_ge(h_rs, i + 1)
                dve.tensor_scalar(xn[0:r, i % 2, :], xt[0:r, i % 2, :], rs[0:r, i % 2, 0:1], None, ALU.mult)\
                    .then_inc(h_xn, 1)

            def input_gain(i):
                r = nrows(i)
                for half in range(2):
                    j = 2 * i + half
                    dve.wait_ge(h_t, j + 1)
                    if i:
                        dve.wait_ge(h_lo, j - 1)
                    dve.tensor_tensor(hn[:, half, :].rearrange("p (k r) -> p k r", k=4)[:, :, 0:r],
                                      bank(2 * (i % 2) + half).rearrange("p (k r) -> p k r", k=4)[:, :, 0:r],
                                      gcol[:, 4 * half:4 * half + 4].unsqueeze(2).to_broadcast([P, 4, r]),
                                      ALU.mult).then_inc(h_hn, 1)

            dve.wait_ge(const_in, N_CONST)
            for i in range(TILES):
                rows_scale(i)
                if i:
                    input_gain(i - 1)
            input_gain(TILES - 1)
            for j in range(2):
                dve.tensor_tensor_reduce(out=lamv[:, 2 * j, :], in0=lamv[:, 2 * j, :], in1=lamv[:, 2 * j + 1, :],
                                         scale=1.0, scalar=0.0, op0=ALU.mult, op1=ALU.add,
                                         accum_out=lam[:, j:j + 1]).then_inc(setup, 1)
            dve.wait_ge(setup, 3)
            link(dve.tensor_tensor(lam[:, 4:5], lam[:, 3:4], lam[:, 2:3], ALU.subtract))
            link(dve.tensor_scalar(lam[:, 5:6], lam[:, 4:5], -LAM_INIT, None, ALU.add))
            link(dve.tensor_scalar(subrow[:, :], subrow[:, :], 1.0 - LAM_INIT, None, ALU.mult))
            link(dve.scalar_tensor_tensor(out=coef[:, 0:1], in0=coef[:, 1:2], scalar=lam[0:NS, 5:6],
                                          in1=coef[:, 0:1], op0=ALU.mult, op1=ALU.add))
            dve.tensor_scalar(qcol[:, :], qcol[:, :], -(HD ** -0.5), None, ALU.mult).then_inc(setup, 1)

            def block_(u):
                kind, G = U[u][0], U[u][1]
                br = 1 if kind[-1] == "b" else 0
                for i in range(TILES):
                    n, r = TILES * u + i, nrows(i)
                    z = bank(n % 3)[0:r]
                    if kind in "qk":
                        m = mi(G, kind, i)
                        dve.wait_ge(sq_ready, m + 1)
                        dve.tensor_reduce(ss[0:r, m % 2, :],
                                          bank(5 + m % 2)[0:r].rearrange("p (h d) -> p h d", h=8),
                                          AX_X, ALU.add).then_inc(ss_ready, 1)
                        dve.wait_ge(rs_ready, m + 1)
                        if m >= 2:
                            G2, m2 = divmod(m - 2, 18)
                            if m2 < 9:
                                dve.wait_ge(t_ready, ti(G2, "q", m2) + 1)
                            else:
                                dve.wait_ge(kn_ready, TILES * G2 + m2 - 9 + 1)
                        dve.tensor_tensor(zn[0:r, m % 2, :].rearrange("p (h d) -> p h d", h=8),
                                          z.rearrange("p (h d) -> p h d", h=8),
                                          rs[0:r, m % 2, :].unsqueeze(2).to_broadcast([r, 8, HD]),
                                          ALU.mult).then_inc(zn_ready, 1)
                    if kind == "v":
                        dve.wait_ge(z_ready, n + 1)
                        if i == 0 and G:
                            dve.wait_ge(v_out, v_sent[G - 1])
                        dve.tensor_copy(v_sb[0:r, i, :], z).then_inc(v_ready, 1)
                    if kind in ("ga", "gb"):
                        y = 9 * br + i
                        s = y % 2
                        dve.wait_ge(sg_ready, y + 1)
                        dve.tensor_tensor(sg[0:r, s, :], sg[0:r, s, :], z, ALU.mult).then_inc(silu_ready, 1)
                        if y >= 2:
                            dve.wait_ge(y_t, y - 1)
                        heads = 8 if br == 0 else 4
                        o = og[0:r, s, 0, :].rearrange("p (h d) -> p h d", h=heads)
                        dve.wait_ge(og_in[s], og_total(y))
                        if br == 0 and i < NT:
                            link(dve.tensor_tensor(o, o, ew[:, i, 0, :].unsqueeze(2).to_broadcast([P, 8, HD]),
                                                   ALU.mult))
                            dve.wait_ge(og_pool, i + 1)
                            link(dve.tensor_tensor(og[:, s, 0, :], og[:, s, 0, :], og[:, s, 1, :], ALU.add))
                            link(dve.tensor_tensor(og[:, s, 0, :], og[:, s, 0, :], og[:, s, 2, :], ALU.add))
                        if br == 1:
                            dve.wait_ge(osq, i + 1)
                            dve.tensor_reduce(ss[0:r, i % 2, 0:4],
                                              og[0:r, s, 1, :].rearrange("p (h d) -> p h d", h=4),
                                              AX_X, ALU.add).then_inc(oss, 1)
                            dve.wait_ge(ors, i + 1)
                            link(dve.tensor_tensor(o, o, rs[0:r, i % 2, 0:4].unsqueeze(2).to_broadcast([r, 4, P]),
                                                   ALU.mult))
                            link(dve.tensor_tensor(o, o, subrow[0:r, :].unsqueeze(1).to_broadcast([r, 4, P]),
                                                   ALU.mult))
                        dve.wait_ge(silu_ready, y + 1)
                        dve.tensor_tensor(zy[0:r, s, :], og[0:r, s, 0, :], sg[0:r, s, :], ALU.mult)\
                            .then_inc(y_ready, 1)
                        if i:
                            y_low(y - 1)
                    if kind in ("ma", "mb") and i == 0 and G == 0:
                        y_low(9 * br + NT)
                    if kind in ("pa", "pb"):
                        idx = 18 * br + 9 * G + i
                        dve.wait_ge(z_ready, n + 1)
                        dve.wait_ge(sig_ready, idx + 1)
                        ins = dve.tensor_tensor(sig[0:r, i, :], sig[0:r, i, :], z, ALU.mult)
                        if br:
                            link(ins)
                            dve.wait_ge(ml_in[(9 * G + i) % 2], 16 * ((9 * G + i) // 2 + 1))
                            ins = dve.tensor_tensor(sig[0:r, i, :], sig[0:r, i, :],
                                                    zy[0:r, (9 * G + i) % 2, :], ALU.add)
                        ins.then_inc(m_ready, 1)
                    if kind == "out":
                        if G == 0:
                            if i == 0:
                                m_low(0)
                            if i + 1 < TILES:
                                m_low(i + 1)
                        idx = 9 * G + i
                        dve.wait_ge(z_ready, n + 1)
                        dve.wait_ge(xl_in[idx % 2], 16 * (idx // 2 + 1))
                        if idx >= 3:
                            dve.wait_ge(yo_out[idx % 3], 16 * (idx // 3))
                        dve.tensor_tensor(yo[0:r, idx % 3, :], z, xl[0:r, idx % 2, :], ALU.add)\
                            .then_inc(yo_ready, 1)

            def y_low(y):
                i = y % TILES
                dve.wait_ge(y_hi, y + 1)
                dve.tensor_tensor(yT_lo[:, :, i * P:i * P + nrows(i)],
                                  bank(3 + y % 2).rearrange("p (c r) -> p c r", c=NC)[:, :, 0:nrows(i)],
                                  yT_hi[:, :, i * P:i * P + nrows(i)].bitcast(F32), ALU.subtract)\
                    .then_inc(y_lo, 1)

            def m_low(i):
                for half in range(2):
                    dve.wait_ge(m_hi, 2 * i + half + 1)
                    cols = slice(i * P, i * P + nrows(i))
                    dve.tensor_tensor(
                        hT_lo[:, 4 * half:4 * half + 4, cols],
                        bank(3 + 2 * (i % 2) + half).rearrange("p (c r) -> p c r", c=4)[:, :, 0:nrows(i)],
                        hT_hi[:, 4 * half:4 * half + 4, cols].bitcast(F32), ALU.subtract).then_inc(m_lo, 1)

            def attention_b():
                A = att[0]
                dve.sem_inc(bs, 16)
                dve.sem_inc(ba, 8)
                with dve.Fori(0, 2) as I:
                    for par in range(2):
                        wait_reg(dve, btab2 if par else btab, 16 * I + 16)
                        for s in range(NT + 1):
                            if s < NT:
                                W = P * (s + 1)
                                for mp in range(2):
                                    n = 2 * s + mp
                                    N = 16 + 32 * I + 16 * par + n
                                    wait_reg(dve, bq, N + 1)
                                    if mp:
                                        wait_reg(dve, ba, 8 + 16 * I + 8 * par + s - 1)
                                    else:
                                        wait_reg(dve, bt, 12 + 24 * I + 12 * par + (pieces_before(s - 1) if s >= 2 else 2 * s - 2))
                                    dve.tensor_tensor_reduce(
                                        out=A["sB"][:, n % 4, 0:W], in0=ps[:, (n % 2) * 1024:(n % 2) * 1024 + W],
                                        in1=A["tB"][:, par, SEQ - W:SEQ], scale=1.0, scalar=3e38,
                                        op0=ALU.add, op1=ALU.min, accum_out=st_sum[:, par, 0, n:n + 1])\
                                        .then_inc(bs, 1)
                            if s:
                                i = s - 1
                                W = P * (i + 1)
                                NW = 32 * I + 16 * par + 2 * i
                                wait_reg(dve, be, 16 + 32 * I + 16 * par + 2 * i + 2)
                                dve.reciprocal(rlB[:, par, i, :], st_sum[:, par, 1, 2 * i:2 * i + 2])\
                                    .then_inc(bw, 1)
                                wait_reg(dve, bw, NW + 1)
                                dve.scalar_tensor_tensor(out=wB[:, par, i:i + 1], in0=rlB[:, par, i, 1:2],
                                                         scalar=st_sum[:, par, 1, 2 * i:2 * i + 1],
                                                         in1=lam[:, 5:6], op0=ALU.mult, op1=ALU.mult)\
                                    .then_inc(bw, 1)
                                wait_reg(dve, bw, NW + 2)
                                p1 = A["sB"][:, (2 * i) % 4, 0:W]
                                p2 = A["sB"][:, (2 * i + 1) % 4, 0:W]
                                dve.scalar_tensor_tensor(out=p1, in0=p2, scalar=wB[:, par, i:i + 1], in1=p1,
                                                         op0=ALU.mult, op1=ALU.add).then_inc(ba, 1)

            def attention_a(G):
                A = att[(3 * G + 2) % 2]
                base = 16 + 64 * (G - 1)
                if G == 1:
                    dve.sem_inc(as_, 16)
                    dve.sem_inc(am, 16)
                else:
                    dve.wait_ge(o_out, 16 * 8 * (2 * G - 1))
                with dve.Fori(0, 2) as I:
                    for par in range(2):
                        wait_reg(dve, atab2 if par else atab, 16 * I + 16 + 32 * (G - 1))
                        for s in range(16 + 2):
                            if s < 16:
                                N = base + 32 * I + 16 * par + s
                                W = width_a(G, s // 2)
                                wait_reg(dve, aq, N + 1)
                                wait_reg(dve, atp, N - 3)
                                dve.tensor_tensor_reduce(
                                    out=A["sA"][:, s % 4, 0:W], in0=bank(s % 4)[:, 0:W],
                                    in1=A["tA"][:, par, s % 2, 256 - W:256], scale=1.0, scalar=3e38,
                                    op0=ALU.add, op1=ALU.min, accum_out=st_sum[:, par, 0, s:s + 1])\
                                    .then_inc(as_, 1)
                            if s >= 2:
                                n = s - 2
                                N = base + 32 * I + 16 * par + n
                                W = width_a(G, n // 2)
                                wait_reg(dve, atp, N + 1)
                                wait_reg(dve, av, N - 2)
                                dve.tensor_copy(A["ptA"][:, n % 3, 0:W], bank(4 + n % 2)[:, 0:W]).then_inc(am, 1)
                        wait_reg(dve, ae, base + 32 * I + 16 * par + 16)
                        c2 = (2 * I + par) * 2
                        for j in range(2):
                            ins = dve.tensor_copy(st[:, :, ds(c2 + 8 * j, 2)],
                                                  st_sum[:, par, j, :].rearrange("p (i h) -> p i h", h=2))
                        ins.then_inc(ast, 1)

            for G in range(4):
                for kind in range(3):
                    block_(3 * G + kind)
                attention_a(G) if G else attention_b()

            dve.sem_inc(s_pbm, 2)
            dve.sem_inc(s_om, 2)
            dve.wait_ge(s_const, 80)
            dve.wait_ge(s_zero, 1)
            with dve.Fori(0, DEC_B) as b:
                def biased(out, in_, table, acc):
                    return dve.tensor_tensor_reduce(out=out, in0=in_, in1=table, scale=1.0, scalar=3e38,
                                                    op0=ALU.add, op1=ALU.min, accum_out=acc)

                wait_reg(dve, s_qk, 29 * b + 29 + 13)
                biased(s_a[:, :], bank(2)[0:NS, 0:NEW_A], bias_sa[:, :], sc_s[:, 0:1]).then_inc(s_ta, 1)
                wait_reg(dve, s_pb, 2 * b + 2)
                biased(s_b[:, PAST:KEYS_B], bank(2)[0:NS, NEW_A:NEW_A + DEC_T], bias_sb[:, PAST:KEYS_B],
                       sc_s[:, 2:3]).then_inc(s_ta, 1)
                for q in range(4):
                    wait_reg(dve, s_qk, 29 * b + 29 + 13 + 4 * (q + 1))
                    biased(s_b[:, q * CW:(q + 1) * CW], bank(3 + q % 2)[0:NS], bias_sb[:, q * CW:(q + 1) * CW],
                           sc_s[:, 3 + q:4 + q]).then_inc(s_tb, 1)
                wait_reg(dve, s_tb, 4 * b + 4)
                dve.tensor_reduce(sc_s[:, 8:9], sc_s[:, 2:7], AX_X, ALU.min).then_inc(s_min, 1)
                wait_reg(dve, s_pa, b + 1)
                wait_reg(dve, s_va, b + 1)
                dve.tensor_copy(pT0[:, :], bank(5)[:, 0:NS])

                def dims(ap, off, d):
                    return bass.AP(ap.tensor, ap.offset + off, [list(ap.ap[0])] + d)

                dve.tensor_copy(dims(pT1[:, 0, 0:1], 0, [[NS + 2, 4], [8, 8], [1, 2]]),
                                dims(ps[:, 5 * CW + NS:5 * CW + NS + 1], 0, [[2, 4], [8, 8], [1, 2]]))
                dve.tensor_copy(dims(pT2[:, 0, 0:1], 0, [[NS + 2, 8], [16, 4], [1, 2]]),
                                dims(ps[:, 5 * CW + 2 * NS:5 * CW + 2 * NS + 1], 0, [[2, 8], [16, 4], [1, 2]]))
                dve.tensor_copy(pTn[:, 0:3, :], bank(5)[0:DEC_T, 192:384].rearrange("p (g q) -> p g q", g=3))\
                    .then_inc(s_pam, 1)
                wait_reg(dve, s_vb, b + 1)
                for j in range(2):
                    wait_reg(dve, s_pb, 2 * b + 2 + j + 1)
                    if j:
                        dve.tensor_copy(pTn[:, 3, :], bank(5)[0:DEC_T, 0:NS])
                    dve.tensor_copy(pTb[:, 8 * j:8 * j + 8, :], bank(3 + j).rearrange("p (g q) -> p g q", g=8))\
                        .then_inc(s_pbm, 1)
                wait_reg(dve, s_ea, b + 1)
                dve.reciprocal(sc_s[:, 10:11], sc_s[:, 1:2]).then_inc(s_rec, 1)
                wait_reg(dve, s_eb, b + 1)
                dve.reciprocal(sc_s[:, 11:12], sc_s[:, 9:10]).then_inc(s_rec, 1)
                wait_reg(dve, s_rec, 3 * b + 2)
                dve.tensor_scalar(sc_s[:, 12:13], sc_s[:, 11:12], coef[:, 0:1], None, ALU.mult).then_inc(s_rec, 1)
                wait_reg(dve, s_rec, 3 * b + 3)
                wait_reg(dve, s_va, b + 2)
                dve.scalar_tensor_tensor(out=om[:, 0, :], in0=bank(7)[0:NS], scalar=sc_s[:, 10:11],
                                         in1=mask[:, 0, :], op0=ALU.mult, op1=ALU.mult).then_inc(s_om, 1)
                wait_reg(dve, s_vb, b + 2)
                dve.scalar_tensor_tensor(out=om[:, 1, :], in0=bank(6)[0:NS], scalar=sc_s[:, 12:13],
                                         in1=mask[:, 1, :], op0=ALU.mult, op1=ALU.mult).then_inc(s_om, 1)

            dve.wait_ge(st_in, 48)

            def nm(g):
                return stc[:, :, g, 0:8]

            link(dve.tensor_tensor(nmin[:, :, :], nm(0), nm(1), ALU.min))
            link(dve.tensor_tensor(nmin[:, :, :], nmin[:, :, :], nm(2), ALU.min))
            for g in range(3):
                link(dve.tensor_tensor(ew[:, :, g, :], nmin[:, :, :], nm(g), ALU.subtract))
            dve.sem_inc(ew_exp, 1)
            dve.wait_ge(ew_exp, 2)
            for g in range(3):
                link(dve.tensor_tensor(el[:, :, g, :], ew[:, :, g, :], stc[:, :, g, 8:16], ALU.mult))
            link(dve.tensor_tensor(den[:, :, :], el[:, :, 0, :], el[:, :, 1, :], ALU.add))
            link(dve.tensor_tensor(den[:, :, :], den[:, :, :], el[:, :, 2, :], ALU.add))
            link(dve.reciprocal(den[:, :, :], den[:, :, :]))
            for g in range(3):
                link(dve.tensor_tensor(ew[:, :, g, :], ew[:, :, g, :], den[:, :, :], ALU.mult))
            dve.sem_inc(ew_ready, 1)
            for u in range(FIRST_GATE, len(U)):
                block_(u)

        @block.tensor
        def _(pe):
            pe.wait_ge(const_in, N_CONST)

            for i in range(TILES):
                r = nrows(i)
                pe.wait_ge(h_xn, i + 1)
                for half in range(2):
                    if i >= 2:
                        pe.wait_ge(h_hn, 2 * (i - 2) + half + 1)
                    for k in range(4):
                        c = 4 * half + k
                        ins = pe.transpose(bank(2 * (i % 2) + half)[:, k * P:k * P + r],
                                           xn[0:r, i % 2, c * P:(c + 1) * P], ident[0:r, 0:r])
                    ins.then_inc(h_t, 1)

            def turn(G, kind, i):
                t, r = ti(G, kind, i), nrows(i)
                if kind == "q":
                    pe.wait_ge(zn_ready, mi(G, "q", i) + 1)
                    src = zn[0:r, mi(G, "q", i) % 2, :]
                else:
                    kk = TILES * G + i
                    pe.wait_ge(kn_ready, kk + 1)
                    src = kn[0:r, kk % 3, :]
                if t >= 2:
                    pe.wait_ge(t_moved, t - 1)
                for c in range(NC):
                    ins = pe.transpose(bank(3 + t % 2)[:, c * P:c * P + r], src[:, c * P:(c + 1) * P],
                                       ident[0:r, 0:r])
                ins.then_inc(t_ready, 1)

            def turn_y(y):
                r = nrows(y % TILES)
                pe.wait_ge(y_ready, y + 1)
                if y >= 2:
                    pe.wait_ge(y_lo, y - 1)
                for c in range(NC):
                    ins = pe.transpose(bank(3 + y % 2)[:, c * P:c * P + r], zy[0:r, y % 2, c * P:(c + 1) * P],
                                       ident[0:r, 0:r])
                ins.then_inc(y_t, 1)

            def turn_m(i):
                r = nrows(i)
                pe.wait_ge(mt_in[i % 2], 16 * (i // 2 + 1))
                for half in range(2):
                    if i >= 2:
                        pe.wait_ge(m_lo, 2 * (i - 2) + half + 1)
                    for k in range(4):
                        c = 4 * half + k
                        ins = pe.transpose(bank(3 + 2 * (i % 2) + half)[:, k * P:k * P + r],
                                           mt[0:r, i % 2, c * P:(c + 1) * P], ident[0:r, 0:r])
                    ins.then_inc(m_t, 1)

            def block_(u):
                kind, G, _, _, K = U[u]
                br = 1 if kind[-1] == "b" else 0
                order = G if kind in "qkv" else 0
                hi, lo = (yT_hi, yT_lo) if kind in ("pa", "pb") else (hT_hi, hT_lo)
                if kind == "out" and G == 0:
                    turn_m(0)
                    turn_m(1)
                for i in range(TILES):
                    n, r = TILES * u + i, nrows(i)
                    if i == 0:
                        pe.wait_ge(lo_done, first_chunk[u + 1])
                    if n == 0:
                        pe.wait_ge(h_hn, 2 * TILES)
                    if u < 3:
                        pe.wait_ge(h_lo, 2 * i + 2)
                    if kind in ("pa", "pb"):
                        pe.wait_ge(y_lo, 9 * br + i + 1)
                    if kind == "out":
                        pe.wait_ge(m_lo, 2 * i + 2)
                    if n >= 3:
                        pe.wait_ge(*z_freed(n - 3))
                    z = bank(n % 3)[0:r]
                    for k in range(K):
                        sh, sl = hT_of(hi, order, k, i), hT_of(lo, order, k, i)
                        pe.matmul(z, sh, w_hi[u % 2][:, k, :], start=(k == 0), stop=False)
                        pe.matmul(z, sh, w_lo[u % 2][:, k, :], start=False, stop=False)
                        ins = pe.matmul(z, sl, w_hi[u % 2][:, k, :], start=False, stop=(k == K - 1))
                    ins.then_inc(z_ready, 1)
                    if kind == "q" and i:
                        turn(G, "q", i - 1)
                    if kind == "k":
                        turn(G, "q", NT) if i == 0 else turn(G, "k", i - 1)
                    if kind in ("ga", "gb") and i:
                        turn_y(9 * br + i - 1)
                    if kind == "out" and G == 0 and i + 2 < TILES:
                        turn_m(i + 2)
                if kind in ("ga", "gb"):
                    turn_y(9 * br + NT)

            def attention_b():
                A = att[0]
                pe.sem_inc(bq, 16)
                pe.sem_inc(bt, 12)
                pe.sem_inc(bp, 12)
                with pe.Fori(0, 2) as I:
                    for par in range(2):
                        h = 2 * I + par
                        for s in range(NT + 1):
                            if s < NT:
                                W = P * (s + 1)
                                for mp in range(2):
                                    n = 2 * s + mp
                                    N = 16 + 32 * I + 16 * par + n
                                    if n == 0:
                                        wait_reg(pe, qz_ready, h + 1)
                                    wait_reg(pe, bs, N - 1)
                                    for w0 in range(0, W, CW):
                                        w = min(CW, W - w0)
                                        ins = pe.matmul(ps[:, (n % 2) * 1024 + w0:(n % 2) * 1024 + w0 + w],
                                                        qz[:, mp, s * P:(s + 1) * P],
                                                        kT[:, ds(h * SEQ + w0, w)],
                                                        start=True, stop=True)
                                    ins.then_inc(bq, 1)
                            if s:
                                i = s - 1
                                wait_reg(pe, ba, 8 + 16 * I + 8 * par + i + 1)
                                for p, j0, nb in pieces_of(i):
                                    NP = 12 + 24 * I + 12 * par + p
                                    wait_reg(pe, bm, NP - 1)
                                    for j in range(nb):
                                        ins = pe.transpose(bank(4 + p % 2)[:, j * P:(j + 1) * P],
                                                           A["sB"][:, (2 * i) % 4, (j0 + j) * P:(j0 + j + 1) * P],
                                                           ident[:, :])
                                    ins.then_inc(bt, 1)
                                wait_reg(pe, bo, 8 + 16 * I + 8 * par + i - 1)
                                for p, j0, nb in pieces_of(i):
                                    NP = 12 + 24 * I + 12 * par + p
                                    wait_reg(pe, bm, NP + 1)
                                    for j in range(nb):
                                        ins = pe.matmul(bank(6 + i % 2)[:, 0:P], A["ptB"][:, p % 2, j * P:(j + 1) * P],
                                                        v_sb[:, j0 + j, ds(h * P, P)],
                                                        start=(j0 + j == 0), stop=(j0 + j == i))
                                    ins.then_inc(bp, 1)

            def attention_a(G):
                A = att[(3 * G + 2) % 2]
                base, tbase = 16 + 64 * (G - 1), 8 + 32 * (G - 1)
                if G == 1:
                    for s in (aq, atp, av):
                        pe.sem_inc(s, 16)
                with pe.Fori(0, 2) as I:
                    for par in range(2):
                        c = 2 * I + par
                        for s in range(16 + 3):
                            if s < 16:
                                i, hh = divmod(s, 2)
                                N = base + 32 * I + 16 * par + s
                                W = width_a(G, i)
                                if s == 0:
                                    wait_reg(pe, qz_ready, c + 4 * G + 1)
                                wait_reg(pe, as_, N - 3)
                                pe.matmul(bank(s % 4)[:, 0:W], qz[:, hh, i * P:(i + 1) * P],
                                          kT[:, ds(c * SEQ + (i + 1) * P - W, W)],
                                          start=True, stop=True).then_inc(aq, 1)
                            if 2 <= s < 18:
                                n = s - 2
                                N = base + 32 * I + 16 * par + n
                                wait_reg(pe, ae, N + 1)
                                wait_reg(pe, am, N - 1)
                                for j in range(width_a(G, n // 2) // P):
                                    ins = pe.transpose(bank(4 + n % 2)[:, j * P:(j + 1) * P],
                                                       A["sA"][:, n % 4, j * P:(j + 1) * P], ident[:, :])
                                ins.then_inc(atp, 1)
                            if s >= 3:
                                n = s - 3
                                i, hh = divmod(n, 2)
                                N = base + 32 * I + 16 * par + n
                                nb = width_a(G, i) // P
                                wait_reg(pe, am, N + 1)
                                if hh == 0:
                                    wait_reg(pe, ao, tbase + 16 * I + 8 * par + i - 1)
                                for j in range(nb):
                                    ins = pe.matmul(bank(6 + i % 2)[:, hh * HD:(hh + 1) * HD],
                                                    A["ptA"][:, n % 3, j * P:(j + 1) * P],
                                                    v_sb[:, i + 1 - nb + j, ds(c * P + hh * HD, HD)],
                                                    start=(j == 0), stop=(j == nb - 1))
                                ins.then_inc(av, 1)

            for G in range(4):
                for kind in range(3):
                    block_(3 * G + kind)
                pe.wait_ge(v_ready, 9 * G + 9)
                pe.wait_ge(t_moved, 17 * G + 17)
                attention_a(G) if G else attention_b()

            for s, c in ((s_kt, 29), (s_qk, 29), (s_pv, 29), (s_va, 1), (s_vb, 1), (s_pb, 2)):
                pe.sem_inc(s, c)
            with pe.Fori(0, DEC_B) as b:
                wait_reg(pe, sn_in, 128 * b + 128)
                wait_reg(pe, s_pbm, 2 * b + 2)
                for g in range(4):
                    for c in range(NC):
                        j = 4 * g + c
                        ins = pe.transpose(bank(5)[:, 384 + 8 * j:392 + 8 * j],
                                           kv_new[:, 0, g, c * P:(c + 1) * P], ident[0:DEC_T, 0:DEC_T])
                ins.then_inc(s_nt, 1)

                def keys_turn(T):
                    per = 4 if T % NKS < 5 else 3
                    wait_reg(pe, sk_in[T % NKS], 16 * per * b + 16 * (T // NKS + 1))
                    wait_reg(pe, s_km, 29 * b + 29 + T - 1 if T >= 2 else 29 * b + 29 - (1 if T else 0))
                    for c in range(NC):
                        ins = pe.transpose(bank(T % 2)[:, c * P:(c + 1) * P],
                                           k_in[:, T % NKS, c * P:(c + 1) * P], ident[:, :])
                    ins.then_inc(s_kt, 1)

                def score(T):
                    wait_reg(pe, s_km, 29 * b + 29 + T + 1)
                    if T < 13:
                        if T == 0:
                            q, col, g = q_all[:, 1, :, :], 0, 0
                        elif T < 5:
                            q, col, g = q_g1[:, T - 1, :, :], P + DEC_T, 1
                        else:
                            q, col, g = q_g2[:, T - 5, :, :], 2 * (P + DEC_T), 2
                        out = bank(2)[0:NS, col:col + P]
                        first = False
                    else:
                        j = T - 13
                        q = q_all[:, 0, :, :]
                        out = bank(3 + (j // 4) % 2)[0:NS, (j % 4) * P:(j % 4 + 1) * P]
                        first = j % 4 == 0
                        if j in (0, 4):
                            wait_reg(pe, s_pbm, 2 * b + 2)
                        if j in (8, 12):
                            wait_reg(pe, s_tb, 4 * b + (1 if j == 8 else 2))
                    for c in range(NC):
                        ins = pe.matmul(out, q[:, c, :], kTs[:, T % 2, c, :], start=(first and c == 0),
                                        stop=(c == NC - 1), skip_group_check=True)
                    ins.then_inc(s_qk, 1)

                keys_turn(0)
                wait_reg(pe, s_nm, b + 1)
                wait_reg(pe, sq_b, b + 1)
                wait_reg(pe, s_oc, 2 * b + 2)
                for g in range(4):
                    G = (g + 1) % 4
                    col = g * (P + DEC_T) + P if g < 3 else NEW_A
                    for c in range(NC):
                        pe.matmul(bank(2)[0:NS, col:col + DEC_T], q_all[:, G, c, :], kTn[:, 4 * g + c, :],
                                  start=(g == 0 and c == 0), stop=(c == NC - 1), skip_group_check=True)
                for T in range(29):
                    if T + 1 < 29:
                        keys_turn(T + 1)
                    score(T)

                wait_reg(pe, s_ea, b + 1)
                for g in range(3):
                    col = g * (P + DEC_T)
                    pe.transpose(bank(5)[:, g * NS:(g + 1) * NS], s_a[:, col:col + P], ident[0:NS, 0:NS])
                    ins = pe.transpose(bank(5)[0:DEC_T, 192 + g * NS:192 + (g + 1) * NS],
                                       s_a[:, col + P:col + P + DEC_T], ident[0:NS, 0:NS])
                ins.then_inc(s_pa, 1)
                wait_reg(pe, s_pam, b + 1)
                wait_reg(pe, s_om, 2 * b + 1 + 1)
                for T in range(13):
                    per = 2 if T < 9 else 1
                    wait_reg(pe, sv_in[T], 16 * per * b + 16)
                    pt = pT0[:, :] if T == 0 else (pT1[:, T - 1, :] if T < 5 else pT2[:, T - 5, :])
                    pe.matmul(bank(7)[0:NS], pt, v_in[:, T, :], start=(T == 0), stop=False,
                              skip_group_check=True).then_inc(s_pv, 1)
                for g in range(3):
                    ins = pe.matmul(bank(7)[0:NS], pTn[:, g, :], kv_new[:, 1, g, :], start=False, stop=(g == 2),
                                    skip_group_check=True)
                ins.then_inc(s_va, 1)
                wait_reg(pe, s_eb, b + 1)
                for j in range(2):
                    for p in range(8):
                        pg = 8 * j + p
                        ins = pe.transpose(bank(3 + j)[:, p * NS:(p + 1) * NS], s_b[:, pg * P:(pg + 1) * P],
                                           ident[0:NS, 0:NS])
                    if j == 1:
                        ins = pe.transpose(bank(5)[0:DEC_T, 0:NS], s_b[:, PAST:KEYS_B], ident[0:NS, 0:NS])
                    ins.then_inc(s_pb, 1)
                wait_reg(pe, s_om, 2 * b + 2)
                for pg in range(N_PAGES):
                    T = 13 + pg
                    if pg % 8 == 0:
                        wait_reg(pe, s_pbm, 2 * b + 2 + pg // 8 + 1)
                    slot, per, k = (T, 1, 1) if T < 20 else (T - 20, 2, 2)
                    wait_reg(pe, sv_in[slot], 16 * per * b + 16 * k)
                    pe.matmul(bank(6)[0:NS], pTb[:, pg, :], v_in[:, slot, :], start=(pg == 0), stop=False,
                              skip_group_check=True).then_inc(s_pv, 1)
                pe.matmul(bank(6)[0:NS], pTn[:, 3, :], kv_new[:, 1, 3, :], start=False, stop=True,
                          skip_group_check=True).then_inc(s_vb, 1)
                wait_reg(pe, s_om, 2 * b + 2 + 1)
                pe.matmul(bank(2)[0:DEC_T], sel[:, :], om[:, 0, :], start=True, stop=True).then_inc(s_sel, 1)
                wait_reg(pe, s_om, 2 * b + 2 + 2)
                wait_reg(pe, s_oc, 2 * b + 2 + 1)
                pe.matmul(bank(2)[0:DEC_T], sel[:, :], om[:, 1, :], start=True, stop=True).then_inc(s_sel, 1)

            for u in range(FIRST_GATE, len(U)):
                block_(u)


def shape_constants():
    f = np.float32
    slopes_a = (2.0 ** (-8.0 * np.arange(1, 25) / 24)).astype(f).reshape(3, A_HEADS)
    slopes_b = (2.0 ** (-8.0 * np.arange(1, B_HEADS + 1) / B_HEADS)).astype(f)
    p = np.arange(P)[:, None]
    x = np.arange(2 * P)[None, :]
    bias_a = np.full((3, A_HEADS, P, 2 * P), MASKED, f)
    steps = p + P - x
    for g in range(2):
        ok = (steps >= 0) & (steps <= P)
        for h in range(A_HEADS):
            bias_a[g, h] = np.where(ok, slopes_a[g, h] * (steps * WINDOWS[g][1]).astype(f), f(MASKED))
    ok = (steps >= 0) & (steps % 2 == 0) & (x >= P)
    for h in range(A_HEADS):
        bias_a[2, h] = np.where(ok, slopes_a[2, h] * (steps * 8).astype(f), f(MASKED))
    dist = p - (np.arange(SEQ)[None, :] - (SEQ - P))
    bias_b = np.stack([np.where(dist >= 0, s * dist.astype(f), f(MASKED)) for s in slopes_b]).astype(f)
    c, t, hh = (a.reshape(-1) for a in np.meshgrid(np.arange(NC), np.arange(DEC_T), np.arange(2), indexing="ij"))
    bias_sa = np.full((NS, NEW_A), MASKED, f)
    bias_sb = np.full((NS, KEYS_B), MASKED, f)
    m = np.arange(P)[None, :]
    j = np.arange(DEC_T)[None, :]
    for g, (win, dil) in enumerate(WINDOWS):
        n = win // dil
        s = n + (t[:, None] // dil if dil < DEC_T else 0 * t[:, None]) - m
        slope = slopes_a[g][2 * c + hh][:, None]
        col = g * (P + DEC_T)
        bias_sa[:, col:col + P] = np.where(s <= n, slope * (s * dil).astype(f), f(MASKED))
        back = t[:, None] - j
        bias_sa[:, col + P:col + P + DEC_T] = np.where((back >= 0) & (back % dil == 0) & (back <= win),
                                                       slope * back.astype(f), f(MASKED))
    back = PAST + t[:, None] - np.arange(KEYS_B)[None, :]
    bias_sb[:] = np.where(back >= 0, slopes_b[c][:, None] * back.astype(f), f(MASKED))
    e = np.arange(CW)[None, :]
    mask = np.stack([e // HD == (2 * c + hh)[:, None], e // P == c[:, None]]).astype(f)
    sel = (t[:, None] == j).astype(f)
    coef = np.stack([hh == 0, hh == 1], axis=1).astype(f)
    return dict(ident=np.eye(P, dtype=f), bias_a=bias_a, bias_b=bias_b, bias_sa=bias_sa, bias_sb=bias_sb,
                mask=mask, sel=sel, coef=coef)


_INS = ["x_prompt", "x_sample", "cache_a0_kv", "cache_a1_kv", "cache_a2_kv", "cache_b_kv", "page_table", "norm_g",
        "w_in", "q_norm_a", "k_norm_a", "q_norm_b", "k_norm_b", "lambda_q1", "lambda_k1", "lambda_q2",
        "lambda_k2", "subln_g", "w_proj_a", "w_proj_b", "w_out"]
_OUTS = [(1, SEQ, D_MODEL), (DEC_B, DEC_T, D_MODEL),
         (1, 1, 128, 2, A_HEADS, HD), (1, 1, 512, 2, A_HEADS, HD), (1, 1, 1024, 2, A_HEADS, HD),
         (1, 1, SEQ, 2, B_HEADS, P),
         (1, DEC_B, 128, 2, A_HEADS, HD), (1, DEC_B, 512, 2, A_HEADS, HD), (1, DEC_B, 2048, 2, A_HEADS, HD),
         (1, DEC_B, DEC_T, 2, B_HEADS, P)]


def kernel(**inputs):
    import concourse.bacc as bacc
    from concourse.bass_utils import run_bass_kernel_spmd

    nc = bacc.Bacc("TRN2", target_bir_lowering=False, num_devices=1)
    arrays, aps = {}, {}
    for name, a in [(n, inputs[n]) for n in _INS] + list(shape_constants().items()):
        a = np.ascontiguousarray(a)
        arrays[f"in_{name}"] = a
        aps[name] = nc.dram_tensor(f"in_{name}", a.shape, mybir.dt.from_np(a.dtype), kind="ExternalInput").ap()
    outs = [nc.dram_tensor(f"out_{i}", shape, F32, kind="ExternalOutput").ap() for i, shape in enumerate(_OUTS)]
    i = aps
    build_step(nc, i["x_prompt"], i["x_sample"], [i["cache_a0_kv"], i["cache_a1_kv"], i["cache_a2_kv"]],
               i["cache_b_kv"], i["page_table"], i["norm_g"], i["w_in"], i["q_norm_a"], i["k_norm_a"],
               i["q_norm_b"], i["k_norm_b"], i["lambda_q1"], i["lambda_k1"], i["lambda_q2"], i["lambda_k2"],
               i["subln_g"], i["w_proj_a"], i["w_proj_b"], i["w_out"], i["ident"], i["bias_a"], i["bias_b"],
               i["bias_sa"], i["bias_sb"], i["mask"], i["sel"], i["coef"],
               outs[0], outs[1], outs[2:5], outs[5], outs[6:9], outs[9])
    r = run_bass_kernel_spmd(nc, [arrays], core_ids=[0])
    return tuple(r.results[0][f"out_{k}"] for k in range(len(_OUTS)))
```

```python
from contextlib import ExitStack

import numpy as np

import concourse.bass as bass
from concourse import mybir

ALU = mybir.AluOpType
ACT = mybir.ActivationFunctionType
AX_X = mybir.AxisListType.X
F32 = mybir.dt.float32
F32R = mybir.dt.float32r
I32 = mybir.dt.int32

P = 128
D_MODEL = 1024
SEQ = 1024
DEC_B = 8
DEC_T = 8
NS = DEC_B * DEC_T
ROWS = SEQ + NS
HD = 64
WINDOWS = ((128, 1), (512, 4), (2048, 16))
PAST = 2048
PAGE = 128
N_PAGES = PAST // PAGE
A_HEADS = 8
B_HEADS = 4
CW = 512
EPS = 1e-6
LAM_INIT = 0.2
MASKED = 1e30
NT = SEQ // P
TILES = NT + 1
NC = CW // P
KC = D_MODEL // P
NEW_A = 3 * (P + DEC_T)
KEYS_B = PAST + DEC_T

A_QKV = len(WINDOWS) * CW
COL = dict(qa=0, ka=A_QKV, va=2 * A_QKV, ga=3 * A_QKV, qb=3 * A_QKV + CW, kb=3 * A_QKV + 2 * CW,
           vb=3 * A_QKV + 3 * CW, gb=3 * A_QKV + 4 * CW, ma=3 * A_QKV + 5 * CW,
           mb=3 * A_QKV + 5 * CW + D_MODEL)


def weight_blocks():
    blocks = []
    for part, kind in (("qb", "q"), ("kb", "k"), ("vb", "v")):
        blocks.append((kind, 0, "in", COL[part], KC))
    for g in range(3):
        for part, kind in (("qa", "q"), ("ka", "k"), ("va", "v")):
            blocks.append((kind, g + 1, "in", COL[part] + g * CW, KC))
    for br in ("a", "b"):
        blocks.append(("g" + br, 0, "in", COL["g" + br], KC))
        for half in range(2):
            blocks.append(("m" + br, half, "in", COL["m" + br] + half * CW, KC))
            blocks.append(("p" + br, half, "proj_" + br, half * CW, NC))
    for half in range(2):
        blocks.append(("out", half, "out", half * CW, KC))
    return blocks


def width_a(G, i):
    if G == 1:
        return P if i == 0 else 2 * P
    if G == 2:
        return 2 * P if i % 2 else P
    return P


COPIES_IN = ((0, 1, 2), (3, 4), (5, 6), (7,))
TILE_ORDER = (7, 0, 6, 1, 5, 2, 4, 3)


def pieces_of(e):
    n = TILE_ORDER[e % 8] + 1
    p = pieces_before(e)
    return [(p, 0, n)] if n <= 4 else [(p, 0, 4), (p + 1, 4, n - 4)]


def pieces_before(e):
    whole, e = divmod(e, 16)
    return 24 * whole + sum(1 if TILE_ORDER[x % 8] < 4 else 2 for x in range(e))


def build_step(nc, x_p, x_s, ca, cb, page_table, norm_g, w_in, qna, kna, qnb, knb, lq1, lk1, lq2, lk2,
               subln, w_pa, w_pb, w_o, c_ident, c_bias_a, c_bias_b, c_bias_sa, c_bias_sb, c_mask, c_sel,
               c_coef, y_p, y_s, na_p, nb_p, na_s, nb_s):
    ds = bass.ds
    U = weight_blocks()
    w_dram = {"in": w_in[0], "proj_a": w_pa[0], "proj_b": w_pb[0], "out": w_o[0]}
    first_chunk = [0]
    for blk in U:
        first_chunk.append(first_chunk[-1] + blk[4])
    n_phys = cb.shape[1]
    FIRST_GATE = 12
    U_OUT = 22

    def nrows(i):
        return P if i < NT else NS

    with ExitStack() as ctx:
        def sem(name):
            return ctx.enter_context(nc.semaphore(name))

        def dram(name, shape):
            return nc.dram_tensor(name, shape, F32, kind="Internal").ap()

        top = [(nc.sbuf_base + 63) // 64 * 64]

        def place(name, shape, dt=F32, at=None):
            size = 4 * int(np.prod(shape[1:]))
            off = top[0] if at is None else at[0]
            t = nc.alloc_sbuf_tensor_at(name, list(shape), dt, offset=off)
            (top if at is None else at)[0] = off + (size + 31) // 32 * 32
            return t

        hT_hi = place("hT_hi", [P, KC, ROWS], F32R)
        hT_lo = place("hT_lo", [P, KC, ROWS], F32R)
        ident = place("ident", [P, P])
        gcol = place("gcol", [P, KC])
        qcol = place("qcol", [P, 2])
        krow = place("krow", [P, 2, HD])
        lamv = place("lamv", [P, 4, HD])
        lam = place("lam", [P, 8])
        subrow = place("subrow", [P, P])
        half_pow = place("half_pow", [P, 8])
        ss = place("ss", [P, 2, 8])
        rs = place("rs", [P, 2, 8])
        ss_x = place("ss_x", [P, 2, 1])
        rs_x = place("rs_x", [P, 2, 1])
        qTs = place("qTs", [P, 4, NC, NS])
        coef = place("coef", [NS, 2])
        st_sum = place("st_sum", [P, 2, 2, 16])
        st = place("st", [P, NT, 16])
        rlB = place("rlB", [P, 2, NT, 2])
        wB = place("wB", [P, 2, NT])
        sc_s = place("sc_s", [NS, 16])
        w_base = top[0]
        raw = place("raw", [P, 4, CW])
        w_hi, w_lo, set_at = [], [], []
        for s in range(2):
            set_at.append(top[0])
            w_hi.append(place(f"w_hi{s}", [P, KC, CW], F32R))
            w_lo.append(place(f"w_lo{s}", [P, KC, CW], F32R))
        q_base = top[0]
        qT = place("qT", [P, NC * SEQ])
        k_base = top[0]
        kT = place("kT", [P, NC * SEQ])
        v_sb = place("v_sb", [P, TILES, CW])
        work = top[0]
        zn = place("zn", [P, 2, CW])
        kn = place("kn", [P, 3, CW])
        end = top[0]
        assert end <= nc.sbuf_usable_end, end
        at = [k_base]
        xt = place("xt", [P, 2, D_MODEL], at=at)
        xn = place("xn", [P, 2, D_MODEL], at=at)
        hn = place("hn", [P, 2, CW], at=at)
        at = [work]
        qz = place("qz", [P, 2, SEQ], at=at)
        att = []
        for s in range(2):
            at = [set_at[s]]
            if s == 0:
                sB = [place(f"sB{j}", [P, 2, P * (1 + max(TILE_ORDER[j::4]))], at=at) for j in range(4)]
                ptB = place("ptB", [P, 4, CW], at=at)
                assert at[0] <= set_at[s] + 2 * 4 * KC * CW
            at = [set_at[s]]
            att.append(dict(sA=place(f"sA{s}", [P, 8, 256], at=at), tA=place(f"tA{s}", [P, 2, 2, 256], at=at),
                            ptA=place(f"ptA{s}", [P, 4, 256], at=at)))
        tB = place("tB", [P, 2, SEQ], at=[w_base])
        NKS, NVS = 8, 20
        at = [w_base]
        k_in = place("k_in", [P, NKS, CW], at=at)
        v_in = place("v_in", [P, NVS, CW], at=at)
        new_and_out = place("new_and_out", [P, 2, 4, CW], at=at)
        kv_new = new_and_out[0:DEC_T]
        os_ = new_and_out[HD:HD + DEC_T, 0, 0:2, :]
        q_all = place("q_all", [P, 4, NC, NS], at=at)
        q_g1 = place("q_g1", [P, 4, NC, NS], at=at)
        q_g2 = place("q_g2", [P, 8, NC, NS], at=at)
        kTs = place("kTs", [P, 2, NC, P], at=at)
        kTn = place("kTn", [P, 16, DEC_T], at=at)
        s_a = place("s_a", [NS, NEW_A], at=at)
        bias_sa = place("bias_sa", [NS, NEW_A], at=at)
        s_b = place("s_b", [NS, KEYS_B], at=at)
        bias_sb = place("bias_sb", [NS, KEYS_B], at=at)
        pT0 = place("pT0", [P, NS], at=at)
        pT1 = place("pT1", [P, 4, NS], at=at)
        pT2 = place("pT2", [P, 8, NS], at=at)
        pTn = place("pTn", [DEC_T, 4, NS], at=at)
        pTb = place("pTb", [P, N_PAGES, NS], at=at)
        mask = place("mask", [NS, 2, CW], at=at)
        om = place("om", [NS, 2, CW], at=at)
        sel = place("sel", [NS, DEC_T], at=at)
        pids = place("pids", [1, DEC_B * N_PAGES], I32, at=at)
        assert at[0] <= end, (at[0], end)
        at = [q_base]
        yT_hi = place("yT_hi", [P, NC, ROWS], F32R, at=at)
        yT_lo = place("yT_lo", [P, NC, ROWS], F32R, at=at)
        sig_at = at[0]
        sig = place("sig", [P, TILES, CW], at=at)
        zy = place("zy", [P, 2, CW], at=at)
        stc = place("stc", [P, NT, 3, 16], at=at)
        ew = place("ew", [P, NT, 3, 8], at=at)
        el = place("el", [P, NT, 3, 8], at=at)
        nmin = place("nmin", [P, NT, 8], at=at)
        den = place("den", [P, NT, 8], at=at)
        assert at[0] <= end, (at[0], end)
        at = [sig_at]
        og = place("og", [P, 2, 3, CW], at=at)
        sg = place("sg", [P, 2, CW], at=at)
        at = [q_base]
        mt = place("mt", [P, 2, D_MODEL], at=at)
        xl = place("xl", [P, 2, CW], at=at)
        yo = place("yo", [P, 3, CW], at=at)

        ps = ctx.enter_context(nc.psum_tensor("ps", [P, 8 * CW], F32))

        def bank(b, n=1):
            return ps[:, b * CW:(b + n) * CW]

        o_scr = [dram(f"o_scr{g}", [SEQ, CW]) for g in range(4)]
        st_scr = [dram(f"st_scr{g}", [SEQ, 16]) for g in range(3)]
        os_scr = dram("os_scr", [2, NS, CW])
        ma_scr = dram("ma_scr", [ROWS, D_MODEL])
        m_scr = dram("m_scr", [ROWS, D_MODEL])

        const_in = sem("const_in")
        setup = sem("setup")
        x_in = [sem(f"x_in{s}") for s in range(2)]
        h_ss, h_rs, h_xn, h_t, h_hn, h_hi, h_lo = (sem(n) for n in (
            "h_ss", "h_rs", "h_xn", "h_t", "h_hn", "h_hi", "h_lo"))
        pool_step = sem("pool_step")
        dve_step = sem("dve_step")
        raw_in = [sem(f"raw_in{s}") for s in range(4)]
        hi_done, lo_done = sem("hi_done"), sem("lo_done")
        z_ready = sem("z_ready")
        sq_ready, ss_ready, rs_ready = sem("sq_ready"), sem("ss_ready"), sem("rs_ready")
        zn_ready, kn_ready, v_ready = sem("zn_ready"), sem("kn_ready"), sem("v_ready")
        t_ready, t_moved = sem("t_ready"), sem("t_moved")
        k_out = [sem(f"k_out{s}") for s in range(3)]
        v_out, o_out = sem("v_out"), sem("o_out")
        copies = sem("copies")
        bq, bs, be, ba, bt, bm, bp, bo, bw, btab = (sem(n) for n in (
            "b_scores", "b_biased", "b_exp", "b_diff", "b_probsT", "b_probsT_moved", "b_piece_used",
            "b_stored", "b_weight", "b_table"))
        aq, as_, ae, atp, am, av, ao, ast, atab = (sem(n) for n in (
            "a_scores", "a_biased", "a_exp", "a_probsT", "a_probsT_moved", "a_values", "a_stored",
            "a_stats", "a_table"))
        btab2, atab2 = sem("b_table1"), sem("a_table1")
        qz_ready = sem("qz_ready")
        s_const = sem("s_const")
        sk_in = [sem(f"sk_in{s}") for s in range(NKS)]
        sv_in = [sem(f"sv_in{s}") for s in range(NVS)]
        sn_in, sq_b = sem("sn_in"), sem("s_queries")
        s_kt, s_km, s_qk, s_nt, s_nm = (sem(n) for n in (
            "s_keysT", "s_keysT_moved", "s_scored", "s_newT", "s_newT_moved"))
        s_ta, s_tb, s_min, s_ea, s_eb = (sem(n) for n in (
            "s_biased_a", "s_biased_b", "s_min_b", "s_exp_a", "s_exp_b"))
        s_pa, s_pam, s_pb, s_pbm = (sem(n) for n in (
            "s_probsT_a", "s_probsT_a_moved", "s_probsT_b", "s_probsT_b_moved"))
        s_pv, s_va, s_vb, s_om, s_sel, s_oc, s_out, s_rec = (sem(n) for n in (
            "s_tile_used", "s_values_a", "s_values_b", "s_masked", "s_summed", "s_o_copied", "s_o_out",
            "s_recip"))
        s_zero = sem("s_zero")
        st_in, ew_ready, ew_exp = sem("st_in"), sem("ew_ready"), sem("ew_exp")
        og_in = [sem(f"og_in{s}") for s in range(2)]
        sg_ready, silu_ready, og_pool, y_ready, y_t, y_hi, y_lo = (sem(n) for n in (
            "sg_ready", "silu_ready", "og_pool", "y_ready", "y_t", "y_hi", "y_lo"))
        osq, oss, ors = sem("o_square"), sem("o_sum"), sem("o_rstd")
        sig_ready, m_ready = sem("sig_ready"), sem("m_ready")
        m_out = sem("m_out")
        ml_in = [sem(f"ml_in{s}") for s in range(2)]
        mt_in = [sem(f"mt_in{s}") for s in range(2)]
        m_t, m_hi, m_lo = sem("m_t"), sem("m_hi"), sem("m_lo")
        xl_in = [sem(f"xl_in{s}") for s in range(2)]
        yo_ready = sem("yo_ready")
        yo_out = [sem(f"yo_out{s}") for s in range(3)]

        N_CONST = 16 * 14

        def mi(G, kind, i):
            return 18 * G + (9 if kind == "k" else 0) + i

        def ti(G, kind, i):
            return 17 * G + (9 if kind == "k" else 0) + i

        def x_bank(j):
            return 4 + j if j < 4 else 7

        def z_freed(n):
            u, i = divmod(n, TILES)
            kind, G = U[u][0], U[u][1]
            br = 9 if kind[-1] == "b" else 0
            if kind in "qk":
                return zn_ready, mi(G, kind, i) + 1
            if kind == "v":
                return v_ready, 9 * G + i + 1
            if kind in ("ga", "gb"):
                return silu_ready, br + i + 1
            if kind in ("ma", "mb"):
                return sig_ready, 2 * br + 9 * G + i + 1
            if kind in ("pa", "pb"):
                return m_ready, 2 * br + 9 * G + i + 1
            return yo_ready, 9 * G + i + 1

        def row_start_step(G, i):
            if G <= 1:
                return i * P, 1
            if G == 2:
                return (i // 2) + (i % 2) * 512, 4
            return i, 8

        def rows_of(ap, G, i):
            a, s = row_start_step(G, i)
            return ap[a:a + s * (P - 1) + 1:s] if s > 1 else ap[a:a + P]

        def hT_of(h, G, k, i):
            if i == NT:
                return h[:, k, SEQ:ROWS]
            a, s = row_start_step(G, i)
            return h[:, k, a:a + s * (P - 1) + 1:s]

        def kept(G, i, kv):
            if G == 0:
                return nb_p[0, 0, i * P:(i + 1) * P, kv].rearrange("s h e -> s (h e)")
            out = na_p[G - 1][0, 0, :, kv].rearrange("s h e -> s (h e)")
            if G == 1:
                return out if i == NT - 1 else None
            if G == 2:
                return out[i // 2::4] if i % 2 else None
            return out[i::8]

        def kept_new(G, kv):
            if G == 0:
                return nb_s[0, :, :, kv].rearrange("b t h e -> b t (h e)")
            length = WINDOWS[G - 1][0]
            return na_s[G - 1][0, :, length - DEC_T:length, kv].rearrange("b t h e -> b t (h e)")

        k_sent = {s: [0] * (4 * TILES) for s in range(3)}
        v_sent = []
        for s in range(3):
            c = 0
            for kk in range(4 * TILES):
                G, i = divmod(kk, TILES)
                if kk % 3 == s and (i == NT or kept(G, i, 0) is not None):
                    c += 16
                k_sent[s][kk] = c
        c = 0
        for G in range(4):
            for i in range(TILES):
                c += 16 if (i == NT or kept(G, i, 1) is not None) else 0
            v_sent.append(c)

        def og_total(y):
            return sum(48 if yy < NT else 16 for yy in range(y % 2, y + 1, 2))

        def wait_reg(eng, s, value):
            eng.wait_ge(s, value)
            eng.nop(nofuse=True)

        block = ctx.enter_context(nc.Block())

        @block.sync
        def _(sp):
            sp.dma_start(ident[:, :], c_ident).then_inc(const_in, 16)
            sp.dma_start(gcol[:, :], norm_g[0].rearrange("(c p) -> p c", p=P), allow_slow_non_contiguous=True).then_inc(const_in, 16)

            def load_x(i):
                if i >= 2:
                    sp.wait_ge(h_xn, i - 1)
                src = x_p[0, i * P:(i + 1) * P, :] if i < NT else x_s.rearrange("b t d -> (b t) d")
                sp.dma_start(xt[0:nrows(i), i % 2, :], src).then_inc(x_in[i % 2], 16)

            load_x(0)
            load_x(1)
            for col, vec in ((0, qna), (1, qnb)):
                for h in range(2):
                    sp.dma_start(qcol[h * HD:(h + 1) * HD, col:col + 1],
                                 vec[0].rearrange("(d o) -> d o", o=1)).then_inc(const_in, 16)
            for col, vec in ((0, kna), (1, knb)):
                sp.dma_start(krow[:, col, :], vec[0].partition_broadcast(P)).then_inc(const_in, 16)
            for col, vec in enumerate((lq1, lk1, lq2, lk2)):
                sp.dma_start(lamv[:, col, :], vec[0].partition_broadcast(P)).then_inc(const_in, 16)
            sp.dma_start(coef[:, :], c_coef).then_inc(const_in, 16)
            sp.dma_start(subrow[:, :], subln[0].partition_broadcast(P)).then_inc(const_in, 16)

            def load_chunk(u, k):
                q = first_chunk[u] + k
                if q >= 4:
                    sp.wait_ge(lo_done, q - 3)
                _, _, name, col, _ = U[u]
                sp.dma_start(raw[:, q % 4, :], w_dram[name][k * P:(k + 1) * P, col:col + CW])\
                    .then_inc(raw_in[q % 4], 16)

            for k in range(4):
                load_chunk(0, k)
            load_x(2)
            for k in range(4, KC):
                load_chunk(0, k)

            def block_io(u):
                kind, G = U[u][0], U[u][1]
                prefetch = u + 1 < len(U) and u + 1 != FIRST_GATE
                for i in range(TILES):
                    if u == 0 and 3 <= i + 3 < TILES:
                        load_x(i + 3)
                    if prefetch and i < U[u + 1][4]:
                        load_chunk(u + 1, i)
                    if kind == "k":
                        kk = TILES * G + i
                        dst = kept(G, i, 0) if i < NT else kept_new(G, 0)
                        if dst is not None:
                            sp.wait_ge(kn_ready, kk + 1)
                            sp.dma_start(dst, kn[0:nrows(i), kk % 3, :])\
                                .then_inc(k_out[kk % 3], 16)
                    if kind == "v":
                        dst = kept(G, i, 1) if i < NT else kept_new(G, 1)
                        if dst is not None:
                            sp.wait_ge(v_ready, TILES * G + i + 1)
                            sp.dma_start(dst, v_sb[0:nrows(i), i, :]).then_inc(v_out, 16)

            def tables(G):
                set_ = (3 * G + 2) % 2
                if G == 0:
                    sp.wait_ge(lo_done, first_chunk[4])
                    for h in range(B_HEADS):
                        if h >= 2:
                            sp.wait_ge(bs, 16 + 16 * (h - 1))
                        sp.dma_start(tB[:, h % 2, :], c_bias_b[h])\
                            .then_inc(btab if h % 2 == 0 else btab2, 16)
                else:
                    for c in range(NC):
                        if c < 2:
                            sp.wait_ge(z_ready, 27 * (G + 1))
                        else:
                            sp.wait_ge(as_, 16 + 64 * (G - 1) + 16 * (c - 1))
                        sp.dma_start(att[set_]["tA"][:, c % 2, :, :],
                                     c_bias_a[G - 1, 2 * c:2 * c + 2].rearrange("h p x -> p h x"))\
                            .then_inc(atab if c % 2 == 0 else atab2, 16)

            def attention_out(G):
                if G == 0:
                    sp.wait_ge(bo, 8 + 32)
                else:
                    sp.wait_ge(ao, 8 + 32 * G)
                    sp.wait_ge(ast, 4 * G)
                for i in range(NT):
                    sp.dma_start(rows_of(o_scr[G], G, i).rearrange("s (c e) -> s c e", c=NC),
                                 qT[:, :].rearrange("p (c s) -> p c s", c=NC)[:, :, i * P:(i + 1) * P])\
                        .then_inc(o_out, 16)
                    if G:
                        sp.dma_start(rows_of(st_scr[G - 1], G, i), st[:, i, :]).then_inc(o_out, 16)

            for G in range(4):
                for kind in range(3):
                    block_io(3 * G + kind)
                tables(G)
                attention_out(G)

            sp.wait_ge(o_out, 16 * 8 * 7)
            sp.dma_start(pids[0:1, :], page_table.rearrange("b n -> (b n)").rearrange("(o n) -> o n", o=1))\
                .then_inc(s_const, 16)
            sp.dma_start(bias_sa[:, :], c_bias_sa).then_inc(s_const, 16)
            sp.dma_start(bias_sb[:, :], c_bias_sb).then_inc(s_const, 16)
            sp.dma_start(mask[:, :, :], c_mask.rearrange("g q e -> q g e")).then_inc(s_const, 16)
            sp.dma_start(sel[:, :], c_sel).then_inc(s_const, 16)
            sp.wait_ge(s_const, 80)
            for s in range(3):
                sp.wait_ge(k_out[s], k_sent[s][-1])
            sp.wait_ge(v_out, v_sent[-1])

            with sp.Fori(0, DEC_B) as b:
                wait_reg(sp, s_vb, b + 1)
                for kv in range(2):
                    for g in range(3):
                        ln = WINDOWS[g][0]
                        sp.dma_start(kv_new[:, kv, g, :],
                                     na_s[g][0, ds(b, 1), ln - DEC_T:ln, kv].rearrange("o t h e -> (o t) (h e)"))\
                            .then_inc(sn_in, 16)
                    sp.dma_start(kv_new[:, kv, 3, :],
                                 nb_s[0, ds(b, 1), :, kv].rearrange("o t h e -> (o t) (h e)"))\
                        .then_inc(sn_in, 16)

                def rows_a(T, kv):
                    g, r = (0, 0) if T == 0 else ((1, T - 1) if T < 5 else (2, T - 5))
                    dil = WINDOWS[g][1]
                    return ca[g][0, ds(b, 1), r::dil, kv].rearrange("o m h e -> (o m) (h e)")

                def load_k(T, src):
                    if T >= NKS:
                        wait_reg(sp, s_kt, 29 * b + 29 + T - 7)
                    else:
                        wait_reg(sp, s_kt, 29 * b + (T + 24 if T + 24 <= 28 else T + 16) + 1)
                    sp.dma_start(k_in[:, T % NKS, :], src).then_inc(sk_in[T % NKS], 16)

                def load_v(T, src):
                    if T < 13:
                        slot, last = T, (29 * b + 20 + T + 1 if T < 9 else 29 * b + T + 1)
                    elif T < 20:
                        slot, last = T, 29 * b + T + 1
                    else:
                        slot, last = T - 20, 29 * b + 29 + T - 20 + 1
                    wait_reg(sp, s_pv, last)
                    sp.dma_start(v_in[:, slot, :], src).then_inc(sv_in[slot], 16)

                for T in range(13):
                    load_k(T, rows_a(T, 0))
                    load_v(T, rows_a(T, 1))
                pages = []
                for j in range(N_PAGES):
                    pid = sp.value_load(pids[0:1, ds(b * N_PAGES + j, 1)], min_val=0, max_val=n_phys - 1)
                    load_k(13 + j, cb[0, ds(pid, 1), :, 0].rearrange("o s h e -> (o s) (h e)"))
                    if j < 7:
                        load_v(13 + j, cb[0, ds(pid, 1), :, 1].rearrange("o s h e -> (o s) (h e)"))
                for j in range(7, N_PAGES):
                    pid = sp.value_load(pids[0:1, ds(b * N_PAGES + j, 1)], min_val=0, max_val=n_phys - 1)
                    load_v(13 + j, cb[0, ds(pid, 1), :, 1].rearrange("o s h e -> (o s) (h e)"))

            sp.wait_ge(s_out, 32 + 32 * DEC_B)
            for k in range(KC):
                load_chunk(FIRST_GATE, k)
            for g in range(3):
                sp.dma_start(stc[:, :, g, :], st_scr[g].rearrange("(i p) s -> p i s", p=P)).then_inc(st_in, 16)

            def load_og(y):
                br, i = divmod(y, TILES)
                if y >= 2:
                    sp.wait_ge(y_ready, y - 1)
                if i == NT:
                    sp.dma_start(og[0:NS, y % 2, 0, :], os_scr[br]).then_inc(og_in[y % 2], 16)
                else:
                    for g in range(3 if br == 0 else 1):
                        src = o_scr[g + 1 if br == 0 else 0]
                        sp.dma_start(og[:, y % 2, g, :], src[i * P:(i + 1) * P, :]).then_inc(og_in[y % 2], 16)

            def rows_m(scr, i, half):
                return scr[i * P:i * P + nrows(i), half * CW:(half + 1) * CW]

            for u in range(FIRST_GATE, len(U)):
                kind, half = U[u][0], U[u][1]
                br = 1 if kind[-1] == "b" else 0
                if kind in ("ga", "gb"):
                    if br:
                        sp.wait_ge(m_out, 16 * 18)
                    load_og(9 * br)
                    load_og(9 * br + 1)
                if kind == "pb" and half == 0:
                    sp.wait_ge(y_t, 18)
                    for i in range(2):
                        sp.dma_start(zy[:, i, :], rows_m(ma_scr, i, 0)).then_inc(ml_in[i], 16)
                for i in range(TILES):
                    if u + 1 < len(U) and i < U[u + 1][4]:
                        load_chunk(u + 1, i)
                    if kind in ("ga", "gb") and i + 2 < TILES:
                        load_og(9 * br + i + 2)
                    if kind in ("pa", "pb"):
                        idx = 18 * br + 9 * half + i
                        sp.wait_ge(m_ready, idx + 1)
                        sp.dma_start(rows_m(m_scr if br else ma_scr, i, half), sig[0:nrows(i), i, :])\
                            .then_inc(m_out, 16)
                        nxt = 9 * half + i + 2
                        if br and nxt < 18:
                            hn_, in_ = divmod(nxt, 9)
                            sp.dma_start(zy[0:nrows(in_), nxt % 2, :], rows_m(ma_scr, in_, hn_))\
                                .then_inc(ml_in[nxt % 2], 16)
                    if kind == "out":
                        idx = 9 * half + i
                        if half == 0 and i == 0:
                            sp.wait_ge(m_out, 16 * 36)
                            for ii in range(2):
                                sp.dma_start(mt[0:nrows(ii), ii % 2, :], m_scr[ii * P:ii * P + nrows(ii), :])\
                                    .then_inc(mt_in[ii % 2], 16)
                            for ii in range(2):
                                sp.dma_start(xl[:, ii % 2, :], x_p[0, ii * P:(ii + 1) * P, 0:CW])\
                                    .then_inc(xl_in[ii % 2], 16)
                        if half == 0 and i + 2 < TILES:
                            ii = i + 2
                            sp.wait_ge(m_t, 2 * i + 2)
                            sp.dma_start(mt[0:nrows(ii), ii % 2, :], m_scr[ii * P:ii * P + nrows(ii), :])\
                                .then_inc(mt_in[ii % 2], 16)
                        sp.wait_ge(yo_ready, idx + 1)
                        dst = (y_p[0, i * P:(i + 1) * P, :] if i < NT else y_s.rearrange("b t d -> (b t) d"))
                        sp.dma_start(dst[:, half * CW:(half + 1) * CW], yo[0:nrows(i), idx % 3, :])\
                            .then_inc(yo_out[idx % 3], 16)
                        nxt = idx + 2
                        if nxt < 18:
                            hn_, in_ = divmod(nxt, 9)
                            src = (x_p[0, in_ * P:(in_ + 1) * P, :] if in_ < NT else
                                   x_s.rearrange("b t d -> (b t) d"))
                            sp.dma_start(xl[0:nrows(in_), nxt % 2, :], src[:, hn_ * CW:(hn_ + 1) * CW])\
                                .then_inc(xl_in[nxt % 2], 16)
            for s in range(3):
                sp.wait_ge(yo_out[s], 16 * 6)
            sp.wait_ge(copies, 16 * 3 * DEC_B)
            for s in range(3):
                sp.wait_ge(k_out[s], k_sent[s][-1])
            sp.wait_ge(v_out, v_sent[-1])

        @block.gpsimd
        def _(pool):
            steps = [0]

            def link(ins):
                steps[0] += 1
                ins.then_inc(pool_step, 1)
                pool.wait_ge(pool_step, steps[0])

            link(pool.memset(half_pow[:, :], -0.5))

            def rstd(out, in_, n, heads):
                r = in_.shape[0]
                link(pool.tensor_scalar(in_, in_, 1.0 / n, EPS, ALU.mult, ALU.add))
                return pool.tensor_tensor(out, in_, half_pow[0:r, 0:heads], ALU.pow)

            def input_lo(i):
                for half in range(2):
                    j = 2 * i + half
                    pool.wait_ge(h_hi, j + 1)
                    c0 = i * P
                    pool.tensor_tensor(hT_lo[:, 4 * half:4 * half + 4, c0:c0 + nrows(i)],
                                       hn[:, half, :].rearrange("p (k r) -> p k r", k=4)[:, :, 0:nrows(i)],
                                       hT_hi[:, 4 * half:4 * half + 4, c0:c0 + nrows(i)].bitcast(F32),
                                       ALU.subtract).then_inc(h_lo, 1)

            def split_lo(u, k):
                q = first_chunk[u] + k
                pool.wait_ge(hi_done, q + 1)
                pool.tensor_tensor(w_lo[u % 2][:, k, :], raw[:, q % 4, :],
                                   w_hi[u % 2][:, k, :].bitcast(F32), ALU.subtract).then_inc(lo_done, 1)

            def input_step(i):
                if i < TILES:
                    pool.wait_ge(h_ss, i + 1)
                    rstd(rs_x[0:nrows(i), i % 2, 0:1], ss_x[0:nrows(i), i % 2, 0:1], D_MODEL, 1)\
                        .then_inc(h_rs, 1)
                if 1 <= i <= TILES:
                    input_lo(i - 1)

            for i in range(3):
                input_step(i)
            for k in range(KC):
                split_lo(0, k)

            def block_(u):
                kind, G = U[u][0], U[u][1]
                prefetch = u + 1 < len(U) and u + 1 != FIRST_GATE
                for i in range(TILES):
                    r = nrows(i)
                    if u == 0:
                        input_step(i + 3)
                    if kind in "qk":
                        m = mi(G, kind, i)
                        pool.wait_ge(ss_ready, m + 1)
                        rstd(rs[0:r, m % 2, :], ss[0:r, m % 2, :], HD, 8).then_inc(rs_ready, 1)
                    if prefetch and i < U[u + 1][4]:
                        split_lo(u + 1, i)
                    if kind == "k":
                        kk = TILES * G + i
                        pool.wait_ge(zn_ready, m + 1)
                        if kk >= 3:
                            G3, i3 = divmod(kk - 3, TILES)
                            pool.wait_ge(t_ready, ti(G3, "k", min(i3, NT - 1)) + 1)
                            if k_sent[kk % 3][kk - 3]:
                                pool.wait_ge(k_out[kk % 3], k_sent[kk % 3][kk - 3])
                        pool.tensor_tensor(kn[0:r, kk % 3, :].rearrange("p (h d) -> p h d", h=8),
                                           zn[0:r, m % 2, :].rearrange("p (h d) -> p h d", h=8),
                                           krow[0:r, 0 if G else 1, :].unsqueeze(1).to_broadcast([r, 8, HD]),
                                           ALU.mult).then_inc(kn_ready, 1)
                    if kind == "ga" and i < NT:
                        y = i
                        pool.wait_ge(ew_ready, 1)
                        pool.wait_ge(og_in[y % 2], 48 * (y // 2 + 1))
                        for g in (1, 2):
                            ins = pool.tensor_tensor(
                                og[:, y % 2, g, :].rearrange("p (h d) -> p h d", h=8),
                                og[:, y % 2, g, :].rearrange("p (h d) -> p h d", h=8),
                                ew[:, i, g, :].unsqueeze(2).to_broadcast([P, 8, HD]), ALU.mult)
                        ins.then_inc(og_pool, 1)
                    if kind == "gb":
                        pool.wait_ge(oss, i + 1)
                        rstd(rs[0:r, i % 2, 0:4], ss[0:r, i % 2, 0:4], P, 4).then_inc(ors, 1)

            def pad_queries(G):
                pool.wait_ge(t_ready, 17 * G + 17)
                for s in range(3):
                    pool.wait_ge(k_out[s], k_sent[s][TILES * G + NT])
                link(pool.memset(qz[0:HD, 1, :], 0.0))
                link(pool.memset(qz[HD:P, 0, :], 0.0))
                pool.wait_ge(t_moved, 17 * G + 9)
                scored = aq if G else bq
                first = 16 + 64 * (G - 1) if G else 16
                order = range(NT) if G else TILE_ORDER
                for i in order:
                    cols = slice(i * P, (i + 1) * P)
                    pool.tensor_copy(qz[0:HD, 0, cols], qT[0:HD, cols])
                    pool.tensor_copy(qz[HD:P, 1, cols], qT[HD:P, cols]).then_inc(qz_ready, 1)
                with pool.Fori(0, NC - 1) as c:
                    for s, i in enumerate(order):
                        wait_reg(pool, scored, first + 16 * c + 2 * s + 2)
                        cols = slice(i * P, (i + 1) * P)
                        pool.tensor_copy(qz[0:HD, 0, cols], qT[0:HD, ds((c + 1) * SEQ + i * P, P)])
                        pool.tensor_copy(qz[HD:P, 1, cols], qT[HD:P, ds((c + 1) * SEQ + i * P, P)])\
                            .then_inc(qz_ready, 1)

            for G in range(4):
                for kind in range(3):
                    block_(3 * G + kind)
                pad_queries(G)
                if G:
                    pool.wait_ge(aq, 16 + 64 * G)
                else:
                    pool.wait_ge(bq, 16 + 64)

            pool.wait_ge(o_out, 16 * 8 * 7)
            link(pool.memset(q_all[:, :, :, :], 0.0))
            link(pool.memset(q_g1[:, :, :, :], 0.0))
            link(pool.memset(q_g2[:, :, :, :], 0.0))
            link(pool.memset(pT1[:, :, :], 0.0))
            link(pool.memset(pT2[:, :, :], 0.0))
            pool.sem_inc(s_zero, 1)

            def spread(t, off, dims, hh):
                base = t[hh * HD:(hh + 1) * HD, 0, 0, 0:1]
                return bass.AP(base.tensor, base.offset + off, [list(base.ap[0])] + dims)

            with pool.Fori(0, DEC_B) as b:
                wait_reg(pool, s_qk, 29 * b + 29)
                for hh in range(2):
                    src = qTs[hh * HD:(hh + 1) * HD, :, :, ds(b * DEC_T, DEC_T)]
                    pool.tensor_copy(spread(q_all, hh, [[NC * NS, 4], [NS + 16, NC], [2, DEC_T]], hh), src)
                    pool.tensor_copy(
                        spread(q_g1, hh, [[NC * NS + 2, 4], [NS + 16, NC], [8, 2]], hh),
                        qTs[hh * HD:(hh + 1) * HD, 2, :, ds(b * DEC_T, DEC_T)].rearrange("p c (u r) -> p r c u", u=2))
                    ins = pool.tensor_copy(
                        spread(q_g2, hh, [[NC * NS + 2, 8], [NS + 16, NC]], hh),
                        qTs[hh * HD:(hh + 1) * HD, 3, :, ds(b * DEC_T, DEC_T)].rearrange("p c r -> p r c"))
                ins.then_inc(sq_b, 1)

            for k in range(KC):
                split_lo(FIRST_GATE, k)
            for u in range(FIRST_GATE, len(U)):
                block_(u)

        @block.scalar
        def _(act):
            def copy_cache(b):
                for g, piece in ((0, 1536), (1, 1536), (2, 2560)):
                    keep = WINDOWS[g][0] - DEC_T
                    dst = na_s[g][0, b, 0:keep].rearrange("s v h e -> (s v h e)")
                    src = ca[g][0, b, DEC_T:keep + DEC_T].rearrange("s v h e -> (s v h e)")
                    act.dma_start(dst.rearrange("(a m x) -> a m x", a=16, x=piece),
                                  src.rearrange("(a m x) -> a m x", a=16, x=piece)).then_inc(copies, 16)

            def input_hi(i):
                for half in range(2):
                    j = 2 * i + half
                    act.wait_ge(h_hn, j + 1)
                    act.activation(hT_hi[:, 4 * half:4 * half + 4, i * P:i * P + nrows(i)],
                                   hn[:, half, :].rearrange("p (k r) -> p k r", k=4)[:, :, 0:nrows(i)],
                                   ACT.Copy).then_inc(h_hi, 1)

            def split_hi(u, k):
                q = first_chunk[u] + k
                act.wait_ge(raw_in[q % 4], 16 * (q // 4 + 1))
                if u >= 2:
                    act.wait_ge(z_ready, TILES * (u - 1))
                act.activation(w_hi[u % 2][:, k, :], raw[:, q % 4, :], ACT.Copy).then_inc(hi_done, 1)

            def input_step(i):
                r = nrows(i)
                if i < TILES:
                    act.wait_ge(x_in[i % 2], 16 * (i // 2 + 1))
                    if i >= 2:
                        act.wait_ge(h_t, 2 * i - 2)
                        act.wait_ge(h_rs, i - 1)
                    act.activation(xn[0:r, i % 2, :], xt[0:r, i % 2, :], ACT.Square,
                                   accum_out=ss_x[0:r, i % 2, 0:1]).then_inc(h_ss, 1)
                if 1 <= i <= TILES:
                    input_hi(i - 1)

            for i in range(3):
                input_step(i)
            for k in range(KC):
                split_hi(0, k)
            act.wait_ge(setup, 2)
            act.activation(lam[:, 2:4], lam[:, 0:2], ACT.Exp).then_inc(setup, 1)

            def move(G, kind, i):
                t = ti(G, kind, i)
                act.wait_ge(t_ready, t + 1)
                src = bank(3 + t % 2).rearrange("p (c r) -> p c r", c=NC)
                if kind == "k":
                    act.activation(kT[:, :].rearrange("p (c s) -> p c s", c=NC)[:, :, i * P:(i + 1) * P], src, ACT.Copy).then_inc(t_moved, 1)
                    return
                if i == 0:
                    act.wait_ge(setup, 4)
                    if G:
                        act.wait_ge(o_out, 16 * 8 * (2 * G - 1))
                scale = qcol[:, (0 if G else 1):(0 if G else 1) + 1]
                if i < NT:
                    act.activation(qT[:, :].rearrange("p (c s) -> p c s", c=NC)[:, :, i * P:(i + 1) * P],
                                   src, ACT.Copy, scale=scale).then_inc(t_moved, 1)
                else:
                    act.activation(qTs[:, G, :, :],
                                   src[:, :, 0:NS], ACT.Copy, scale=scale).then_inc(t_moved, 1)

            def block_(u):
                kind, G = U[u][0], U[u][1]
                prefetch = u + 1 < len(U) and u + 1 != FIRST_GATE
                br = 1 if kind[-1] == "b" else 0
                for i in range(TILES):
                    n, r = TILES * u + i, nrows(i)
                    z = bank(n % 3)[0:r]
                    if u == 0:
                        input_step(i + 3)
                    if kind in "qk":
                        m = mi(G, kind, i)
                        act.wait_ge(z_ready, n + 1)
                        if m >= 2:
                            act.wait_ge(ss_ready, m - 1)
                        act.activation(bank(5 + m % 2)[0:r], z, ACT.Square).then_inc(sq_ready, 1)
                    if kind == "q" and i:
                        move(G, "q", i - 1)
                    if kind == "k":
                        move(G, "q", NT) if i == 0 else move(G, "k", i - 1)
                    if kind in ("ga", "gb"):
                        y = 9 * br + i
                        if y == TILES:
                            act.wait_ge(m_out, 16 * 18)
                        act.wait_ge(z_ready, n + 1)
                        if y >= 2:
                            act.wait_ge(y_ready, y - 1)
                        act.activation(sg[0:r, y % 2, :], z, ACT.Sigmoid).then_inc(sg_ready, 1)
                        if br:
                            act.wait_ge(og_in[y % 2], og_total(y))
                            act.activation(og[0:r, y % 2, 1, :], og[0:r, y % 2, 0, :], ACT.Square)\
                                .then_inc(osq, 1)
                        if i:
                            move_y(y - 1)
                    if kind in ("ma", "mb"):
                        idx = 18 * br + 9 * G + i
                        if i == 0 and G == 0:
                            move_y(9 * br + NT)
                        if i == 0 and G == 1:
                            act.wait_ge(m_out, 16 * (18 * br + 9))
                        act.wait_ge(z_ready, n + 1)
                        act.activation(sig[0:r, i, :], z, ACT.Sigmoid).then_inc(sig_ready, 1)
                    if kind == "out" and G == 0:
                        if i == 0:
                            m_hi_move(0)
                        if i + 1 < TILES:
                            m_hi_move(i + 1)
                    if prefetch and i < U[u + 1][4]:
                        split_hi(u + 1, i)

            def move_y(y):
                i = y % TILES
                act.wait_ge(y_t, y + 1)
                act.activation(yT_hi[:, :, i * P:i * P + nrows(i)],
                               bank(3 + y % 2).rearrange("p (c r) -> p c r", c=NC)[:, :, 0:nrows(i)],
                               ACT.Copy).then_inc(y_hi, 1)

            def m_hi_move(i):
                for half in range(2):
                    act.wait_ge(m_t, 2 * i + half + 1)
                    act.activation(hT_hi[:, 4 * half:4 * half + 4, i * P:i * P + nrows(i)],
                                   bank(3 + 2 * (i % 2) + half).rearrange("p (c r) -> p c r", c=4)[:, :, 0:nrows(i)],
                                   ACT.Copy).then_inc(m_hi, 1)

            def attention_b():
                act.sem_inc(be, 16)
                act.sem_inc(bm, 12)
                act.sem_inc(bo, 8)
                with act.Fori(0, 2) as I:
                    def piece_move(e):
                        for p, _, nb in pieces_of(e):
                            wait_reg(act, bt, 12 + 24 * I + p + 1)
                            wait_reg(act, bp, 12 + 24 * I + p - 3)
                            act.activation(ptB[:, p % 4, 0:nb * P], bank(4 + p % 2)[:, 0:nb * P],
                                           ACT.Copy).then_inc(bm, 1)

                    def out_move(e):
                        wait_reg(act, bp, 12 + 24 * I + pieces_before(e + 1))
                        act.activation(qT[:, ds((2 * I + e // 8) * SEQ + TILE_ORDER[e % 8] * P, P)],
                                       bank(6 + e % 2)[:, 0:P], ACT.Copy,
                                       scale=rlB[:, e // 8, e % 8, 0:1]).then_inc(bo, 1)

                    for s in range(16 + 3):
                        if s >= 3:
                            out_move(s - 3)
                        if 2 <= s < 18:
                            piece_move(s - 2)
                        if s < 16:
                            for mp in range(2):
                                wait_reg(act, bs, 16 + 32 * I + 2 * s + mp + 1)
                                sb = sB[s % 4][:, mp, 0:P * (TILE_ORDER[s % 8] + 1)]
                                n = 2 * (s % 8) + mp
                                act.activation(sb, sb, ACT.Exp, bias=st_sum[:, s // 8, 0, n:n + 1],
                                               scale=-1.0, accum_out=st_sum[:, s // 8, 1, n:n + 1])\
                                    .then_inc(be, 1)

            def attention_a(G):
                A = att[(3 * G + 2) % 2]
                base, tbase = 16 + 64 * (G - 1), 8 + 32 * (G - 1)
                if G == 1:
                    act.sem_inc(ae, 16)
                    act.sem_inc(ao, 8)
                with act.Fori(0, 2) as I:
                    for s in range(32 + 6):
                        if s < 32:
                            wait_reg(act, as_, base + 32 * I + s + 1)
                            sb = A["sA"][:, s % 8, 0:width_a(G, s // 2 % 8)]
                            par, n = divmod(s, 16)
                            act.activation(sb, sb, ACT.Exp, bias=st_sum[:, par, 0, n:n + 1], scale=-1.0,
                                           accum_out=st_sum[:, par, 1, n:n + 1]).then_inc(ae, 1)
                        if s >= 6 and s % 2 == 0:
                            e = (s - 6) // 2
                            wait_reg(act, av, base + 32 * I + 2 * e + 2)
                            act.activation(qT[:, ds((2 * I + e // 8) * SEQ + e % 8 * P, P)],
                                           bank(6 + e % 2)[:, 0:P], ACT.Copy).then_inc(ao, 1)

            for G in range(4):
                for kind in range(3):
                    block_(3 * G + kind)
                for b in COPIES_IN[G]:
                    copy_cache(b)
                attention_a(G) if G else attention_b()

            act.sem_inc(s_km, 29)
            act.sem_inc(s_oc, 2)
            act.sem_inc(s_out, 32)
            act.wait_ge(s_const, 80)
            act.wait_ge(s_zero, 1)
            with act.Fori(0, DEC_B) as b:
                def keys_move(T):
                    wait_reg(act, s_kt, 29 * b + 29 + T + 1)
                    wait_reg(act, s_qk, 29 * b + 29 + T - 1 if T >= 2 else 29 * b + 29 - (1 if T else 0))
                    act.activation(kTs[:, T % 2, :, :], bank(T % 2).rearrange("p (c r) -> p c r", c=NC),
                                   ACT.Copy).then_inc(s_km, 1)

                wait_reg(act, s_nt, b + 1)
                act.activation(kTn[:, :, :], bank(5)[:, 384:512].rearrange("p (c r) -> p c r", c=16),
                               ACT.Copy).then_inc(s_nm, 1)
                for T in range(29):
                    keys_move(T)
                    if T == 17:
                        wait_reg(act, s_ta, 2 * b + 1)
                        act.activation(s_a[:, :], s_a[:, :], ACT.Exp, bias=sc_s[:, 0:1], scale=-1.0,
                                       accum_out=sc_s[:, 1:2]).then_inc(s_ea, 1)
                wait_reg(act, s_min, b + 1)
                act.activation(s_b[:, :], s_b[:, :], ACT.Exp, bias=sc_s[:, 8:9], scale=-1.0,
                               accum_out=sc_s[:, 9:10]).then_inc(s_eb, 1)
                wait_reg(act, s_sel, 2 * b + 1)
                wait_reg(act, s_out, 32 * b + 32)
                act.activation(os_[:, 0, :], bank(2)[0:DEC_T], ACT.Copy).then_inc(s_oc, 1)
                wait_reg(act, s_oc, 2 * b + 3)
                act.dma_start(os_scr[0, ds(b * DEC_T, DEC_T), :], os_[:, 0, :]).then_inc(s_out, 16)
                wait_reg(act, s_sel, 2 * b + 2)
                act.activation(os_[:, 1, :], bank(2)[0:DEC_T], ACT.Copy).then_inc(s_oc, 1)
                wait_reg(act, s_oc, 2 * b + 4)
                act.dma_start(os_scr[1, ds(b * DEC_T, DEC_T), :], os_[:, 1, :]).then_inc(s_out, 16)

            for k in range(KC):
                split_hi(FIRST_GATE, k)
            act.wait_ge(ew_exp, 1)
            act.activation(ew[:, :, :, :], ew[:, :, :, :], ACT.Exp).then_inc(ew_exp, 1)
            for u in range(FIRST_GATE, len(U)):
                block_(u)

        @block.vector
        def _(dve):
            steps = [0]

            def link(ins):
                steps[0] += 1
                ins.then_inc(dve_step, 1)
                dve.wait_ge(dve_step, steps[0])

            def rows_scale(i):
                r = nrows(i)
                dve.wait_ge(h_rs, i + 1)
                dve.tensor_scalar(xn[0:r, i % 2, :], xt[0:r, i % 2, :], rs_x[0:r, i % 2, 0:1], None, ALU.mult)\
                    .then_inc(h_xn, 1)

            def input_gain(i):
                r = nrows(i)
                for half in range(2):
                    j = 2 * i + half
                    dve.wait_ge(h_t, j + 1)
                    if i:
                        dve.wait_ge(h_lo, j - 1)
                    dve.tensor_tensor(hn[:, half, :].rearrange("p (k r) -> p k r", k=4)[:, :, 0:r],
                                      bank(x_bank(j)).rearrange("p (k r) -> p k r", k=4)[:, :, 0:r],
                                      gcol[:, 4 * half:4 * half + 4].unsqueeze(2).to_broadcast([P, 4, r]),
                                      ALU.mult).then_inc(h_hn, 1)

            dve.wait_ge(const_in, N_CONST)

            def input_step(i):
                if i < TILES:
                    rows_scale(i)
                if 1 <= i <= TILES:
                    input_gain(i - 1)

            for i in range(3):
                input_step(i)
            for j in range(2):
                dve.tensor_tensor_reduce(out=lamv[:, 2 * j, :], in0=lamv[:, 2 * j, :], in1=lamv[:, 2 * j + 1, :],
                                         scale=1.0, scalar=0.0, op0=ALU.mult, op1=ALU.add,
                                         accum_out=lam[:, j:j + 1]).then_inc(setup, 1)
            dve.wait_ge(setup, 3)
            link(dve.tensor_tensor(lam[:, 4:5], lam[:, 3:4], lam[:, 2:3], ALU.subtract))
            link(dve.tensor_scalar(lam[:, 5:6], lam[:, 4:5], -LAM_INIT, None, ALU.add))
            link(dve.tensor_scalar(subrow[:, :], subrow[:, :], 1.0 - LAM_INIT, None, ALU.mult))
            link(dve.scalar_tensor_tensor(out=coef[:, 0:1], in0=coef[:, 1:2], scalar=lam[0:NS, 5:6],
                                          in1=coef[:, 0:1], op0=ALU.mult, op1=ALU.add))
            dve.tensor_scalar(qcol[:, :], qcol[:, :], -(HD ** -0.5), None, ALU.mult).then_inc(setup, 1)

            def block_(u):
                kind, G = U[u][0], U[u][1]
                br = 1 if kind[-1] == "b" else 0
                for i in range(TILES):
                    n, r = TILES * u + i, nrows(i)
                    z = bank(n % 3)[0:r]
                    if u == 0:
                        input_step(i + 3)
                    if kind in "qk":
                        m = mi(G, kind, i)
                        dve.wait_ge(sq_ready, m + 1)
                        dve.tensor_reduce(ss[0:r, m % 2, :],
                                          bank(5 + m % 2)[0:r].rearrange("p (h d) -> p h d", h=8),
                                          AX_X, ALU.add).then_inc(ss_ready, 1)
                        dve.wait_ge(rs_ready, m + 1)
                        if m >= 2:
                            G2, m2 = divmod(m - 2, 18)
                            if m2 < 9:
                                dve.wait_ge(t_ready, ti(G2, "q", m2) + 1)
                            else:
                                dve.wait_ge(kn_ready, TILES * G2 + m2 - 9 + 1)
                        dve.tensor_tensor(zn[0:r, m % 2, :].rearrange("p (h d) -> p h d", h=8),
                                          z.rearrange("p (h d) -> p h d", h=8),
                                          rs[0:r, m % 2, :].unsqueeze(2).to_broadcast([r, 8, HD]),
                                          ALU.mult).then_inc(zn_ready, 1)
                    if kind == "v":
                        dve.wait_ge(z_ready, n + 1)
                        if i == 0 and G:
                            dve.wait_ge(v_out, v_sent[G - 1])
                        dve.tensor_copy(v_sb[0:r, i, :], z).then_inc(v_ready, 1)
                    if kind in ("ga", "gb"):
                        y = 9 * br + i
                        s = y % 2
                        dve.wait_ge(sg_ready, y + 1)
                        dve.tensor_tensor(sg[0:r, s, :], sg[0:r, s, :], z, ALU.mult).then_inc(silu_ready, 1)
                        if y >= 2:
                            dve.wait_ge(y_t, y - 1)
                        heads = 8 if br == 0 else 4
                        o = og[0:r, s, 0, :].rearrange("p (h d) -> p h d", h=heads)
                        dve.wait_ge(og_in[s], og_total(y))
                        if br == 0 and i < NT:
                            link(dve.tensor_tensor(o, o, ew[:, i, 0, :].unsqueeze(2).to_broadcast([P, 8, HD]),
                                                   ALU.mult))
                            dve.wait_ge(og_pool, i + 1)
                            link(dve.tensor_tensor(og[:, s, 0, :], og[:, s, 0, :], og[:, s, 1, :], ALU.add))
                            link(dve.tensor_tensor(og[:, s, 0, :], og[:, s, 0, :], og[:, s, 2, :], ALU.add))
                        if br == 1:
                            dve.wait_ge(osq, i + 1)
                            dve.tensor_reduce(ss[0:r, i % 2, 0:4],
                                              og[0:r, s, 1, :].rearrange("p (h d) -> p h d", h=4),
                                              AX_X, ALU.add).then_inc(oss, 1)
                            dve.wait_ge(ors, i + 1)
                            link(dve.tensor_tensor(o, o, rs[0:r, i % 2, 0:4].unsqueeze(2).to_broadcast([r, 4, P]),
                                                   ALU.mult))
                            link(dve.tensor_tensor(o, o, subrow[0:r, :].unsqueeze(1).to_broadcast([r, 4, P]),
                                                   ALU.mult))
                        dve.wait_ge(silu_ready, y + 1)
                        dve.tensor_tensor(zy[0:r, s, :], og[0:r, s, 0, :], sg[0:r, s, :], ALU.mult)\
                            .then_inc(y_ready, 1)
                        if i:
                            y_low(y - 1)
                    if kind in ("ma", "mb") and i == 0 and G == 0:
                        y_low(9 * br + NT)
                    if kind in ("pa", "pb"):
                        idx = 18 * br + 9 * G + i
                        dve.wait_ge(z_ready, n + 1)
                        dve.wait_ge(sig_ready, idx + 1)
                        ins = dve.tensor_tensor(sig[0:r, i, :], sig[0:r, i, :], z, ALU.mult)
                        if br:
                            link(ins)
                            dve.wait_ge(ml_in[(9 * G + i) % 2], 16 * ((9 * G + i) // 2 + 1))
                            ins = dve.tensor_tensor(sig[0:r, i, :], sig[0:r, i, :],
                                                    zy[0:r, (9 * G + i) % 2, :], ALU.add)
                        ins.then_inc(m_ready, 1)
                    if kind == "out":
                        if G == 0:
                            if i == 0:
                                m_low(0)
                            if i + 1 < TILES:
                                m_low(i + 1)
                        idx = 9 * G + i
                        dve.wait_ge(z_ready, n + 1)
                        dve.wait_ge(xl_in[idx % 2], 16 * (idx // 2 + 1))
                        if idx >= 3:
                            dve.wait_ge(yo_out[idx % 3], 16 * (idx // 3))
                        dve.tensor_tensor(yo[0:r, idx % 3, :], z, xl[0:r, idx % 2, :], ALU.add)\
                            .then_inc(yo_ready, 1)

            def y_low(y):
                i = y % TILES
                dve.wait_ge(y_hi, y + 1)
                dve.tensor_tensor(yT_lo[:, :, i * P:i * P + nrows(i)],
                                  bank(3 + y % 2).rearrange("p (c r) -> p c r", c=NC)[:, :, 0:nrows(i)],
                                  yT_hi[:, :, i * P:i * P + nrows(i)].bitcast(F32), ALU.subtract)\
                    .then_inc(y_lo, 1)

            def m_low(i):
                for half in range(2):
                    dve.wait_ge(m_hi, 2 * i + half + 1)
                    cols = slice(i * P, i * P + nrows(i))
                    dve.tensor_tensor(
                        hT_lo[:, 4 * half:4 * half + 4, cols],
                        bank(3 + 2 * (i % 2) + half).rearrange("p (c r) -> p c r", c=4)[:, :, 0:nrows(i)],
                        hT_hi[:, 4 * half:4 * half + 4, cols].bitcast(F32), ALU.subtract).then_inc(m_lo, 1)

            def attention_b():
                dve.sem_inc(bs, 16)
                dve.sem_inc(ba, 8)
                with dve.Fori(0, 2) as I:
                    def biased(e, mp):
                        W = P * (TILE_ORDER[e % 8] + 1)
                        n = 2 * (e % 8) + mp
                        wait_reg(dve, bq, 16 + 32 * I + 2 * e + mp + 1)
                        if mp:
                            wait_reg(dve, ba, 8 + 16 * I + e - 3)
                        else:
                            wait_reg(dve, bt, 12 + 24 * I + pieces_before(e - 3))
                        dve.tensor_tensor_reduce(
                            out=sB[e % 4][:, mp, 0:W], in0=ps[:, mp * 1024:mp * 1024 + W],
                            in1=tB[:, e // 8, SEQ - W:SEQ], scale=1.0, scalar=3e38,
                            op0=ALU.add, op1=ALU.min, accum_out=st_sum[:, e // 8, 0, n:n + 1]).then_inc(bs, 1)

                    def combined(e):
                        par, i = e // 8, e % 8
                        W = P * (TILE_ORDER[i] + 1)
                        wait_reg(dve, be, 16 + 32 * I + 2 * e + 2)
                        dve.reciprocal(rlB[:, par, i, :], st_sum[:, par, 1, 2 * i:2 * i + 2]).then_inc(bw, 1)
                        wait_reg(dve, bw, 32 * I + 2 * e + 1)
                        dve.scalar_tensor_tensor(out=wB[:, par, i:i + 1], in0=rlB[:, par, i, 1:2],
                                                 scalar=st_sum[:, par, 1, 2 * i:2 * i + 1],
                                                 in1=lam[:, 5:6], op0=ALU.mult, op1=ALU.mult).then_inc(bw, 1)
                        wait_reg(dve, bw, 32 * I + 2 * e + 2)
                        p1, p2 = sB[e % 4][:, 0, 0:W], sB[e % 4][:, 1, 0:W]
                        dve.scalar_tensor_tensor(out=p1, in0=p2, scalar=wB[:, par, i:i + 1], in1=p1,
                                                 op0=ALU.mult, op1=ALU.add).then_inc(ba, 1)

                    for s in range(16 + 1):
                        if s in (0, 8):
                            wait_reg(dve, btab2 if s else btab, 16 * I + 16)
                        if s < 16:
                            biased(s, 0)
                        if s:
                            combined(s - 1)
                        if s < 16:
                            biased(s, 1)

            def attention_a(G):
                A = att[(3 * G + 2) % 2]
                base = 16 + 64 * (G - 1)
                if G == 1:
                    dve.sem_inc(as_, 16)
                    dve.sem_inc(am, 16)
                else:
                    dve.wait_ge(o_out, 16 * 8 * (2 * G - 1))
                with dve.Fori(0, 2) as I:
                    def keep_stats(par):
                        wait_reg(dve, ae, base + 32 * I + 16 * par + 16)
                        c2 = (2 * I + par) * 2
                        for j in range(2):
                            ins = dve.tensor_copy(st[:, :, ds(c2 + 8 * j, 2)],
                                                  st_sum[:, par, j, :].rearrange("p (i h) -> p i h", h=2))
                        ins.then_inc(ast, 1)

                    for s in range(32 + 3):
                        if s in (0, 16):
                            wait_reg(dve, atab2 if s else atab, 16 * I + 16 + 32 * (G - 1))
                        if s < 32:
                            par, n = divmod(s, 16)
                            W = width_a(G, n // 2)
                            N = base + 32 * I + s
                            wait_reg(dve, aq, N + 1)
                            wait_reg(dve, atp, N - 7)
                            dve.tensor_tensor_reduce(
                                out=A["sA"][:, s % 8, 0:W], in0=bank(s % 4)[:, 0:W],
                                in1=A["tA"][:, par, s % 2, 256 - W:256], scale=1.0, scalar=3e38,
                                op0=ALU.add, op1=ALU.min, accum_out=st_sum[:, par, 0, n:n + 1]).then_inc(as_, 1)
                        if s >= 3:
                            n = s - 3
                            N = base + 32 * I + n
                            W = width_a(G, n // 2 % 8)
                            wait_reg(dve, atp, N + 1)
                            wait_reg(dve, av, N - 3)
                            dve.tensor_copy(A["ptA"][:, n % 4, 0:W], bank(4 + n % 2)[:, 0:W]).then_inc(am, 1)
                        if s == 19:
                            keep_stats(0)
                    keep_stats(1)

            for G in range(4):
                for kind in range(3):
                    block_(3 * G + kind)
                attention_a(G) if G else attention_b()

            dve.sem_inc(s_pbm, 2)
            dve.sem_inc(s_om, 2)
            dve.wait_ge(s_const, 80)
            dve.wait_ge(s_zero, 1)
            with dve.Fori(0, DEC_B) as b:
                def biased(out, in_, table, acc):
                    return dve.tensor_tensor_reduce(out=out, in0=in_, in1=table, scale=1.0, scalar=3e38,
                                                    op0=ALU.add, op1=ALU.min, accum_out=acc)

                wait_reg(dve, s_qk, 29 * b + 29 + 13)
                biased(s_a[:, :], bank(2)[0:NS, 0:NEW_A], bias_sa[:, :], sc_s[:, 0:1]).then_inc(s_ta, 1)
                wait_reg(dve, s_pb, 2 * b + 2)
                biased(s_b[:, PAST:KEYS_B], bank(2)[0:NS, NEW_A:NEW_A + DEC_T], bias_sb[:, PAST:KEYS_B],
                       sc_s[:, 2:3]).then_inc(s_ta, 1)
                for q in range(4):
                    wait_reg(dve, s_qk, 29 * b + 29 + 13 + 4 * (q + 1))
                    biased(s_b[:, q * CW:(q + 1) * CW], bank(3 + q % 2)[0:NS], bias_sb[:, q * CW:(q + 1) * CW],
                           sc_s[:, 3 + q:4 + q]).then_inc(s_tb, 1)
                wait_reg(dve, s_tb, 4 * b + 4)
                dve.tensor_reduce(sc_s[:, 8:9], sc_s[:, 2:7], AX_X, ALU.min).then_inc(s_min, 1)
                wait_reg(dve, s_pa, b + 1)
                wait_reg(dve, s_va, b + 1)
                dve.tensor_copy(pT0[:, :], bank(5)[:, 0:NS])

                def dims(ap, off, d):
                    return bass.AP(ap.tensor, ap.offset + off, [list(ap.ap[0])] + d)

                dve.tensor_copy(dims(pT1[:, 0, 0:1], 0, [[NS + 2, 4], [8, 8], [1, 2]]),
                                dims(ps[:, 5 * CW + NS:5 * CW + NS + 1], 0, [[2, 4], [8, 8], [1, 2]]))
                dve.tensor_copy(dims(pT2[:, 0, 0:1], 0, [[NS + 2, 8], [16, 4], [1, 2]]),
                                dims(ps[:, 5 * CW + 2 * NS:5 * CW + 2 * NS + 1], 0, [[2, 8], [16, 4], [1, 2]]))
                dve.tensor_copy(pTn[:, 0:3, :], bank(5)[0:DEC_T, 192:384].rearrange("p (g q) -> p g q", g=3))\
                    .then_inc(s_pam, 1)
                wait_reg(dve, s_vb, b + 1)
                for j in range(2):
                    wait_reg(dve, s_pb, 2 * b + 2 + j + 1)
                    if j:
                        dve.tensor_copy(pTn[:, 3, :], bank(5)[0:DEC_T, 0:NS])
                    dve.tensor_copy(pTb[:, 8 * j:8 * j + 8, :], bank(3 + j).rearrange("p (g q) -> p g q", g=8))\
                        .then_inc(s_pbm, 1)
                wait_reg(dve, s_ea, b + 1)
                dve.reciprocal(sc_s[:, 10:11], sc_s[:, 1:2]).then_inc(s_rec, 1)
                wait_reg(dve, s_eb, b + 1)
                dve.reciprocal(sc_s[:, 11:12], sc_s[:, 9:10]).then_inc(s_rec, 1)
                wait_reg(dve, s_rec, 3 * b + 2)
                dve.tensor_scalar(sc_s[:, 12:13], sc_s[:, 11:12], coef[:, 0:1], None, ALU.mult).then_inc(s_rec, 1)
                wait_reg(dve, s_rec, 3 * b + 3)
                wait_reg(dve, s_va, b + 2)
                dve.scalar_tensor_tensor(out=om[:, 0, :], in0=bank(7)[0:NS], scalar=sc_s[:, 10:11],
                                         in1=mask[:, 0, :], op0=ALU.mult, op1=ALU.mult).then_inc(s_om, 1)
                wait_reg(dve, s_vb, b + 2)
                dve.scalar_tensor_tensor(out=om[:, 1, :], in0=bank(6)[0:NS], scalar=sc_s[:, 12:13],
                                         in1=mask[:, 1, :], op0=ALU.mult, op1=ALU.mult).then_inc(s_om, 1)

            dve.wait_ge(st_in, 48)

            def nm(g):
                return stc[:, :, g, 0:8]

            link(dve.tensor_tensor(nmin[:, :, :], nm(0), nm(1), ALU.min))
            link(dve.tensor_tensor(nmin[:, :, :], nmin[:, :, :], nm(2), ALU.min))
            for g in range(3):
                link(dve.tensor_tensor(ew[:, :, g, :], nmin[:, :, :], nm(g), ALU.subtract))
            dve.sem_inc(ew_exp, 1)
            dve.wait_ge(ew_exp, 2)
            for g in range(3):
                link(dve.tensor_tensor(el[:, :, g, :], ew[:, :, g, :], stc[:, :, g, 8:16], ALU.mult))
            link(dve.tensor_tensor(den[:, :, :], el[:, :, 0, :], el[:, :, 1, :], ALU.add))
            link(dve.tensor_tensor(den[:, :, :], den[:, :, :], el[:, :, 2, :], ALU.add))
            link(dve.reciprocal(den[:, :, :], den[:, :, :]))
            for g in range(3):
                link(dve.tensor_tensor(ew[:, :, g, :], ew[:, :, g, :], den[:, :, :], ALU.mult))
            dve.sem_inc(ew_ready, 1)
            for u in range(FIRST_GATE, len(U)):
                block_(u)

        @block.tensor
        def _(pe):
            pe.wait_ge(const_in, N_CONST)

            def turn_x(i, half):
                r, j = nrows(i), 2 * i + half
                pe.wait_ge(h_xn, i + 1)
                if j >= 4:
                    pe.wait_ge(h_hn, j)
                for k in range(4):
                    c = 4 * half + k
                    ins = pe.transpose(bank(x_bank(j))[:, k * P:k * P + r],
                                       xn[0:r, i % 2, c * P:(c + 1) * P], ident[0:r, 0:r])
                ins.then_inc(h_t, 1)

            for i in range(2):
                for half in range(2):
                    turn_x(i, half)

            def turn(G, kind, i):
                t, r = ti(G, kind, i), nrows(i)
                if kind == "q":
                    pe.wait_ge(zn_ready, mi(G, "q", i) + 1)
                    src = zn[0:r, mi(G, "q", i) % 2, :]
                else:
                    kk = TILES * G + i
                    pe.wait_ge(kn_ready, kk + 1)
                    src = kn[0:r, kk % 3, :]
                if t >= 2:
                    pe.wait_ge(t_moved, t - 1)
                for c in range(NC):
                    ins = pe.transpose(bank(3 + t % 2)[:, c * P:c * P + r], src[:, c * P:(c + 1) * P],
                                       ident[0:r, 0:r])
                ins.then_inc(t_ready, 1)

            def turn_y(y):
                r = nrows(y % TILES)
                pe.wait_ge(y_ready, y + 1)
                if y >= 2:
                    pe.wait_ge(y_lo, y - 1)
                for c in range(NC):
                    ins = pe.transpose(bank(3 + y % 2)[:, c * P:c * P + r], zy[0:r, y % 2, c * P:(c + 1) * P],
                                       ident[0:r, 0:r])
                ins.then_inc(y_t, 1)

            def turn_m(i):
                r = nrows(i)
                pe.wait_ge(mt_in[i % 2], 16 * (i // 2 + 1))
                for half in range(2):
                    if i >= 2:
                        pe.wait_ge(m_lo, 2 * (i - 2) + half + 1)
                    for k in range(4):
                        c = 4 * half + k
                        ins = pe.transpose(bank(3 + 2 * (i % 2) + half)[:, k * P:k * P + r],
                                           mt[0:r, i % 2, c * P:(c + 1) * P], ident[0:r, 0:r])
                    ins.then_inc(m_t, 1)

            def block_(u):
                kind, G, _, _, K = U[u]
                br = 1 if kind[-1] == "b" else 0
                order = G if kind in "qkv" else 0
                hi, lo = (yT_hi, yT_lo) if kind in ("pa", "pb") else (hT_hi, hT_lo)
                if kind == "out" and G == 0:
                    turn_m(0)
                    turn_m(1)
                for i in range(TILES):
                    n, r = TILES * u + i, nrows(i)
                    if i == 0:
                        pe.wait_ge(lo_done, first_chunk[u + 1])
                    if n == 0:
                        pe.wait_ge(h_hn, 4)
                    if u < 3:
                        pe.wait_ge(h_lo, 2 * i + 2)
                    if kind in ("pa", "pb"):
                        pe.wait_ge(y_lo, 9 * br + i + 1)
                    if kind == "out":
                        pe.wait_ge(m_lo, 2 * i + 2)
                    if n >= 3:
                        pe.wait_ge(*z_freed(n - 3))
                    z = bank(n % 3)[0:r]
                    for k in range(K):
                        sh, sl = hT_of(hi, order, k, i), hT_of(lo, order, k, i)
                        pe.matmul(z, sh, w_hi[u % 2][:, k, :], start=(k == 0), stop=False)
                        pe.matmul(z, sh, w_lo[u % 2][:, k, :], start=False, stop=False)
                        if u == 0 and k in (1, 5) and i + 2 < TILES:
                            turn_x(i + 2, k // 4)
                        ins = pe.matmul(z, sl, w_hi[u % 2][:, k, :], start=False, stop=(k == K - 1))
                    ins.then_inc(z_ready, 1)
                    if kind == "q" and i:
                        turn(G, "q", i - 1)
                    if kind == "k":
                        turn(G, "q", NT) if i == 0 else turn(G, "k", i - 1)
                    if kind in ("ga", "gb") and i >= 2:
                        turn_y(9 * br + i - 2)
                    if kind == "out" and G == 0 and i + 2 < TILES:
                        turn_m(i + 2)
                if kind in ("ga", "gb"):
                    turn_y(9 * br + NT - 1)
                    turn_y(9 * br + NT)

            def attention_b():
                pe.sem_inc(bq, 16)
                pe.sem_inc(bt, 12)
                pe.sem_inc(bp, 12)
                with pe.Fori(0, 2) as I:
                    def scores(e, mp):
                        h, s = 2 * I + e // 8, TILE_ORDER[e % 8]
                        W, N = P * (s + 1), 16 + 32 * I + 2 * e + mp
                        if mp == 0:
                            wait_reg(pe, qz_ready, 16 * I + e + 1)
                        wait_reg(pe, bs, N - 1)
                        for w0 in range(0, W, CW):
                            w = min(CW, W - w0)
                            ins = pe.matmul(ps[:, mp * 1024 + w0:mp * 1024 + w0 + w],
                                            qz[:, mp, s * P:(s + 1) * P], kT[:, ds(h * SEQ + w0, w)],
                                            start=True, stop=True)
                        ins.then_inc(bq, 1)

                    def probs_turn(e):
                        wait_reg(pe, ba, 8 + 16 * I + e + 1)
                        for p, j0, nb in pieces_of(e):
                            wait_reg(pe, bm, 12 + 24 * I + p - 1)
                            for j in range(nb):
                                ins = pe.transpose(bank(4 + p % 2)[:, j * P:(j + 1) * P],
                                                   sB[e % 4][:, 0, (j0 + j) * P:(j0 + j + 1) * P], ident[:, :])
                            ins.then_inc(bt, 1)

                    def values(e, half):
                        h = 2 * I + e // 8
                        if half == 0:
                            wait_reg(pe, bo, 8 + 16 * I + e - 1)
                        for p, j0, nb in pieces_of(e)[half:half + 1]:
                            wait_reg(pe, bm, 12 + 24 * I + p + 1)
                            for j in range(nb):
                                ins = pe.matmul(bank(6 + e % 2)[:, 0:P], ptB[:, p % 4, j * P:(j + 1) * P],
                                                v_sb[:, j0 + j, ds(h * P, P)], start=(j0 + j == 0),
                                                stop=(j0 + j == TILE_ORDER[e % 8]))
                            ins.then_inc(bp, 1)

                    for s in range(16 + 2):
                        if s >= 2:
                            probs_turn(s - 2)
                        for half in range(2):
                            if s < 16:
                                scores(s, half)
                            if s >= 2:
                                values(s - 2, half)

            def attention_a(G):
                A = att[(3 * G + 2) % 2]
                base, tbase = 16 + 64 * (G - 1), 8 + 32 * (G - 1)
                if G == 1:
                    for s in (aq, atp, av):
                        pe.sem_inc(s, 16)
                with pe.Fori(0, 2) as I:
                    for s in range(32 + 5):
                        if s < 32:
                            c, (i, hh) = 2 * I + s // 16, divmod(s % 16, 2)
                            N = base + 32 * I + s
                            W = width_a(G, i)
                            if hh == 0:
                                wait_reg(pe, qz_ready, 32 * G + 16 * I + s // 2 + 1)
                            wait_reg(pe, as_, N - 3)
                            pe.matmul(bank(s % 4)[:, 0:W], qz[:, hh, i * P:(i + 1) * P],
                                      kT[:, ds(c * SEQ + (i + 1) * P - W, W)],
                                      start=True, stop=True).then_inc(aq, 1)
                        if 3 <= s < 35:
                            n = s - 3
                            N = base + 32 * I + n
                            wait_reg(pe, ae, N + 1)
                            wait_reg(pe, am, N - 1)
                            for j in range(width_a(G, n // 2 % 8) // P):
                                ins = pe.transpose(bank(4 + n % 2)[:, j * P:(j + 1) * P],
                                                   A["sA"][:, n % 8, j * P:(j + 1) * P], ident[:, :])
                            ins.then_inc(atp, 1)
                        if s >= 5:
                            n = s - 5
                            e, hh = divmod(n, 2)
                            c, i = 2 * I + e // 8, e % 8
                            N = base + 32 * I + n
                            nb = width_a(G, i) // P
                            wait_reg(pe, am, N + 1)
                            if hh == 0:
                                wait_reg(pe, ao, tbase + 16 * I + e - 1)
                            for j in range(nb):
                                ins = pe.matmul(bank(6 + e % 2)[:, hh * HD:(hh + 1) * HD],
                                                A["ptA"][:, n % 4, j * P:(j + 1) * P],
                                                v_sb[:, i + 1 - nb + j, ds(c * P + hh * HD, HD)],
                                                start=(j == 0), stop=(j == nb - 1))
                            ins.then_inc(av, 1)

            for G in range(4):
                for kind in range(3):
                    block_(3 * G + kind)
                pe.wait_ge(v_ready, 9 * G + 9)
                pe.wait_ge(t_moved, 17 * G + 17)
                attention_a(G) if G else attention_b()

            for s, c in ((s_kt, 29), (s_qk, 29), (s_pv, 29), (s_va, 1), (s_vb, 1), (s_pb, 2)):
                pe.sem_inc(s, c)
            with pe.Fori(0, DEC_B) as b:
                wait_reg(pe, sn_in, 128 * b + 128)
                wait_reg(pe, s_pbm, 2 * b + 2)
                for g in range(4):
                    for c in range(NC):
                        j = 4 * g + c
                        ins = pe.transpose(bank(5)[:, 384 + 8 * j:392 + 8 * j],
                                           kv_new[:, 0, g, c * P:(c + 1) * P], ident[0:DEC_T, 0:DEC_T])
                ins.then_inc(s_nt, 1)

                def keys_turn(T):
                    per = 4 if T % NKS < 5 else 3
                    wait_reg(pe, sk_in[T % NKS], 16 * per * b + 16 * (T // NKS + 1))
                    wait_reg(pe, s_km, 29 * b + 29 + T - 1 if T >= 2 else 29 * b + 29 - (1 if T else 0))
                    for c in range(NC):
                        ins = pe.transpose(bank(T % 2)[:, c * P:(c + 1) * P],
                                           k_in[:, T % NKS, c * P:(c + 1) * P], ident[:, :])
                    ins.then_inc(s_kt, 1)

                def score(T):
                    wait_reg(pe, s_km, 29 * b + 29 + T + 1)
                    if T < 13:
                        if T == 0:
                            q, col, g = q_all[:, 1, :, :], 0, 0
                        elif T < 5:
                            q, col, g = q_g1[:, T - 1, :, :], P + DEC_T, 1
                        else:
                            q, col, g = q_g2[:, T - 5, :, :], 2 * (P + DEC_T), 2
                        out = bank(2)[0:NS, col:col + P]
                        first = False
                    else:
                        j = T - 13
                        q = q_all[:, 0, :, :]
                        out = bank(3 + (j // 4) % 2)[0:NS, (j % 4) * P:(j % 4 + 1) * P]
                        first = j % 4 == 0
                        if j in (0, 4):
                            wait_reg(pe, s_pbm, 2 * b + 2)
                        if j in (8, 12):
                            wait_reg(pe, s_tb, 4 * b + (1 if j == 8 else 2))
                    for c in range(NC):
                        ins = pe.matmul(out, q[:, c, :], kTs[:, T % 2, c, :], start=(first and c == 0),
                                        stop=(c == NC - 1), skip_group_check=True)
                    ins.then_inc(s_qk, 1)

                keys_turn(0)
                wait_reg(pe, s_nm, b + 1)
                wait_reg(pe, sq_b, b + 1)
                wait_reg(pe, s_oc, 2 * b + 2)
                for g in range(4):
                    G = (g + 1) % 4
                    col = g * (P + DEC_T) + P if g < 3 else NEW_A
                    for c in range(NC):
                        pe.matmul(bank(2)[0:NS, col:col + DEC_T], q_all[:, G, c, :], kTn[:, 4 * g + c, :],
                                  start=(g == 0 and c == 0), stop=(c == NC - 1), skip_group_check=True)
                for T in range(29):
                    if T + 1 < 29:
                        keys_turn(T + 1)
                    score(T)

                wait_reg(pe, s_ea, b + 1)
                for g in range(3):
                    col = g * (P + DEC_T)
                    pe.transpose(bank(5)[:, g * NS:(g + 1) * NS], s_a[:, col:col + P], ident[0:NS, 0:NS])
                    ins = pe.transpose(bank(5)[0:DEC_T, 192 + g * NS:192 + (g + 1) * NS],
                                       s_a[:, col + P:col + P + DEC_T], ident[0:NS, 0:NS])
                ins.then_inc(s_pa, 1)
                wait_reg(pe, s_pam, b + 1)
                wait_reg(pe, s_om, 2 * b + 1 + 1)
                for T in range(13):
                    per = 2 if T < 9 else 1
                    wait_reg(pe, sv_in[T], 16 * per * b + 16)
                    pt = pT0[:, :] if T == 0 else (pT1[:, T - 1, :] if T < 5 else pT2[:, T - 5, :])
                    pe.matmul(bank(7)[0:NS], pt, v_in[:, T, :], start=(T == 0), stop=False,
                              skip_group_check=True).then_inc(s_pv, 1)
                for g in range(3):
                    ins = pe.matmul(bank(7)[0:NS], pTn[:, g, :], kv_new[:, 1, g, :], start=False, stop=(g == 2),
                                    skip_group_check=True)
                ins.then_inc(s_va, 1)
                wait_reg(pe, s_eb, b + 1)
                for j in range(2):
                    for p in range(8):
                        pg = 8 * j + p
                        ins = pe.transpose(bank(3 + j)[:, p * NS:(p + 1) * NS], s_b[:, pg * P:(pg + 1) * P],
                                           ident[0:NS, 0:NS])
                    if j == 1:
                        ins = pe.transpose(bank(5)[0:DEC_T, 0:NS], s_b[:, PAST:KEYS_B], ident[0:NS, 0:NS])
                    ins.then_inc(s_pb, 1)
                wait_reg(pe, s_om, 2 * b + 2)
                for pg in range(N_PAGES):
                    T = 13 + pg
                    if pg % 8 == 0:
                        wait_reg(pe, s_pbm, 2 * b + 2 + pg // 8 + 1)
                    slot, per, k = (T, 1, 1) if T < 20 else (T - 20, 2, 2)
                    wait_reg(pe, sv_in[slot], 16 * per * b + 16 * k)
                    pe.matmul(bank(6)[0:NS], pTb[:, pg, :], v_in[:, slot, :], start=(pg == 0), stop=False,
                              skip_group_check=True).then_inc(s_pv, 1)
                pe.matmul(bank(6)[0:NS], pTn[:, 3, :], kv_new[:, 1, 3, :], start=False, stop=True,
                          skip_group_check=True).then_inc(s_vb, 1)
                wait_reg(pe, s_om, 2 * b + 2 + 1)
                pe.matmul(bank(2)[0:DEC_T], sel[:, :], om[:, 0, :], start=True, stop=True).then_inc(s_sel, 1)
                wait_reg(pe, s_om, 2 * b + 2 + 2)
                wait_reg(pe, s_oc, 2 * b + 2 + 1)
                pe.matmul(bank(2)[0:DEC_T], sel[:, :], om[:, 1, :], start=True, stop=True).then_inc(s_sel, 1)

            for u in range(FIRST_GATE, len(U)):
                block_(u)


def shape_constants():
    f = np.float32
    slopes_a = (2.0 ** (-8.0 * np.arange(1, 25) / 24)).astype(f).reshape(3, A_HEADS)
    slopes_b = (2.0 ** (-8.0 * np.arange(1, B_HEADS + 1) / B_HEADS)).astype(f)
    p = np.arange(P)[:, None]
    x = np.arange(2 * P)[None, :]
    bias_a = np.full((3, A_HEADS, P, 2 * P), MASKED, f)
    steps = p + P - x
    for g in range(2):
        ok = (steps >= 0) & (steps <= P)
        for h in range(A_HEADS):
            bias_a[g, h] = np.where(ok, slopes_a[g, h] * (steps * WINDOWS[g][1]).astype(f), f(MASKED))
    ok = (steps >= 0) & (steps % 2 == 0) & (x >= P)
    for h in range(A_HEADS):
        bias_a[2, h] = np.where(ok, slopes_a[2, h] * (steps * 8).astype(f), f(MASKED))
    dist = p - (np.arange(SEQ)[None, :] - (SEQ - P))
    bias_b = np.stack([np.where(dist >= 0, s * dist.astype(f), f(MASKED)) for s in slopes_b]).astype(f)
    c, t, hh = (a.reshape(-1) for a in np.meshgrid(np.arange(NC), np.arange(DEC_T), np.arange(2), indexing="ij"))
    bias_sa = np.full((NS, NEW_A), MASKED, f)
    bias_sb = np.full((NS, KEYS_B), MASKED, f)
    m = np.arange(P)[None, :]
    j = np.arange(DEC_T)[None, :]
    for g, (win, dil) in enumerate(WINDOWS):
        n = win // dil
        s = n + (t[:, None] // dil if dil < DEC_T else 0 * t[:, None]) - m
        slope = slopes_a[g][2 * c + hh][:, None]
        col = g * (P + DEC_T)
        bias_sa[:, col:col + P] = np.where(s <= n, slope * (s * dil).astype(f), f(MASKED))
        back = t[:, None] - j
        bias_sa[:, col + P:col + P + DEC_T] = np.where((back >= 0) & (back % dil == 0) & (back <= win),
                                                       slope * back.astype(f), f(MASKED))
    back = PAST + t[:, None] - np.arange(KEYS_B)[None, :]
    bias_sb[:] = np.where(back >= 0, slopes_b[c][:, None] * back.astype(f), f(MASKED))
    e = np.arange(CW)[None, :]
    mask = np.stack([e // HD == (2 * c + hh)[:, None], e // P == c[:, None]]).astype(f)
    sel = (t[:, None] == j).astype(f)
    coef = np.stack([hh == 0, hh == 1], axis=1).astype(f)
    return dict(ident=np.eye(P, dtype=f), bias_a=bias_a, bias_b=bias_b, bias_sa=bias_sa, bias_sb=bias_sb,
                mask=mask, sel=sel, coef=coef)


_INS = ["x_prompt", "x_sample", "cache_a0_kv", "cache_a1_kv", "cache_a2_kv", "cache_b_kv", "page_table", "norm_g",
        "w_in", "q_norm_a", "k_norm_a", "q_norm_b", "k_norm_b", "lambda_q1", "lambda_k1", "lambda_q2",
        "lambda_k2", "subln_g", "w_proj_a", "w_proj_b", "w_out"]
_OUTS = [(1, SEQ, D_MODEL), (DEC_B, DEC_T, D_MODEL),
         (1, 1, 128, 2, A_HEADS, HD), (1, 1, 512, 2, A_HEADS, HD), (1, 1, 1024, 2, A_HEADS, HD),
         (1, 1, SEQ, 2, B_HEADS, P),
         (1, DEC_B, 128, 2, A_HEADS, HD), (1, DEC_B, 512, 2, A_HEADS, HD), (1, DEC_B, 2048, 2, A_HEADS, HD),
         (1, DEC_B, DEC_T, 2, B_HEADS, P)]


def kernel(**inputs):
    import concourse.bacc as bacc
    from concourse.bass_utils import run_bass_kernel_spmd

    nc = bacc.Bacc("TRN2", target_bir_lowering=False, num_devices=1)
    arrays, aps = {}, {}
    for name, a in [(n, inputs[n]) for n in _INS] + list(shape_constants().items()):
        a = np.ascontiguousarray(a)
        arrays[f"in_{name}"] = a
        aps[name] = nc.dram_tensor(f"in_{name}", a.shape, mybir.dt.from_np(a.dtype), kind="ExternalInput").ap()
    outs = [nc.dram_tensor(f"out_{i}", shape, F32, kind="ExternalOutput").ap() for i, shape in enumerate(_OUTS)]
    i = aps
    build_step(nc, i["x_prompt"], i["x_sample"], [i["cache_a0_kv"], i["cache_a1_kv"], i["cache_a2_kv"]],
               i["cache_b_kv"], i["page_table"], i["norm_g"], i["w_in"], i["q_norm_a"], i["k_norm_a"],
               i["q_norm_b"], i["k_norm_b"], i["lambda_q1"], i["lambda_k1"], i["lambda_q2"], i["lambda_k2"],
               i["subln_g"], i["w_proj_a"], i["w_proj_b"], i["w_out"], i["ident"], i["bias_a"], i["bias_b"],
               i["bias_sa"], i["bias_sb"], i["mask"], i["sel"], i["coef"],
               outs[0], outs[1], outs[2:5], outs[5], outs[6:9], outs[9])
    r = run_bass_kernel_spmd(nc, [arrays], core_ids=[0])
    return tuple(r.results[0][f"out_{k}"] for k in range(len(_OUTS)))
```

```python
from contextlib import ExitStack

import numpy as np

import concourse.bass as bass
from concourse import mybir

ALU = mybir.AluOpType
ACT = mybir.ActivationFunctionType
AX_X = mybir.AxisListType.X
F32 = mybir.dt.float32
F32R = mybir.dt.float32r
I32 = mybir.dt.int32

P = 128
D_MODEL = 1024
SEQ = 1024
DEC_B = 8
DEC_T = 8
NS = DEC_B * DEC_T
ROWS = SEQ + NS
HD = 64
WINDOWS = ((128, 1), (512, 4), (2048, 16))
PAST = 2048
PAGE = 128
N_PAGES = PAST // PAGE
A_HEADS = 8
B_HEADS = 4
CW = 512
EPS = 1e-6
LAM_INIT = 0.2
MASKED = 1e30
NT = SEQ // P
TILES = NT + 1
NC = CW // P
KC = D_MODEL // P
NEW_A = 3 * (P + DEC_T)
KEYS_B = PAST + DEC_T

A_QKV = len(WINDOWS) * CW
COL = dict(qa=0, ka=A_QKV, va=2 * A_QKV, ga=3 * A_QKV, qb=3 * A_QKV + CW, kb=3 * A_QKV + 2 * CW,
           vb=3 * A_QKV + 3 * CW, gb=3 * A_QKV + 4 * CW, ma=3 * A_QKV + 5 * CW,
           mb=3 * A_QKV + 5 * CW + D_MODEL)


def weight_blocks():
    blocks = []
    for part, kind in (("qb", "q"), ("kb", "k"), ("vb", "v")):
        blocks.append((kind, 0, "in", COL[part], KC))
    for g in range(3):
        for part, kind in (("qa", "q"), ("ka", "k"), ("va", "v")):
            blocks.append((kind, g + 1, "in", COL[part] + g * CW, KC))
    for br in ("a", "b"):
        blocks.append(("g" + br, 0, "in", COL["g" + br], KC))
        for half in range(2):
            blocks.append(("m" + br, half, "in", COL["m" + br] + half * CW, KC))
            blocks.append(("p" + br, half, "proj_" + br, half * CW, NC))
    for half in range(2):
        blocks.append(("out", half, "out", half * CW, KC))
    return blocks


def width_a(G, i):
    if G == 1:
        return P if i == 0 else 2 * P
    if G == 2:
        return 2 * P if i % 2 else P
    return P


COPY_PARTS = ((0, 0, 120, 1536), (1, 0, 504, 1536)) + tuple((2, 510 * j, 510, 2720) for j in range(4))
COPY_AT = (1, 4, 7)
PV_FROM, PV_EARLY = 20, 8
A_TURN, A_VALUES = 4, 6
SCALE_AT = 420
NEW_AT, OUT_AT = 64, 96
TILE_ORDER = (7, 0, 6, 1, 5, 2, 4, 3)


def pieces_of(e):
    n = TILE_ORDER[e % 8] + 1
    p = pieces_before(e)
    return [(p, 0, n)] if n <= 4 else [(p, 0, 4), (p + 1, 4, n - 4)]


def pieces_before(e):
    whole, e = divmod(e, 16)
    return 24 * whole + sum(1 if TILE_ORDER[x % 8] < 4 else 2 for x in range(e))


def build_step(nc, x_p, x_s, ca, cb, page_table, norm_g, w_in, qna, kna, qnb, knb, lq1, lk1, lq2, lk2,
               subln, w_pa, w_pb, w_o, c_ident, c_bias_a, c_bias_b, c_bias_sa, c_bias_sb, c_mask, c_sel,
               c_coef, y_p, y_s, na_p, nb_p, na_s, nb_s):
    ds = bass.ds
    U = weight_blocks()
    w_dram = {"in": w_in[0], "proj_a": w_pa[0], "proj_b": w_pb[0], "out": w_o[0]}
    first_chunk = [0]
    for blk in U:
        first_chunk.append(first_chunk[-1] + blk[4])
    n_phys = cb.shape[1]
    FIRST_GATE = 12
    U_OUT = 22

    def nrows(i):
        return P if i < NT else NS

    with ExitStack() as ctx:
        def sem(name):
            return ctx.enter_context(nc.semaphore(name))

        def dram(name, shape):
            return nc.dram_tensor(name, shape, F32, kind="Internal").ap()

        top = [(nc.sbuf_base + 63) // 64 * 64]

        def place(name, shape, dt=F32, at=None):
            size = 4 * int(np.prod(shape[1:]))
            off = top[0] if at is None else at[0]
            t = nc.alloc_sbuf_tensor_at(name, list(shape), dt, offset=off)
            (top if at is None else at)[0] = off + (size + 31) // 32 * 32
            return t

        hT_hi = place("hT_hi", [P, KC, ROWS], F32R)
        hT_lo = place("hT_lo", [P, KC, ROWS], F32R)
        ident = place("ident", [P, P])
        gcol = place("gcol", [P, KC])
        qcol = place("qcol", [P, 2])
        krow = place("krow", [P, 2, HD])
        lam = place("lam", [P, 8])
        subrow = place("subrow", [P, P])
        half_pow = place("half_pow", [P, 8])
        ss = place("ss", [P, 2, 8])
        rs = place("rs", [P, 2, 8])
        ss_x = place("ss_x", [P, 2, 1])
        rs_x = place("rs_x", [P, 2, 1])
        qTs = place("qTs", [P, 4, NC, NS + DEC_T])
        coef = place("coef", [NS, 2])
        st_sum = place("st_sum", [P, 2, 2, 16])
        st = place("st", [P, NT, 16])
        rlB = place("rlB", [P, 2, NT, 2])
        wB = place("wB", [P, 2, NT])
        sc_s = place("sc_s", [NS, 16])
        w_base = top[0]
        raw = place("raw", [P, 4, CW])
        w_hi, w_lo, set_at = [], [], []
        for s in range(2):
            set_at.append(top[0])
            w_hi.append(place(f"w_hi{s}", [P, KC, CW], F32R))
            w_lo.append(place(f"w_lo{s}", [P, KC, CW], F32R))
        q_base = top[0]
        qT = place("qT", [P, NC * SEQ])
        k_base = top[0]
        kT = place("kT", [P, NC * SEQ])
        v_sb = place("v_sb", [P, TILES, CW])
        work = top[0]
        zn = place("zn", [P, 2, CW])
        kn = place("kn", [P, 3, CW])
        end = top[0]
        assert end <= nc.sbuf_usable_end, end
        at = [k_base]
        xt = place("xt", [P, 2, D_MODEL], at=at)
        xn = place("xn", [P, 2, D_MODEL], at=at)
        hn = place("hn", [P, 2, CW], at=at)
        lamv = place("lamv", [P, 4, HD], at=at)
        at = [work]
        qz = place("qz", [P, 2, SEQ], at=at)
        att = []
        for s in range(2):
            at = [set_at[s]]
            if s == 0:
                sB = [place(f"sB{j}", [P, 2, P * (1 + max(TILE_ORDER[j::4]))], at=at) for j in range(4)]
                ptB = place("ptB", [P, 4, CW], at=at)
                assert at[0] <= set_at[s] + 2 * 4 * KC * CW
            at = [set_at[s]]
            att.append(dict(sA=place(f"sA{s}", [P, 8, 256], at=at), tA=place(f"tA{s}", [P, 2, 2, 256], at=at),
                            ptA=place(f"ptA{s}", [P, 8, 256], at=at)))
        tB = place("tB", [P, 2, SEQ], at=[w_base])
        NKS, NVS, NVH = 6, 10, 6
        at = [w_base]
        k_in = place("k_in", [P, NKS, CW], at=at)
        v_lo = place("v_lo", [P, NVS, CW], F32R, at=[at[0]])
        v_in = place("v_in", [P, NVS, CW], at=at)
        v_hi = place("v_hi", [P, NVH, CW], F32R, at=at)
        wide = place("wide", [P, 2 * KEYS_B], at=at)
        s_b, bias_sb = wide[0:NS, 0:KEYS_B], wide[0:NS, KEYS_B:2 * KEYS_B]
        kv_new = wide[NEW_AT:NEW_AT + DEC_T, 0:8 * CW].rearrange("p (v g x) -> p v g x", v=2, g=4)
        os_ = wide[OUT_AT:OUT_AT + DEC_T, 0:2 * CW].rearrange("p (v x) -> p v x", v=2)
        q_all = [place(f"q_all{x}", [P, 4, NC, NS], F32R, at=at) for x in range(2)]
        q_g1 = [place(f"q_g1{x}", [P, 4, NC, NS], F32R, at=at) for x in range(2)]
        q_g2 = [place(f"q_g2{x}", [P, 8, NC, NS], F32R, at=at) for x in range(2)]
        kTs = [place(f"kTs{x}", [P, 3, NC, P], F32R, at=at) for x in range(2)]
        kTn = [place(f"kTn{x}", [P, 16, DEC_T], F32R, at=at) for x in range(2)]
        narrow = place("narrow", [P, NEW_A], at=at)
        s_a = narrow[0:NS]
        pTn = narrow[NEW_AT:NEW_AT + DEC_T, 0:4 * NS].rearrange("p (g q) -> p g q", g=4)
        bias_sa = place("bias_sa", [NS, NEW_A], at=at)
        pT0 = place("pT0", [P, 2 * NS], F32R, at=at)
        pT1 = place("pT1", [P, 4, 2 * NS], F32R, at=at)
        pT2 = place("pT2", [P, 8, 2 * NS], F32R, at=at)
        pTb = place("pTb", [P, N_PAGES, 2 * NS], F32R, at=at)
        mask = place("mask", [2 * NS, 2, CW], at=at)
        om = place("om", [2 * NS, 2, CW], at=at)
        twice = place("twice", [NS, 2 * NS], at=at)
        scale2 = place("scale2", [2 * NS, 2], at=at)
        sel = place("sel", [2 * NS, DEC_T], at=at)
        pids = place("pids", [1, DEC_B * N_PAGES], I32, at=at)
        assert at[0] <= end, (at[0], end)
        at = [q_base]
        yT_hi = place("yT_hi", [P, NC, ROWS], F32R, at=at)
        yT_lo = place("yT_lo", [P, NC, ROWS], F32R, at=at)
        sig_at = at[0]
        sig = place("sig", [P, TILES, CW], at=at)
        zy = place("zy", [P, 2, CW], at=at)
        stc = place("stc", [P, NT, 3, 16], at=at)
        ew = place("ew", [P, NT, 3, 8], at=at)
        el = place("el", [P, NT, 3, 8], at=at)
        nmin = place("nmin", [P, NT, 8], at=at)
        den = place("den", [P, NT, 8], at=at)
        assert at[0] <= end, (at[0], end)
        at = [sig_at]
        og = place("og", [P, 2, 3, CW], at=at)
        sg = place("sg", [P, 2, CW], at=at)
        at = [q_base]
        mt = place("mt", [P, 2, D_MODEL], at=at)
        xl = place("xl", [P, 2, CW], at=at)
        yo = place("yo", [P, 3, CW], at=at)

        ps = ctx.enter_context(nc.psum_tensor("ps", [P, 8 * CW], F32))

        def bank(b, n=1):
            return ps[:, b * CW:(b + n) * CW]

        o_scr = [dram(f"o_scr{g}", [SEQ, CW]) for g in range(4)]
        st_scr = [dram(f"st_scr{g}", [SEQ, 16]) for g in range(3)]
        os_scr = dram("os_scr", [2, NS, CW])
        ma_scr = dram("ma_scr", [ROWS, D_MODEL])
        m_scr = dram("m_scr", [ROWS, D_MODEL])

        first_in = sem("first_in")
        const_in = sem("const_in")
        setup = sem("setup")
        x_in = [sem(f"x_in{s}") for s in range(2)]
        h_ss, h_rs, h_xn, h_t, h_hn, h_hi, h_lo = (sem(n) for n in (
            "h_ss", "h_rs", "h_xn", "h_t", "h_hn", "h_hi", "h_lo"))
        pool_step = sem("pool_step")
        dve_step = sem("dve_step")
        raw_in = [sem(f"raw_in{s}") for s in range(4)]
        hi_done, lo_done = sem("hi_done"), sem("lo_done")
        z_ready = sem("z_ready")
        sq_ready, ss_ready, rs_ready = sem("sq_ready"), sem("ss_ready"), sem("rs_ready")
        zn_ready, kn_ready, v_ready = sem("zn_ready"), sem("kn_ready"), sem("v_ready")
        t_ready, t_moved = sem("t_ready"), sem("t_moved")
        k_out = [sem(f"k_out{s}") for s in range(3)]
        v_out, o_out = sem("v_out"), sem("o_out")
        copies = sem("copies")
        bq, bs, be, ba, bt, bm, bp, bo, bw, btab = (sem(n) for n in (
            "b_scores", "b_biased", "b_exp", "b_diff", "b_probsT", "b_probsT_moved", "b_piece_used",
            "b_stored", "b_weight", "b_table"))
        aq, as_, ae, atp, am, av, ao, ast, atab = (sem(n) for n in (
            "a_scores", "a_biased", "a_exp", "a_probsT", "a_probsT_moved", "a_values", "a_stored",
            "a_stats", "a_table"))
        btab2, atab2 = sem("b_table1"), sem("a_table1")
        qz_ready = sem("qz_ready")
        s_const = sem("s_const")
        sk_in = [sem(f"sk_in{s}") for s in range(NKS)]
        sv_in = [sem(f"sv_in{s}") for s in range(NVS)]
        sn_in, sq_b = sem("sn_in"), sem("s_queries")
        s_kt, s_km, s_qk, s_nt, s_nm = (sem(n) for n in (
            "s_keysT", "s_keysT_moved", "s_scored", "s_newT", "s_newT_moved"))
        s_ta, s_tb, s_min, s_ea, s_eb = (sem(n) for n in (
            "s_biased_a", "s_biased_b", "s_min_b", "s_exp_a", "s_exp_b"))
        s_pa, s_pam, s_pb, s_pbm = (sem(n) for n in (
            "s_probsT_a", "s_probsT_a_moved", "s_probsT_b", "s_probsT_b_moved"))
        s_pv, s_va, s_vb, s_om, s_sel, s_oc, s_out, s_rec = (sem(n) for n in (
            "s_tile_used", "s_values_a", "s_values_b", "s_masked", "s_summed", "s_o_copied", "s_o_out",
            "s_recip"))
        s_zero = sem("s_zero")
        s_kh, s_nh, svn_in, s_vh, s_vlp, s_vld, s_qh, s_twice, s_scale, s_ph = (sem(n) for n in (
            "s_keysT_hi", "s_newT_hi", "s_new_values", "s_values_hi", "s_values_lo_pool",
            "s_values_lo_dve", "s_queries_hi", "s_scale_twice", "s_scale_moved", "s_probsT_hi"))
        st_in, ew_ready, ew_exp = sem("st_in"), sem("ew_ready"), sem("ew_exp")
        og_in = [sem(f"og_in{s}") for s in range(2)]
        sg_ready, silu_ready, og_pool, y_ready, y_t, y_hi, y_lo = (sem(n) for n in (
            "sg_ready", "silu_ready", "og_pool", "y_ready", "y_t", "y_hi", "y_lo"))
        osq, oss, ors = sem("o_square"), sem("o_sum"), sem("o_rstd")
        sig_ready, m_ready = sem("sig_ready"), sem("m_ready")
        m_out = sem("m_out")
        ml_in = [sem(f"ml_in{s}") for s in range(2)]
        mt_in = [sem(f"mt_in{s}") for s in range(2)]
        m_t, m_hi, m_lo = sem("m_t"), sem("m_hi"), sem("m_lo")
        xl_in = [sem(f"xl_in{s}") for s in range(2)]
        yo_ready = sem("yo_ready")
        yo_out = [sem(f"yo_out{s}") for s in range(3)]

        N_CONST = 16 * 12
        N_COPIES = len(COPY_PARTS) * DEC_B

        def mi(G, kind, i):
            return 18 * G + (9 if kind == "k" else 0) + i

        def ti(G, kind, i):
            return 17 * G + (9 if kind == "k" else 0) + i

        def x_bank(j):
            return 4 + j if j < 4 else 7

        def z_freed(n):
            u, i = divmod(n, TILES)
            kind, G = U[u][0], U[u][1]
            br = 9 if kind[-1] == "b" else 0
            if kind in "qk":
                return zn_ready, mi(G, kind, i) + 1
            if kind == "v":
                return v_ready, 9 * G + i + 1
            if kind in ("ga", "gb"):
                return silu_ready, br + i + 1
            if kind in ("ma", "mb"):
                return sig_ready, 2 * br + 9 * G + i + 1
            if kind in ("pa", "pb"):
                return m_ready, 2 * br + 9 * G + i + 1
            return yo_ready, 9 * G + i + 1

        def row_start_step(G, i):
            if G <= 1:
                return i * P, 1
            if G == 2:
                return (i // 2) + (i % 2) * 512, 4
            return i, 8

        def rows_of(ap, G, i):
            a, s = row_start_step(G, i)
            return ap[a:a + s * (P - 1) + 1:s] if s > 1 else ap[a:a + P]

        def hT_of(h, G, k, i):
            if i == NT:
                return h[:, k, SEQ:ROWS]
            a, s = row_start_step(G, i)
            return h[:, k, a:a + s * (P - 1) + 1:s]

        def kept(G, i, kv):
            if G == 0:
                return nb_p[0, 0, i * P:(i + 1) * P, kv].rearrange("s h e -> s (h e)")
            out = na_p[G - 1][0, 0, :, kv].rearrange("s h e -> s (h e)")
            if G == 1:
                return out if i == NT - 1 else None
            if G == 2:
                return out[i // 2::4] if i % 2 else None
            return out[i::8]

        def kept_new(G, kv):
            if G == 0:
                return nb_s[0, :, :, kv].rearrange("b t h e -> b t (h e)")
            length = WINDOWS[G - 1][0]
            return na_s[G - 1][0, :, length - DEC_T:length, kv].rearrange("b t h e -> b t (h e)")

        k_sent = {s: [0] * (4 * TILES) for s in range(3)}
        v_sent = []
        for s in range(3):
            c = 0
            for kk in range(4 * TILES):
                G, i = divmod(kk, TILES)
                if kk % 3 == s and (i == NT or kept(G, i, 0) is not None):
                    c += 16
                k_sent[s][kk] = c
        c = 0
        for G in range(4):
            for i in range(TILES):
                c += 16 if (i == NT or kept(G, i, 1) is not None) else 0
            v_sent.append(c)

        def og_total(y):
            return sum(48 if yy < NT else 16 for yy in range(y % 2, y + 1, 2))

        NTS = 13 + N_PAGES

        def uses(slots, T):
            return len(range(T % slots, NTS, slots))

        def before(slots, T):
            last = T - slots if T >= slots else max(range(T, NTS, slots)) - NTS
            return last + 1

        def x_bank_s(T):
            return (0, 1, 6)[T % 3]

        def lo_of(T):
            if T < 13:
                return s_vlp, 21, T
            k = T - 13
            return (s_vlp, 21, 13 + k // 2) if k % 2 == 0 else (s_vld, 8, k // 2)

        def dims(ap, off, d):
            return bass.AP(ap.tensor, ap.offset + off, [list(ap.ap[0])] + d)

        def spread(t, h, src_q):
            def on(x, d):
                return dims(x[h * HD:(h + 1) * HD, 0, 0, 0:1], h, d)
            return ((on(t[0], [[NC * NS, 4], [NS + 16, NC], [2, DEC_T]]), src_q),
                    (on(t[1], [[NC * NS + 2, 4], [NS + 16, NC], [8, 2]]),
                     src_q[:, 2, :, :].rearrange("p c (u r) -> p r c u", u=2)),
                    (on(t[2], [[NC * NS + 2, 8], [NS + 16, NC]]),
                     src_q[:, 3, :, :].rearrange("p c r -> p r c")))

        def a_probs(part):
            def at_psum(off, d):
                return dims(ps[:, 5 * CW + off:5 * CW + off + 1], 0, d)
            W2 = 2 * NS
            return ((pT0[:, part * NS:(part + 1) * NS], bank(5)[:, 0:NS]),
                    (dims(pT1[:, 0, 0:1], part * NS, [[W2 + 2, 4], [8, 8], [1, 2]]),
                     at_psum(NS, [[2, 4], [8, 8], [1, 2]])),
                    (dims(pT2[:, 0, 0:1], part * NS, [[W2 + 2, 8], [16, 4], [1, 2]]),
                     at_psum(2 * NS, [[2, 8], [16, 4], [1, 2]])))

        def wait_reg(eng, s, value):
            eng.wait_ge(s, value)
            eng.nop(nofuse=True)

        block = ctx.enter_context(nc.Block())

        @block.sync
        def _(sp):
            sp.dma_start(ident[:, :], c_ident).then_inc(first_in, 16)
            sp.dma_start(gcol[:, :], norm_g[0].rearrange("(c p) -> p c", p=P), allow_slow_non_contiguous=True).then_inc(first_in, 16)

            def load_x(i):
                if i >= 2:
                    sp.wait_ge(h_xn, i - 1)
                src = x_p[0, i * P:(i + 1) * P, :] if i < NT else x_s.rearrange("b t d -> (b t) d")
                sp.dma_start(xt[0:nrows(i), i % 2, :], src).then_inc(x_in[i % 2], 16)

            def load_chunk(u, k):
                q = first_chunk[u] + k
                if q >= 4:
                    sp.wait_ge(lo_done, q - 3)
                _, _, name, col, _ = U[u]
                sp.dma_start(raw[:, q % 4, :], w_dram[name][k * P:(k + 1) * P, col:col + CW])\
                    .then_inc(raw_in[q % 4], 16)

            load_x(0)
            load_x(1)
            for k in range(4):
                load_chunk(0, k)
            load_x(2)
            for k in range(4, KC):
                load_chunk(0, k)
            for col, vec in ((0, qna), (1, qnb)):
                for h in range(2):
                    sp.dma_start(qcol[h * HD:(h + 1) * HD, col:col + 1],
                                 vec[0].rearrange("(d o) -> d o", o=1)).then_inc(const_in, 16)
            for col, vec in ((0, kna), (1, knb)):
                sp.dma_start(krow[:, col, :], vec[0].partition_broadcast(P)).then_inc(const_in, 16)
            for col, vec in enumerate((lq1, lk1, lq2, lk2)):
                sp.dma_start(lamv[:, col, :], vec[0].partition_broadcast(P)).then_inc(const_in, 16)
            sp.dma_start(coef[:, :], c_coef).then_inc(const_in, 16)
            sp.dma_start(subrow[:, :], subln[0].partition_broadcast(P)).then_inc(const_in, 16)


            def block_io(u):
                kind, G = U[u][0], U[u][1]
                prefetch = u + 1 < len(U) and u + 1 != FIRST_GATE
                for i in range(TILES):
                    if u == 0 and 3 <= i + 3 < TILES:
                        load_x(i + 3)
                    if prefetch and i < U[u + 1][4]:
                        load_chunk(u + 1, i)
                    if kind == "k":
                        kk = TILES * G + i
                        dst = kept(G, i, 0) if i < NT else kept_new(G, 0)
                        if dst is not None:
                            sp.wait_ge(kn_ready, kk + 1)
                            sp.dma_start(dst, kn[0:nrows(i), kk % 3, :])\
                                .then_inc(k_out[kk % 3], 16)
                    if kind == "v":
                        dst = kept(G, i, 1) if i < NT else kept_new(G, 1)
                        if dst is not None:
                            sp.wait_ge(v_ready, TILES * G + i + 1)
                            sp.dma_start(dst, v_sb[0:nrows(i), i, :]).then_inc(v_out, 16)

            def tables(G):
                set_ = (3 * G + 2) % 2
                if G == 0:
                    sp.wait_ge(lo_done, first_chunk[4])
                    for h in range(B_HEADS):
                        if h >= 2:
                            sp.wait_ge(bs, 16 + 16 * (h - 1))
                        sp.dma_start(tB[:, h % 2, :], c_bias_b[h])\
                            .then_inc(btab if h % 2 == 0 else btab2, 16)
                else:
                    for c in range(NC):
                        if c < 2:
                            sp.wait_ge(z_ready, 27 * (G + 1))
                        else:
                            sp.wait_ge(as_, 16 + 64 * (G - 1) + 16 * (c - 1))
                        sp.dma_start(att[set_]["tA"][:, c % 2, :, :],
                                     c_bias_a[G - 1, 2 * c:2 * c + 2].rearrange("h p x -> p h x"))\
                            .then_inc(atab if c % 2 == 0 else atab2, 16)

            def attention_out(G):
                if G == 0:
                    sp.wait_ge(bo, 8 + 32)
                else:
                    sp.wait_ge(ao, 8 + 32 * G)
                    sp.wait_ge(ast, 4 * G)
                for i in range(NT):
                    sp.dma_start(rows_of(o_scr[G], G, i).rearrange("s (c e) -> s c e", c=NC),
                                 qT[:, :].rearrange("p (c s) -> p c s", c=NC)[:, :, i * P:(i + 1) * P])\
                        .then_inc(o_out, 16)
                    if G:
                        sp.dma_start(rows_of(st_scr[G - 1], G, i), st[:, i, :]).then_inc(o_out, 16)

            for G in range(4):
                for kind in range(3):
                    block_io(3 * G + kind)
                tables(G)
                attention_out(G)

            sp.wait_ge(o_out, 16 * 8 * 7)
            sp.dma_start(pids[0:1, :], page_table.rearrange("b n -> (b n)").rearrange("(o n) -> o n", o=1))\
                .then_inc(s_const, 16)
            sp.dma_start(bias_sa[:, :], c_bias_sa).then_inc(s_const, 16)
            sp.dma_start(bias_sb, c_bias_sb).then_inc(s_const, 16)
            for x in range(2):
                rows = slice(x * NS, (x + 1) * NS)
                sp.dma_start(mask[rows, :, :], c_mask.rearrange("g q e -> q g e")).then_inc(s_const, 16)
                sp.dma_start(sel[rows, :], c_sel).then_inc(s_const, 16)
            sp.wait_ge(s_const, 112)
            for s in range(3):
                sp.wait_ge(k_out[s], k_sent[s][-1])
            sp.wait_ge(v_out, v_sent[-1])

            with sp.Fori(0, DEC_B) as b:
                def load_new(kv, landed):
                    for g in range(3):
                        ln = WINDOWS[g][0]
                        sp.dma_start(kv_new[:, kv, g, :],
                                     na_s[g][0, ds(b, 1), ln - DEC_T:ln, kv].rearrange("o t h e -> (o t) (h e)"))\
                            .then_inc(landed, 16)
                    sp.dma_start(kv_new[:, kv, 3, :],
                                 nb_s[0, ds(b, 1), :, kv].rearrange("o t h e -> (o t) (h e)"))\
                        .then_inc(landed, 16)

                def rows(T, kv):
                    if T >= 13:
                        pid = sp.value_load(pids[0:1, ds(b * N_PAGES + T - 13, 1)], min_val=0, max_val=n_phys - 1)
                        return cb[0, ds(pid, 1), :, kv].rearrange("o s h e -> (o s) (h e)")
                    g, r = (0, 0) if T == 0 else ((1, T - 1) if T < 5 else (2, T - 5))
                    return ca[g][0, ds(b, 1), r::WINDOWS[g][1], kv].rearrange("o m h e -> (o m) (h e)")

                def load_k(T):
                    wait_reg(sp, s_kt, 29 * b + 29 + before(NKS, T))
                    sp.dma_start(k_in[:, T % NKS, :], rows(T, 0)).then_inc(sk_in[T % NKS], 16)

                def load_v(T):
                    wait_reg(sp, s_pv, 29 * b + 29 + before(NVS, T))
                    sp.dma_start(v_in[:, T % NVS, :], rows(T, 1)).then_inc(sv_in[T % NVS], 16)

                for T in range(NKS):
                    load_k(T)
                wait_reg(sp, s_nt, b + 1)
                load_new(0, sn_in)
                for T in range(NVS):
                    load_v(T)
                    load_k(NKS + T)
                wait_reg(sp, s_vb, b + 1)
                load_new(1, svn_in)
                for T in range(NKS + NVS, PV_FROM + NKS + 1):
                    load_k(T)
                for T in range(NVS, NTS):
                    load_v(T)
                    if PV_FROM + NKS + 1 + T - NVS < NTS:
                        load_k(PV_FROM + NKS + 1 + T - NVS)

            sp.wait_ge(s_out, 32 + 32 * DEC_B)
            for k in range(KC):
                load_chunk(FIRST_GATE, k)
            for g in range(3):
                sp.dma_start(stc[:, :, g, :], st_scr[g].rearrange("(i p) s -> p i s", p=P)).then_inc(st_in, 16)

            def load_og(y):
                br, i = divmod(y, TILES)
                if y >= 2:
                    sp.wait_ge(y_ready, y - 1)
                if i == NT:
                    sp.dma_start(og[0:NS, y % 2, 0, :], os_scr[br]).then_inc(og_in[y % 2], 16)
                else:
                    for g in range(3 if br == 0 else 1):
                        src = o_scr[g + 1 if br == 0 else 0]
                        sp.dma_start(og[:, y % 2, g, :], src[i * P:(i + 1) * P, :]).then_inc(og_in[y % 2], 16)

            def rows_m(scr, i, half):
                return scr[i * P:i * P + nrows(i), half * CW:(half + 1) * CW]

            for u in range(FIRST_GATE, len(U)):
                kind, half = U[u][0], U[u][1]
                br = 1 if kind[-1] == "b" else 0
                if kind in ("ga", "gb"):
                    if br:
                        sp.wait_ge(m_out, 16 * 18)
                    load_og(9 * br)
                    load_og(9 * br + 1)
                if kind == "pb" and half == 0:
                    sp.wait_ge(y_t, 18)
                    for i in range(2):
                        sp.dma_start(zy[:, i, :], rows_m(ma_scr, i, 0)).then_inc(ml_in[i], 16)
                for i in range(TILES):
                    if u + 1 < len(U) and i < U[u + 1][4]:
                        load_chunk(u + 1, i)
                    if kind in ("ga", "gb") and i + 2 < TILES:
                        load_og(9 * br + i + 2)
                    if kind in ("pa", "pb"):
                        idx = 18 * br + 9 * half + i
                        sp.wait_ge(m_ready, idx + 1)
                        sp.dma_start(rows_m(m_scr if br else ma_scr, i, half), sig[0:nrows(i), i, :])\
                            .then_inc(m_out, 16)
                        nxt = 9 * half + i + 2
                        if br and nxt < 18:
                            hn_, in_ = divmod(nxt, 9)
                            sp.dma_start(zy[0:nrows(in_), nxt % 2, :], rows_m(ma_scr, in_, hn_))\
                                .then_inc(ml_in[nxt % 2], 16)
                    if kind == "out":
                        idx = 9 * half + i
                        if half == 0 and i == 0:
                            sp.wait_ge(m_out, 16 * 36)
                            for ii in range(2):
                                sp.dma_start(mt[0:nrows(ii), ii % 2, :], m_scr[ii * P:ii * P + nrows(ii), :])\
                                    .then_inc(mt_in[ii % 2], 16)
                            for ii in range(2):
                                sp.dma_start(xl[:, ii % 2, :], x_p[0, ii * P:(ii + 1) * P, 0:CW])\
                                    .then_inc(xl_in[ii % 2], 16)
                        if half == 0 and i + 2 < TILES:
                            ii = i + 2
                            sp.wait_ge(m_t, 2 * i + 2)
                            sp.dma_start(mt[0:nrows(ii), ii % 2, :], m_scr[ii * P:ii * P + nrows(ii), :])\
                                .then_inc(mt_in[ii % 2], 16)
                        sp.wait_ge(yo_ready, idx + 1)
                        dst = (y_p[0, i * P:(i + 1) * P, :] if i < NT else y_s.rearrange("b t d -> (b t) d"))
                        sp.dma_start(dst[:, half * CW:(half + 1) * CW], yo[0:nrows(i), idx % 3, :])\
                            .then_inc(yo_out[idx % 3], 16)
                        nxt = idx + 2
                        if nxt < 18:
                            hn_, in_ = divmod(nxt, 9)
                            src = (x_p[0, in_ * P:(in_ + 1) * P, :] if in_ < NT else
                                   x_s.rearrange("b t d -> (b t) d"))
                            sp.dma_start(xl[0:nrows(in_), nxt % 2, :], src[:, hn_ * CW:(hn_ + 1) * CW])\
                                .then_inc(xl_in[nxt % 2], 16)
            for s in range(3):
                sp.wait_ge(yo_out[s], 16 * 6)
            sp.wait_ge(copies, 16 * N_COPIES)
            for s in range(3):
                sp.wait_ge(k_out[s], k_sent[s][-1])
            sp.wait_ge(v_out, v_sent[-1])

        @block.gpsimd
        def _(pool):
            steps = [0]

            def link(ins):
                steps[0] += 1
                ins.then_inc(pool_step, 1)
                pool.wait_ge(pool_step, steps[0])

            link(pool.memset(half_pow[:, :], -0.5))

            def rstd(out, in_, n, heads):
                r = in_.shape[0]
                link(pool.tensor_scalar(in_, in_, 1.0 / n, EPS, ALU.mult, ALU.add))
                return pool.tensor_tensor(out, in_, half_pow[0:r, 0:heads], ALU.pow)

            def input_lo(i):
                for half in range(2):
                    j = 2 * i + half
                    pool.wait_ge(h_hi, j + 1)
                    c0 = i * P
                    pool.tensor_tensor(hT_lo[:, 4 * half:4 * half + 4, c0:c0 + nrows(i)],
                                       hn[:, half, :].rearrange("p (k r) -> p k r", k=4)[:, :, 0:nrows(i)],
                                       hT_hi[:, 4 * half:4 * half + 4, c0:c0 + nrows(i)].bitcast(F32),
                                       ALU.subtract).then_inc(h_lo, 1)

            def split_lo(u, k):
                q = first_chunk[u] + k
                if k == 0 and u in (1, FIRST_GATE + 1):
                    pool.wait_ge(lo_done, q)
                pool.wait_ge(hi_done, q + 1)
                pool.tensor_tensor(w_lo[u % 2][:, k, :], raw[:, q % 4, :],
                                   w_hi[u % 2][:, k, :].bitcast(F32), ALU.subtract).then_inc(lo_done, 1)

            def input_step(i):
                if i < TILES:
                    pool.wait_ge(h_ss, i + 1)
                    rstd(rs_x[0:nrows(i), i % 2, 0:1], ss_x[0:nrows(i), i % 2, 0:1], D_MODEL, 1)\
                        .then_inc(h_rs, 1)
                if 1 <= i <= TILES:
                    input_lo(i - 1)

            for i in range(3):
                input_step(i)

            def block_(u):
                kind, G = U[u][0], U[u][1]
                prefetch = u + 1 < len(U) and u + 1 != FIRST_GATE
                for i in range(TILES):
                    r = nrows(i)
                    if u == 0:
                        input_step(i + 3)
                    if kind in "qk":
                        m = mi(G, kind, i)
                        pool.wait_ge(ss_ready, m + 1)
                        rstd(rs[0:r, m % 2, :], ss[0:r, m % 2, :], HD, 8).then_inc(rs_ready, 1)
                    if kind == "k":
                        kk = TILES * G + i
                        pool.wait_ge(zn_ready, m + 1)
                        if kk >= 3:
                            G3, i3 = divmod(kk - 3, TILES)
                            pool.wait_ge(t_ready, ti(G3, "k", min(i3, NT - 1)) + 1)
                            if k_sent[kk % 3][kk - 3]:
                                pool.wait_ge(k_out[kk % 3], k_sent[kk % 3][kk - 3])
                        pool.tensor_tensor(kn[0:r, kk % 3, :].rearrange("p (h d) -> p h d", h=8),
                                           zn[0:r, m % 2, :].rearrange("p (h d) -> p h d", h=8),
                                           krow[0:r, 0 if G else 1, :].unsqueeze(1).to_broadcast([r, 8, HD]),
                                           ALU.mult).then_inc(kn_ready, 1)
                    if kind == "ga" and i < NT:
                        y = i
                        pool.wait_ge(ew_ready, 1)
                        pool.wait_ge(og_in[y % 2], 48 * (y // 2 + 1))
                        for g in (1, 2):
                            link(pool.tensor_tensor(
                                og[:, y % 2, g, :].rearrange("p (h d) -> p h d", h=8),
                                og[:, y % 2, g, :].rearrange("p (h d) -> p h d", h=8),
                                ew[:, i, g, :].unsqueeze(2).to_broadcast([P, 8, HD]), ALU.mult))
                        pool.tensor_tensor(og[:, y % 2, 1, :], og[:, y % 2, 1, :], og[:, y % 2, 2, :],
                                           ALU.add).then_inc(og_pool, 1)
                    if kind == "gb":
                        y = TILES + i
                        pool.wait_ge(og_in[y % 2], og_total(y))
                        if y >= TILES + 2:
                            pool.wait_ge(y_ready, y - 1)
                        pool.tensor_tensor(og[0:r, y % 2, 2, :].rearrange("p (h d) -> p h d", h=4),
                                           og[0:r, y % 2, 0, :].rearrange("p (h d) -> p h d", h=4),
                                           subrow[0:r, :].unsqueeze(1).to_broadcast([r, 4, P]), ALU.mult)\
                            .then_inc(og_pool, 1)
                        pool.wait_ge(oss, i + 1)
                        rstd(rs[0:r, i % 2, 0:4], ss[0:r, i % 2, 0:4], P, 4).then_inc(ors, 1)
                    if prefetch and i < U[u + 1][4]:
                        split_lo(u + 1, i)

            def pad_queries(G):
                pool.wait_ge(t_ready, 17 * G + 17)
                for s in range(3):
                    pool.wait_ge(k_out[s], k_sent[s][TILES * G + NT])
                link(pool.memset(qz[0:HD, 1, :], 0.0))
                link(pool.memset(qz[HD:P, 0, :], 0.0))
                pool.wait_ge(t_moved, 17 * G + 9)
                scored = aq if G else bq
                first = 16 + 64 * (G - 1) if G else 16
                order = range(NT) if G else TILE_ORDER
                for i in order:
                    cols = slice(i * P, (i + 1) * P)
                    pool.tensor_copy(qz[0:HD, 0, cols], qT[0:HD, cols])
                    pool.tensor_copy(qz[HD:P, 1, cols], qT[HD:P, cols]).then_inc(qz_ready, 1)
                with pool.Fori(0, NC - 1) as c:
                    for s, i in enumerate(order):
                        wait_reg(pool, scored, first + 16 * c + 2 * s + 2)
                        cols = slice(i * P, (i + 1) * P)
                        pool.tensor_copy(qz[0:HD, 0, cols], qT[0:HD, ds((c + 1) * SEQ + i * P, P)])
                        pool.tensor_copy(qz[HD:P, 1, cols], qT[HD:P, ds((c + 1) * SEQ + i * P, P)])\
                            .then_inc(qz_ready, 1)

            for G in range(4):
                for kind in range(3):
                    block_(3 * G + kind)
                pad_queries(G)
                if G:
                    pool.wait_ge(aq, 16 + 64 * G)
                else:
                    pool.wait_ge(bq, 16 + 64)

            pool.wait_ge(o_out, 16 * 8 * 7)
            for t in q_all:
                link(pool.memset(t[:, :, :, :].bitcast(F32), 0.0))
            link(pool.memset(qTs[:, :, :, NS:NS + DEC_T], 0.0))
            for x in range(2):
                link(pool.tensor_copy(twice[:, x * NS:(x + 1) * NS], ident[0:NS, 0:NS]))
            pool.sem_inc(s_zero, 1)

            def queries_lo(b):
                for h in range(2):
                    src = qTs[h * HD:(h + 1) * HD, :, :, ds(b * DEC_T, DEC_T)]
                    for (hi, q), (lo, _) in zip(spread((q_all[0], q_g1[0], q_g2[0]), h, src),
                                                spread((q_all[1], q_g1[1], q_g2[1]), h, src)):
                        ins = pool.tensor_tensor(lo, q, hi.bitcast(F32), ALU.subtract)
                    ins.then_inc(sq_b, 1)
                    wait_reg(pool, sq_b, 2 * b + h + 1)

            pool.wait_ge(s_zero, 2)
            pool.wait_ge(s_qh, 1)
            queries_lo(0)
            with pool.Fori(0, DEC_B) as b:
                for T in (*range(13), *range(13, NTS, 2)):
                    s = T % NVS
                    wait_reg(pool, s_vh, 29 * b + T + 1)
                    pool.tensor_tensor(v_lo[:, s, :], v_in[:, s, :],
                                       v_hi[:, T % NVH, :].bitcast(F32), ALU.subtract).then_inc(s_vlp, 1)
                    if T == 17:
                        wait_reg(pool, s_qh, b + 2)
                        wait_reg(pool, s_vlp, 21 * b + 16)
                        queries_lo(b + 1)

            for u in range(FIRST_GATE, len(U)):
                block_(u)

        @block.scalar
        def _(act):
            def copy_cache(j):
                b, part = divmod(j, len(COPY_PARTS))
                g, r0, rows, piece = COPY_PARTS[part]
                dst = na_s[g][0, b, r0:r0 + rows].rearrange("s v h e -> (s v h e)")
                src = ca[g][0, b, r0 + DEC_T:r0 + rows + DEC_T].rearrange("s v h e -> (s v h e)")
                act.dma_start(dst.rearrange("(a m x) -> a m x", a=16, x=piece),
                              src.rearrange("(a m x) -> a m x", a=16, x=piece)).then_inc(copies, 16)

            def input_hi(i):
                for half in range(2):
                    j = 2 * i + half
                    act.wait_ge(h_hn, j + 1)
                    act.activation(hT_hi[:, 4 * half:4 * half + 4, i * P:i * P + nrows(i)],
                                   hn[:, half, :].rearrange("p (k r) -> p k r", k=4)[:, :, 0:nrows(i)],
                                   ACT.Copy).then_inc(h_hi, 1)

            def split_hi(u, k):
                q = first_chunk[u] + k
                act.wait_ge(raw_in[q % 4], 16 * (q // 4 + 1))
                if u >= 2:
                    act.wait_ge(z_ready, TILES * (u - 1))
                act.activation(w_hi[u % 2][:, k, :], raw[:, q % 4, :], ACT.Copy).then_inc(hi_done, 1)

            def input_step(i):
                r = nrows(i)
                if i < TILES:
                    act.wait_ge(x_in[i % 2], 16 * (i // 2 + 1))
                    if i >= 2:
                        act.wait_ge(h_t, 2 * i - 2)
                        act.wait_ge(h_rs, i - 1)
                    act.activation(xn[0:r, i % 2, :], xt[0:r, i % 2, :], ACT.Square,
                                   accum_out=ss_x[0:r, i % 2, 0:1]).then_inc(h_ss, 1)
                if 1 <= i <= TILES:
                    input_hi(i - 1)

            for i in range(3):
                if i == 2:
                    for k in range(4):
                        split_hi(0, k)
                input_step(i)
            for k in range(4, KC):
                split_hi(0, k)
            act.wait_ge(setup, 2)
            act.activation(lam[:, 2:4], lam[:, 0:2], ACT.Exp).then_inc(setup, 1)

            def move(G, kind, i):
                t = ti(G, kind, i)
                act.wait_ge(t_ready, t + 1)
                src = bank(3 + t % 2).rearrange("p (c r) -> p c r", c=NC)
                if kind == "k":
                    act.activation(kT[:, :].rearrange("p (c s) -> p c s", c=NC)[:, :, i * P:(i + 1) * P], src, ACT.Copy).then_inc(t_moved, 1)
                    return
                if i == 0:
                    act.wait_ge(setup, 4)
                    if G:
                        act.wait_ge(o_out, 16 * 8 * (2 * G - 1))
                scale = qcol[:, (0 if G else 1):(0 if G else 1) + 1]
                if i < NT:
                    act.activation(qT[:, :].rearrange("p (c s) -> p c s", c=NC)[:, :, i * P:(i + 1) * P],
                                   src, ACT.Copy, scale=scale).then_inc(t_moved, 1)
                else:
                    act.activation(qTs[:, G, :, 0:NS],
                                   src[:, :, 0:NS], ACT.Copy, scale=scale).then_inc(t_moved, 1)

            def block_(u):
                kind, G = U[u][0], U[u][1]
                prefetch = u + 1 < len(U) and u + 1 != FIRST_GATE
                br = 1 if kind[-1] == "b" else 0
                for i in range(TILES):
                    n, r = TILES * u + i, nrows(i)
                    z = bank(n % 3)[0:r]
                    if u == 0:
                        input_step(i + 3)
                    elif i in COPY_AT and 3 * (u - 1) + COPY_AT.index(i) < N_COPIES:
                        copy_cache(3 * (u - 1) + COPY_AT.index(i))
                    if kind in "qk":
                        m = mi(G, kind, i)
                        act.wait_ge(z_ready, n + 1)
                        if m >= 2:
                            act.wait_ge(ss_ready, m - 1)
                        act.activation(bank(5 + m % 2)[0:r], z, ACT.Square).then_inc(sq_ready, 1)
                    if kind == "q" and i:
                        move(G, "q", i - 1)
                    if kind == "k" and i != 1:
                        move(G, "q", NT) if i == 0 else move(G, "k", i - 2)
                    if kind == "v" and i == 0:
                        move(G, "k", NT - 1)
                    if kind in ("ga", "gb"):
                        y = 9 * br + i
                        if y == TILES:
                            act.wait_ge(m_out, 16 * 18)
                        if y >= 2:
                            act.wait_ge(y_ready, y - 1)
                        if br:
                            act.wait_ge(og_in[y % 2], og_total(y))
                            act.activation(og[0:r, y % 2, 1, :], og[0:r, y % 2, 0, :], ACT.Square)\
                                .then_inc(osq, 1)
                        act.wait_ge(z_ready, n + 1)
                        act.activation(sg[0:r, y % 2, :], z, ACT.Sigmoid).then_inc(sg_ready, 1)
                        if i >= 2:
                            move_y(y - 2)
                    if kind in ("ma", "mb"):
                        idx = 18 * br + 9 * G + i
                        if i == 0 and G == 0:
                            move_y(9 * br + NT - 1)
                            move_y(9 * br + NT)
                        if i == 0 and G == 1:
                            act.wait_ge(m_out, 16 * (18 * br + 9))
                        act.wait_ge(z_ready, n + 1)
                        act.activation(sig[0:r, i, :], z, ACT.Sigmoid).then_inc(sig_ready, 1)
                    if kind == "out" and G == 0:
                        if i == 0:
                            m_hi_move(0)
                        if i + 1 < TILES:
                            m_hi_move(i + 1)
                    if prefetch and i < U[u + 1][4]:
                        split_hi(u + 1, i)

            def move_y(y):
                i = y % TILES
                act.wait_ge(y_t, y + 1)
                act.activation(yT_hi[:, :, i * P:i * P + nrows(i)],
                               bank(3 + y % 2).rearrange("p (c r) -> p c r", c=NC)[:, :, 0:nrows(i)],
                               ACT.Copy).then_inc(y_hi, 1)

            def m_hi_move(i):
                for half in range(2):
                    act.wait_ge(m_t, 2 * i + half + 1)
                    act.activation(hT_hi[:, 4 * half:4 * half + 4, i * P:i * P + nrows(i)],
                                   bank(3 + 2 * (i % 2) + half).rearrange("p (c r) -> p c r", c=4)[:, :, 0:nrows(i)],
                                   ACT.Copy).then_inc(m_hi, 1)

            def attention_b():
                act.sem_inc(be, 16)
                act.sem_inc(bm, 12)
                act.sem_inc(bo, 8)
                with act.Fori(0, 2) as I:
                    def piece_move(e):
                        for p, _, nb in pieces_of(e):
                            wait_reg(act, bt, 12 + 24 * I + p + 1)
                            wait_reg(act, bp, 12 + 24 * I + p - 3)
                            act.activation(ptB[:, p % 4, 0:nb * P], bank(4 + p % 2)[:, 0:nb * P],
                                           ACT.Copy).then_inc(bm, 1)

                    def out_move(e):
                        wait_reg(act, bp, 12 + 24 * I + pieces_before(e + 1))
                        act.activation(qT[:, ds((2 * I + e // 8) * SEQ + TILE_ORDER[e % 8] * P, P)],
                                       bank(6 + e % 2)[:, 0:P], ACT.Copy,
                                       scale=rlB[:, e // 8, e % 8, 0:1]).then_inc(bo, 1)

                    for s in range(16 + 5):
                        if s >= 5:
                            out_move(s - 5)
                        if 3 <= s < 19:
                            piece_move(s - 3)
                        if s < 16:
                            for mp in range(2):
                                wait_reg(act, bs, 16 + 32 * I + 2 * s + mp + 1)
                                sb = sB[s % 4][:, mp, 0:P * (TILE_ORDER[s % 8] + 1)]
                                n = 2 * (s % 8) + mp
                                act.activation(sb, sb, ACT.Exp, bias=st_sum[:, s // 8, 0, n:n + 1],
                                               scale=-1.0, accum_out=st_sum[:, s // 8, 1, n:n + 1])\
                                    .then_inc(be, 1)

            def attention_a(G):
                A = att[(3 * G + 2) % 2]
                base, tbase = 16 + 64 * (G - 1), 8 + 32 * (G - 1)
                if G == 1:
                    act.sem_inc(ae, 16)
                    act.sem_inc(ao, 8)
                with act.Fori(0, 2) as I:
                    for s in range(32 + A_VALUES + 1):
                        if s < 32:
                            wait_reg(act, as_, base + 32 * I + s + 1)
                            sb = A["sA"][:, s % 8, 0:width_a(G, s // 2 % 8)]
                            par, n = divmod(s, 16)
                            act.activation(sb, sb, ACT.Exp, bias=st_sum[:, par, 0, n:n + 1], scale=-1.0,
                                           accum_out=st_sum[:, par, 1, n:n + 1]).then_inc(ae, 1)
                        if s > A_VALUES and (s - A_VALUES) % 2 == 0:
                            e = (s - A_VALUES - 2) // 2
                            wait_reg(act, av, base + 32 * I + 2 * e + 2)
                            act.activation(qT[:, ds((2 * I + e // 8) * SEQ + e % 8 * P, P)],
                                           bank(6 + e % 2)[:, 0:P], ACT.Copy).then_inc(ao, 1)

            for G in range(4):
                for kind in range(3):
                    block_(3 * G + kind)
                attention_a(G) if G else attention_b()

            act.sem_inc(s_oc, 2)
            act.sem_inc(s_out, 32)
            act.sem_inc(s_kh, 29)
            act.wait_ge(s_const, 112)
            act.wait_ge(s_zero, 2)

            def queries_hi(b):
                for h in range(2):
                    src = qTs[h * HD:(h + 1) * HD, :, :, ds(b * DEC_T, DEC_T)]
                    for hi, q in spread((q_all[0], q_g1[0], q_g2[0]), h, src):
                        ins = act.activation(hi, q, ACT.Copy)
                ins.then_inc(s_qh, 1)

            queries_hi(0)
            with act.Fori(0, DEC_B) as b:
                def keys_hi(T):
                    wait_reg(act, s_kt, 29 * b + 29 + T + 1)
                    wait_reg(act, s_qk, 29 * b + 29 + before(3, T))
                    act.activation(kTs[0][:, T % 3, :, :],
                                   bank(x_bank_s(T)).rearrange("p (c r) -> p c r", c=NC), ACT.Copy)\
                        .then_inc(s_kh, 1)

                def values_hi(T):
                    s = T % NVS
                    wait_reg(act, sv_in[s], 16 * uses(NVS, T) * b + 16 * (T // NVS + 1))
                    wait_reg(act, s_pv, 29 * b + 29 + before(NVH, T))
                    act.activation(v_hi[:, T % NVH, :], v_in[:, s, :], ACT.Copy).then_inc(s_vh, 1)

                for T in range(NTS):
                    keys_hi(T)
                    if T == 5:
                        wait_reg(act, s_nt, b + 2)
                        act.activation(kTn[0][:, :, :], bank(5)[:, 384:512].rearrange("p (c r) -> p c r", c=16),
                                       ACT.Copy).then_inc(s_nh, 1)
                    if T in range(6, 12):
                        values_hi(T - 6)
                    if T == 15:
                        wait_reg(act, s_ta, 2 * b + 1)
                        act.activation(s_a[:, :], s_a[:, :], ACT.Exp, bias=sc_s[:, 0:1], scale=-1.0,
                                       accum_out=sc_s[:, 1:2]).then_inc(s_ea, 1)
                    if T == 19:
                        wait_reg(act, s_pa, b + 1)
                        wait_reg(act, s_va, b + 1)
                        for out, src in a_probs(0):
                            ins = act.activation(out, src, ACT.Copy)
                        ins.then_inc(s_ph, 1)
                    if T >= PV_FROM + 3:
                        values_hi(T - PV_FROM - 3 + NVH)
                for T in range(NTS - PV_FROM - 3 + NVH, 14):
                    values_hi(T)
                wait_reg(act, s_min, b + 1)
                act.activation(s_b, s_b, ACT.Exp, bias=sc_s[:, 8:9], scale=-1.0,
                               accum_out=sc_s[:, 9:10]).then_inc(s_eb, 1)
                values_hi(14)
                values_hi(15)
                wait_reg(act, s_vb, b + 1)
                for j in range(2):
                    wait_reg(act, s_pb, 2 * b + 2 + j + 1)
                    act.activation(pTb[:, 8 * j:8 * j + 8, 0:NS], bank(3 + j).rearrange("p (g q) -> p g q", g=8),
                                   ACT.Copy).then_inc(s_ph, 1)
                for T in range(16, 19):
                    values_hi(T)
                wait_reg(act, s_qk, 29 * b + 58)
                queries_hi(b + 1)
                for T in range(19, NTS):
                    values_hi(T)
                wait_reg(act, s_sel, 2 * b + 1)
                wait_reg(act, s_out, 32 * b + 32)
                act.activation(os_[:, 0, :], bank(7)[0:DEC_T], ACT.Copy).then_inc(s_oc, 1)
                wait_reg(act, s_oc, 2 * b + 3)
                act.dma_start(os_scr[0, ds(b * DEC_T, DEC_T), :], os_[:, 0, :]).then_inc(s_out, 16)
                wait_reg(act, s_sel, 2 * b + 2)
                act.activation(os_[:, 1, :], bank(5)[0:DEC_T], ACT.Copy).then_inc(s_oc, 1)
                wait_reg(act, s_oc, 2 * b + 4)
                act.dma_start(os_scr[1, ds(b * DEC_T, DEC_T), :], os_[:, 1, :]).then_inc(s_out, 16)

            for k in range(KC):
                split_hi(FIRST_GATE, k)
            act.wait_ge(ew_exp, 1)
            act.activation(ew[:, :, :, :], ew[:, :, :, :], ACT.Exp).then_inc(ew_exp, 1)
            for u in range(FIRST_GATE, len(U)):
                block_(u)

        @block.vector
        def _(dve):
            steps = [0]

            def link(ins):
                steps[0] += 1
                ins.then_inc(dve_step, 1)
                dve.wait_ge(dve_step, steps[0])

            def split_lo(u, k):
                q = first_chunk[u] + k
                dve.wait_ge(hi_done, q + 1)
                dve.tensor_tensor(w_lo[u % 2][:, k, :], raw[:, q % 4, :],
                                  w_hi[u % 2][:, k, :].bitcast(F32), ALU.subtract).then_inc(lo_done, 1)

            def rows_scale(i):
                r = nrows(i)
                dve.wait_ge(h_rs, i + 1)
                dve.tensor_scalar(xn[0:r, i % 2, :], xt[0:r, i % 2, :], rs_x[0:r, i % 2, 0:1], None, ALU.mult)\
                    .then_inc(h_xn, 1)

            def input_gain(i):
                r = nrows(i)
                for half in range(2):
                    j = 2 * i + half
                    dve.wait_ge(h_t, j + 1)
                    if i:
                        dve.wait_ge(h_lo, j - 1)
                    dve.tensor_tensor(hn[:, half, :].rearrange("p (k r) -> p k r", k=4)[:, :, 0:r],
                                      bank(x_bank(j)).rearrange("p (k r) -> p k r", k=4)[:, :, 0:r],
                                      gcol[:, 4 * half:4 * half + 4].unsqueeze(2).to_broadcast([P, 4, r]),
                                      ALU.mult).then_inc(h_hn, 1)

            dve.wait_ge(first_in, 32)

            def input_step(i):
                if i < TILES:
                    rows_scale(i)
                if 1 <= i <= TILES:
                    input_gain(i - 1)

            for i in range(3):
                if i == 2:
                    for k in range(4):
                        split_lo(0, k)
                input_step(i)
            for k in range(4, KC):
                split_lo(0, k)
            dve.wait_ge(const_in, N_CONST)
            for j in range(2):
                dve.tensor_tensor_reduce(out=lamv[:, 2 * j, :], in0=lamv[:, 2 * j, :], in1=lamv[:, 2 * j + 1, :],
                                         scale=1.0, scalar=0.0, op0=ALU.mult, op1=ALU.add,
                                         accum_out=lam[:, j:j + 1]).then_inc(setup, 1)
            dve.wait_ge(setup, 3)
            link(dve.tensor_tensor(lam[:, 4:5], lam[:, 3:4], lam[:, 2:3], ALU.subtract))
            link(dve.tensor_scalar(lam[:, 5:6], lam[:, 4:5], -LAM_INIT, None, ALU.add))
            link(dve.tensor_scalar(subrow[:, :], subrow[:, :], 1.0 - LAM_INIT, None, ALU.mult))
            link(dve.scalar_tensor_tensor(out=coef[:, 0:1], in0=coef[:, 1:2], scalar=lam[0:NS, 5:6],
                                          in1=coef[:, 0:1], op0=ALU.mult, op1=ALU.add))
            dve.tensor_scalar(qcol[:, :], qcol[:, :], -(HD ** -0.5), None, ALU.mult).then_inc(setup, 1)

            def block_(u):
                kind, G = U[u][0], U[u][1]
                br = 1 if kind[-1] == "b" else 0
                for i in range(TILES):
                    n, r = TILES * u + i, nrows(i)
                    z = bank(n % 3)[0:r]
                    if u == 0:
                        input_step(i + 3)
                    if kind in "qk":
                        m = mi(G, kind, i)
                        dve.wait_ge(sq_ready, m + 1)
                        dve.tensor_reduce(ss[0:r, m % 2, :],
                                          bank(5 + m % 2)[0:r].rearrange("p (h d) -> p h d", h=8),
                                          AX_X, ALU.add).then_inc(ss_ready, 1)
                        dve.wait_ge(rs_ready, m + 1)
                        if m >= 2:
                            G2, m2 = divmod(m - 2, 18)
                            if m2 < 9:
                                dve.wait_ge(t_ready, ti(G2, "q", m2) + 1)
                            else:
                                dve.wait_ge(kn_ready, TILES * G2 + m2 - 9 + 1)
                        dve.tensor_tensor(zn[0:r, m % 2, :].rearrange("p (h d) -> p h d", h=8),
                                          z.rearrange("p (h d) -> p h d", h=8),
                                          rs[0:r, m % 2, :].unsqueeze(2).to_broadcast([r, 8, HD]),
                                          ALU.mult).then_inc(zn_ready, 1)
                    if kind == "v":
                        dve.wait_ge(z_ready, n + 1)
                        if i == 0 and G:
                            dve.wait_ge(v_out, v_sent[G - 1])
                        dve.tensor_copy(v_sb[0:r, i, :], z).then_inc(v_ready, 1)
                    if kind in ("ga", "gb"):
                        y = 9 * br + i
                        s = y % 2
                        heads = 8 if br == 0 else 4
                        o = og[0:r, s, 0, :].rearrange("p (h d) -> p h d", h=heads)
                        dve.wait_ge(og_in[s], og_total(y))
                        if br == 0 and i < NT:
                            link(dve.tensor_tensor(o, o, ew[:, i, 0, :].unsqueeze(2).to_broadcast([P, 8, HD]),
                                                   ALU.mult))
                            dve.wait_ge(og_pool, i + 1)
                            link(dve.tensor_tensor(og[:, s, 0, :], og[:, s, 0, :], og[:, s, 1, :], ALU.add))
                        if br == 1:
                            dve.wait_ge(osq, i + 1)
                            dve.tensor_reduce(ss[0:r, i % 2, 0:4],
                                              og[0:r, s, 1, :].rearrange("p (h d) -> p h d", h=4),
                                              AX_X, ALU.add).then_inc(oss, 1)
                            dve.wait_ge(ors, i + 1)
                            dve.wait_ge(og_pool, NT + i + 1)
                            link(dve.tensor_tensor(o, og[0:r, s, 2, :].rearrange("p (h d) -> p h d", h=4),
                                                   rs[0:r, i % 2, 0:4].unsqueeze(2).to_broadcast([r, 4, P]),
                                                   ALU.mult))
                        dve.wait_ge(sg_ready, y + 1)
                        dve.tensor_tensor(sg[0:r, s, :], sg[0:r, s, :], z, ALU.mult).then_inc(silu_ready, 1)
                        if y >= 2:
                            dve.wait_ge(y_t, y - 1)
                        dve.wait_ge(silu_ready, y + 1)
                        dve.tensor_tensor(zy[0:r, s, :], og[0:r, s, 0, :], sg[0:r, s, :], ALU.mult)\
                            .then_inc(y_ready, 1)
                        if i >= 2:
                            y_low(y - 2)
                    if kind in ("ma", "mb") and i == 0 and G == 0:
                        y_low(9 * br + NT - 1)
                        y_low(9 * br + NT)
                    if kind in ("pa", "pb"):
                        idx = 18 * br + 9 * G + i
                        dve.wait_ge(z_ready, n + 1)
                        dve.wait_ge(sig_ready, idx + 1)
                        ins = dve.tensor_tensor(sig[0:r, i, :], sig[0:r, i, :], z, ALU.mult)
                        if br:
                            link(ins)
                            dve.wait_ge(ml_in[(9 * G + i) % 2], 16 * ((9 * G + i) // 2 + 1))
                            ins = dve.tensor_tensor(sig[0:r, i, :], sig[0:r, i, :],
                                                    zy[0:r, (9 * G + i) % 2, :], ALU.add)
                        ins.then_inc(m_ready, 1)
                    if kind == "out":
                        if G == 0:
                            if i == 0:
                                m_low(0)
                            if i + 1 < TILES:
                                m_low(i + 1)
                        idx = 9 * G + i
                        dve.wait_ge(z_ready, n + 1)
                        dve.wait_ge(xl_in[idx % 2], 16 * (idx // 2 + 1))
                        if idx >= 3:
                            dve.wait_ge(yo_out[idx % 3], 16 * (idx // 3))
                        dve.tensor_tensor(yo[0:r, idx % 3, :], z, xl[0:r, idx % 2, :], ALU.add)\
                            .then_inc(yo_ready, 1)

            def y_low(y):
                i = y % TILES
                dve.wait_ge(y_hi, y + 1)
                dve.tensor_tensor(yT_lo[:, :, i * P:i * P + nrows(i)],
                                  bank(3 + y % 2).rearrange("p (c r) -> p c r", c=NC)[:, :, 0:nrows(i)],
                                  yT_hi[:, :, i * P:i * P + nrows(i)].bitcast(F32), ALU.subtract)\
                    .then_inc(y_lo, 1)

            def m_low(i):
                for half in range(2):
                    dve.wait_ge(m_hi, 2 * i + half + 1)
                    cols = slice(i * P, i * P + nrows(i))
                    dve.tensor_tensor(
                        hT_lo[:, 4 * half:4 * half + 4, cols],
                        bank(3 + 2 * (i % 2) + half).rearrange("p (c r) -> p c r", c=4)[:, :, 0:nrows(i)],
                        hT_hi[:, 4 * half:4 * half + 4, cols].bitcast(F32), ALU.subtract).then_inc(m_lo, 1)

            def attention_b():
                dve.sem_inc(bs, 16)
                dve.sem_inc(ba, 8)
                with dve.Fori(0, 2) as I:
                    def biased(e, mp):
                        W = P * (TILE_ORDER[e % 8] + 1)
                        n = 2 * (e % 8) + mp
                        wait_reg(dve, bq, 16 + 32 * I + 2 * e + mp + 1)
                        if mp:
                            wait_reg(dve, ba, 8 + 16 * I + e - 3)
                        else:
                            wait_reg(dve, bt, 12 + 24 * I + pieces_before(e - 3))
                        dve.tensor_tensor_reduce(
                            out=sB[e % 4][:, mp, 0:W], in0=ps[:, mp * 1024:mp * 1024 + W],
                            in1=tB[:, e // 8, SEQ - W:SEQ], scale=1.0, scalar=3e38,
                            op0=ALU.add, op1=ALU.min, accum_out=st_sum[:, e // 8, 0, n:n + 1]).then_inc(bs, 1)

                    def combined(e):
                        par, i = e // 8, e % 8
                        W = P * (TILE_ORDER[i] + 1)
                        wait_reg(dve, be, 16 + 32 * I + 2 * e + 2)
                        dve.reciprocal(rlB[:, par, i, :], st_sum[:, par, 1, 2 * i:2 * i + 2]).then_inc(bw, 1)
                        wait_reg(dve, bw, 32 * I + 2 * e + 1)
                        dve.scalar_tensor_tensor(out=wB[:, par, i:i + 1], in0=rlB[:, par, i, 1:2],
                                                 scalar=st_sum[:, par, 1, 2 * i:2 * i + 1],
                                                 in1=lam[:, 5:6], op0=ALU.mult, op1=ALU.mult).then_inc(bw, 1)
                        wait_reg(dve, bw, 32 * I + 2 * e + 2)
                        p1, p2 = sB[e % 4][:, 0, 0:W], sB[e % 4][:, 1, 0:W]
                        dve.scalar_tensor_tensor(out=p1, in0=p2, scalar=wB[:, par, i:i + 1], in1=p1,
                                                 op0=ALU.mult, op1=ALU.add).then_inc(ba, 1)

                    for s in range(16 + 1):
                        if s in (0, 8):
                            wait_reg(dve, btab2 if s else btab, 16 * I + 16)
                        if s < 16:
                            biased(s, 0)
                        if s:
                            combined(s - 1)
                        if s < 16:
                            biased(s, 1)

            def attention_a(G):
                A = att[(3 * G + 2) % 2]
                base = 16 + 64 * (G - 1)
                if G == 1:
                    dve.sem_inc(as_, 16)
                    dve.sem_inc(am, 16)
                else:
                    dve.wait_ge(o_out, 16 * 8 * (2 * G - 1))
                with dve.Fori(0, 2) as I:
                    def keep_stats(par):
                        wait_reg(dve, ae, base + 32 * I + 16 * par + 16)
                        c2 = (2 * I + par) * 2
                        for j in range(2):
                            ins = dve.tensor_copy(st[:, :, ds(c2 + 8 * j, 2)],
                                                  st_sum[:, par, j, :].rearrange("p (i h) -> p i h", h=2))
                        ins.then_inc(ast, 1)

                    for s in range(32 + A_TURN):
                        if s in (0, 16):
                            wait_reg(dve, atab2 if s else atab, 16 * I + 16 + 32 * (G - 1))
                        if s < 32:
                            par, n = divmod(s, 16)
                            W = width_a(G, n // 2)
                            N = base + 32 * I + s
                            wait_reg(dve, aq, N + 1)
                            dve.tensor_tensor_reduce(
                                out=A["sA"][:, s % 8, 0:W], in0=bank(s % 4)[:, 0:W],
                                in1=A["tA"][:, par, s % 2, 256 - W:256], scale=1.0, scalar=3e38,
                                op0=ALU.add, op1=ALU.min, accum_out=st_sum[:, par, 0, n:n + 1]).then_inc(as_, 1)
                        if s >= A_TURN:
                            n = s - A_TURN
                            N = base + 32 * I + n
                            W = width_a(G, n // 2 % 8)
                            wait_reg(dve, atp, N + 1)
                            if n % 4 == 0:
                                wait_reg(dve, av, N - 4)
                            dve.tensor_copy(A["ptA"][:, n % 8, 0:W], bank(4 + n % 2)[:, 0:W]).then_inc(am, 1)
                        if s == 19:
                            keep_stats(0)
                    keep_stats(1)

            for G in range(4):
                for kind in range(3):
                    block_(3 * G + kind)
                attention_a(G) if G else attention_b()

            dve.sem_inc(s_pbm, 2)
            dve.sem_inc(s_om, 2)
            dve.sem_inc(s_km, 29)
            dve.sem_inc(s_scale, 2)
            dve.wait_ge(o_out, 16 * 8 * 7)
            for t in (q_g1[0], q_g2[0], q_g1[1], q_g2[1]):
                link(dve.memset(t[:, :, :, :].bitcast(F32), 0.0))
            link(dve.memset(pT1[:, :, :].bitcast(F32), 0.0))
            link(dve.memset(pT2[:, :, :].bitcast(F32), 0.0))
            dve.sem_inc(s_zero, 1)
            dve.wait_ge(s_const, 112)
            dve.wait_ge(s_zero, 2)
            with dve.Fori(0, DEC_B) as b:
                def biased(out, in_, table, acc):
                    return dve.tensor_tensor_reduce(out=out, in0=in_, in1=table, scale=1.0, scalar=3e38,
                                                    op0=ALU.add, op1=ALU.min, accum_out=acc)

                def biased_b(q):
                    wait_reg(dve, s_qk, 29 * b + 29 + 13 + 4 * (q + 1))
                    biased(s_b[:, q * CW:(q + 1) * CW], bank(3 + q % 2)[0:NS], bias_sb[:, q * CW:(q + 1) * CW],
                           sc_s[:, 3 + q:4 + q]).then_inc(s_tb, 1)

                def values_lo(T):
                    s = T % NVS
                    wait_reg(dve, s_vh, 29 * b + T + 1)
                    dve.tensor_tensor(v_lo[:, s, :], v_in[:, s, :],
                                      v_hi[:, T % NVH, :].bitcast(F32), ALU.subtract).then_inc(s_vld, 1)

                def scale_moved(j):
                    wait_reg(dve, s_twice, 2 * b + j + 1)
                    dve.tensor_copy(scale2[:, j:j + 1], bank(2)[:, SCALE_AT + j:SCALE_AT + j + 1])\
                        .then_inc(s_scale, 1)

                for T in range(NTS):
                    wait_reg(dve, s_kh, 29 * b + 29 + T + 1)
                    dve.tensor_tensor(kTs[1][:, T % 3, :, :],
                                      bank(x_bank_s(T)).rearrange("p (c r) -> p c r", c=NC),
                                      kTs[0][:, T % 3, :, :].bitcast(F32), ALU.subtract).then_inc(s_km, 1)
                    if T == 5:
                        wait_reg(dve, s_nh, b + 1)
                        dve.tensor_tensor(kTn[1][:, :, :], bank(5)[:, 384:512].rearrange("p (c r) -> p c r", c=16),
                                          kTn[0][:, :, :].bitcast(F32), ALU.subtract).then_inc(s_nm, 1)
                    if T == 14:
                        wait_reg(dve, s_qk, 29 * b + 29 + 13)
                        biased(s_a[:, :], bank(2)[0:NS, 0:NEW_A], bias_sa[:, :], sc_s[:, 0:1]).then_inc(s_ta, 1)
                        wait_reg(dve, s_pb, 2 * b + 2)
                        biased(s_b[:, PAST:KEYS_B], bank(2)[0:NS, NEW_A:NEW_A + DEC_T], bias_sb[:, PAST:KEYS_B],
                               sc_s[:, 2:3]).then_inc(s_ta, 1)
                    if T == 18:
                        wait_reg(dve, s_ea, b + 1)
                        dve.reciprocal(sc_s[:, 10:11], sc_s[:, 1:2]).then_inc(s_rec, 1)
                    if T == 19:
                        wait_reg(dve, s_ph, 3 * b + 1)
                        for (lo, src), (hi, _) in zip(a_probs(1), a_probs(0)):
                            dve.tensor_tensor(lo, src, hi.bitcast(F32), ALU.subtract)
                        dve.tensor_copy(pTn[:, 0:3, :], bank(5)[0:DEC_T, 192:384].rearrange("p (g q) -> p g q", g=3))\
                            .then_inc(s_pam, 1)
                    if T == 20:
                        biased_b(0)
                    if T == 24:
                        biased_b(1)
                    if T == 25:
                        scale_moved(0)
                    if T == 28:
                        biased_b(2)
                biased_b(3)
                wait_reg(dve, s_tb, 4 * b + 4)
                dve.tensor_reduce(sc_s[:, 8:9], sc_s[:, 2:7], AX_X, ALU.min).then_inc(s_min, 1)
                values_lo(14)
                wait_reg(dve, s_vb, b + 1)
                for j in range(2):
                    wait_reg(dve, s_ph, 3 * b + j + 2)
                    if j:
                        dve.tensor_copy(pTn[:, 3, :], bank(5)[0:DEC_T, 0:NS])
                    dve.tensor_tensor(pTb[:, 8 * j:8 * j + 8, NS:2 * NS],
                                      bank(3 + j).rearrange("p (g q) -> p g q", g=8),
                                      pTb[:, 8 * j:8 * j + 8, 0:NS].bitcast(F32), ALU.subtract).then_inc(s_pbm, 1)
                values_lo(16)
                wait_reg(dve, s_eb, b + 1)
                dve.reciprocal(sc_s[:, 11:12], sc_s[:, 9:10]).then_inc(s_rec, 1)
                wait_reg(dve, s_rec, 3 * b + 2)
                dve.tensor_scalar(sc_s[:, 12:13], sc_s[:, 11:12], coef[:, 0:1], None, ALU.mult).then_inc(s_rec, 1)
                values_lo(18)
                wait_reg(dve, s_va, b + 2)
                wait_reg(dve, s_scale, 2 * b + 3)
                dve.scalar_tensor_tensor(out=om[:, 0, :], in0=bank(7), scalar=scale2[:, 0:1],
                                         in1=mask[:, 0, :], op0=ALU.mult, op1=ALU.mult).then_inc(s_om, 1)
                for T in range(20, 26, 2):
                    values_lo(T)
                scale_moved(1)
                for T in range(26, NTS, 2):
                    values_lo(T)
                wait_reg(dve, s_vb, b + 2)
                wait_reg(dve, s_scale, 2 * b + 4)
                dve.scalar_tensor_tensor(out=om[:, 1, :], in0=bank(6), scalar=scale2[:, 1:2],
                                         in1=mask[:, 1, :], op0=ALU.mult, op1=ALU.mult).then_inc(s_om, 1)

            dve.wait_ge(lo_done, first_chunk[FIRST_GATE])
            for k in range(KC):
                split_lo(FIRST_GATE, k)

            dve.wait_ge(st_in, 48)

            def nm(g):
                return stc[:, :, g, 0:8]

            link(dve.tensor_tensor(nmin[:, :, :], nm(0), nm(1), ALU.min))
            link(dve.tensor_tensor(nmin[:, :, :], nmin[:, :, :], nm(2), ALU.min))
            for g in range(3):
                link(dve.tensor_tensor(ew[:, :, g, :], nmin[:, :, :], nm(g), ALU.subtract))
            dve.sem_inc(ew_exp, 1)
            dve.wait_ge(ew_exp, 2)
            for g in range(3):
                link(dve.tensor_tensor(el[:, :, g, :], ew[:, :, g, :], stc[:, :, g, 8:16], ALU.mult))
            link(dve.tensor_tensor(den[:, :, :], el[:, :, 0, :], el[:, :, 1, :], ALU.add))
            link(dve.tensor_tensor(den[:, :, :], den[:, :, :], el[:, :, 2, :], ALU.add))
            link(dve.reciprocal(den[:, :, :], den[:, :, :]))
            for g in range(3):
                link(dve.tensor_tensor(ew[:, :, g, :], ew[:, :, g, :], den[:, :, :], ALU.mult))
            dve.sem_inc(ew_ready, 1)
            for u in range(FIRST_GATE, len(U)):
                block_(u)

        @block.tensor
        def _(pe):
            pe.wait_ge(first_in, 32)

            def turn_x(i, half):
                r, j = nrows(i), 2 * i + half
                pe.wait_ge(h_xn, i + 1)
                if j >= 4:
                    pe.wait_ge(h_hn, j)
                for k in range(4):
                    c = 4 * half + k
                    ins = pe.transpose(bank(x_bank(j))[:, k * P:k * P + r],
                                       xn[0:r, i % 2, c * P:(c + 1) * P], ident[0:r, 0:r])
                ins.then_inc(h_t, 1)

            for i in range(2):
                for half in range(2):
                    turn_x(i, half)

            def turn(G, kind, i):
                t, r = ti(G, kind, i), nrows(i)
                if kind == "q":
                    pe.wait_ge(zn_ready, mi(G, "q", i) + 1)
                    src = zn[0:r, mi(G, "q", i) % 2, :]
                else:
                    kk = TILES * G + i
                    pe.wait_ge(kn_ready, kk + 1)
                    src = kn[0:r, kk % 3, :]
                if t >= 2:
                    pe.wait_ge(t_moved, t - 1)
                for c in range(NC):
                    ins = pe.transpose(bank(3 + t % 2)[:, c * P:c * P + r], src[:, c * P:(c + 1) * P],
                                       ident[0:r, 0:r])
                ins.then_inc(t_ready, 1)

            def turn_y(y):
                r = nrows(y % TILES)
                pe.wait_ge(y_ready, y + 1)
                if y >= 2:
                    pe.wait_ge(y_lo, y - 1)
                for c in range(NC):
                    ins = pe.transpose(bank(3 + y % 2)[:, c * P:c * P + r], zy[0:r, y % 2, c * P:(c + 1) * P],
                                       ident[0:r, 0:r])
                ins.then_inc(y_t, 1)

            def turn_m(i):
                r = nrows(i)
                pe.wait_ge(mt_in[i % 2], 16 * (i // 2 + 1))
                for half in range(2):
                    if i >= 2:
                        pe.wait_ge(m_lo, 2 * (i - 2) + half + 1)
                    for k in range(4):
                        c = 4 * half + k
                        ins = pe.transpose(bank(3 + 2 * (i % 2) + half)[:, k * P:k * P + r],
                                           mt[0:r, i % 2, c * P:(c + 1) * P], ident[0:r, 0:r])
                    ins.then_inc(m_t, 1)

            def block_(u):
                kind, G, _, _, K = U[u]
                br = 1 if kind[-1] == "b" else 0
                order = G if kind in "qkv" else 0
                hi, lo = (yT_hi, yT_lo) if kind in ("pa", "pb") else (hT_hi, hT_lo)
                if kind == "out" and G == 0:
                    turn_m(0)
                    turn_m(1)
                for i in range(TILES):
                    n, r = TILES * u + i, nrows(i)
                    if n == 0:
                        pe.wait_ge(h_hn, 4)
                    if u < 3:
                        pe.wait_ge(h_lo, 2 * i + 2)
                    if kind in ("pa", "pb"):
                        pe.wait_ge(y_lo, 9 * br + i + 1)
                    if kind == "out":
                        pe.wait_ge(m_lo, 2 * i + 2)
                    if n >= 3:
                        pe.wait_ge(*z_freed(n - 3))
                    z = bank(n % 3)[0:r]
                    for k in range(K):
                        if i == 0:
                            pe.wait_ge(lo_done, first_chunk[u] + k + 1)
                        sh, sl = hT_of(hi, order, k, i), hT_of(lo, order, k, i)
                        pe.matmul(z, sh, w_hi[u % 2][:, k, :], start=(k == 0), stop=False)
                        pe.matmul(z, sh, w_lo[u % 2][:, k, :], start=False, stop=False)
                        if u == 0 and k in (1, 5) and i + 2 < TILES:
                            turn_x(i + 2, k // 4)
                        ins = pe.matmul(z, sl, w_hi[u % 2][:, k, :], start=False, stop=(k == K - 1))
                    ins.then_inc(z_ready, 1)
                    if kind == "q" and i:
                        turn(G, "q", i - 1)
                    if kind == "k" and i != 1:
                        turn(G, "q", NT) if i == 0 else turn(G, "k", i - 2)
                    if kind == "v" and i == 0:
                        turn(G, "k", NT - 1)
                    if kind in ("ga", "gb") and i >= 2:
                        turn_y(9 * br + i - 2)
                    if kind == "out" and G == 0 and i + 2 < TILES:
                        turn_m(i + 2)
                if kind in ("ga", "gb"):
                    turn_y(9 * br + NT - 1)
                    turn_y(9 * br + NT)

            def attention_b():
                pe.sem_inc(bq, 16)
                pe.sem_inc(bt, 12)
                pe.sem_inc(bp, 12)
                with pe.Fori(0, 2) as I:
                    def scores(e, mp):
                        h, s = 2 * I + e // 8, TILE_ORDER[e % 8]
                        W, N = P * (s + 1), 16 + 32 * I + 2 * e + mp
                        if mp == 0:
                            wait_reg(pe, qz_ready, 16 * I + e + 1)
                        wait_reg(pe, bs, N - 1)
                        for w0 in range(0, W, CW):
                            w = min(CW, W - w0)
                            ins = pe.matmul(ps[:, mp * 1024 + w0:mp * 1024 + w0 + w],
                                            qz[:, mp, s * P:(s + 1) * P], kT[:, ds(h * SEQ + w0, w)],
                                            start=True, stop=True)
                        ins.then_inc(bq, 1)

                    def probs_turn(e):
                        wait_reg(pe, ba, 8 + 16 * I + e + 1)
                        for p, j0, nb in pieces_of(e):
                            wait_reg(pe, bm, 12 + 24 * I + p - 1)
                            for j in range(nb):
                                ins = pe.transpose(bank(4 + p % 2)[:, j * P:(j + 1) * P],
                                                   sB[e % 4][:, 0, (j0 + j) * P:(j0 + j + 1) * P], ident[:, :])
                            ins.then_inc(bt, 1)

                    def values(e, half):
                        h = 2 * I + e // 8
                        if half == 0:
                            wait_reg(pe, bo, 8 + 16 * I + e - 1)
                        for p, j0, nb in pieces_of(e)[half:half + 1]:
                            wait_reg(pe, bm, 12 + 24 * I + p + 1)
                            for j in range(nb):
                                ins = pe.matmul(bank(6 + e % 2)[:, 0:P], ptB[:, p % 4, j * P:(j + 1) * P],
                                                v_sb[:, j0 + j, ds(h * P, P)], start=(j0 + j == 0),
                                                stop=(j0 + j == TILE_ORDER[e % 8]))
                            ins.then_inc(bp, 1)

                    for s in range(16 + 4):
                        if 3 <= s < 19:
                            probs_turn(s - 3)
                        for half in range(2):
                            if s < 16:
                                scores(s, half)
                            if s >= 4:
                                values(s - 4, half)

            def attention_a(G):
                A = att[(3 * G + 2) % 2]
                base, tbase = 16 + 64 * (G - 1), 8 + 32 * (G - 1)
                if G == 1:
                    for s in (aq, atp, av):
                        pe.sem_inc(s, 16)
                with pe.Fori(0, 2) as I:
                    for s in range(32 + A_VALUES):
                        if s < 32:
                            c, (i, hh) = 2 * I + s // 16, divmod(s % 16, 2)
                            W = width_a(G, i)
                            if hh == 0:
                                wait_reg(pe, qz_ready, 32 * G + 16 * I + s // 2 + 1)
                            wait_reg(pe, as_, base + 32 * I + s - 3)
                            pe.matmul(bank(s % 4)[:, 0:W], qz[:, hh, i * P:(i + 1) * P],
                                      kT[:, ds(c * SEQ + (i + 1) * P - W, W)],
                                      start=True, stop=True).then_inc(aq, 1)
                        if A_TURN <= s < 32 + A_TURN:
                            n = s - A_TURN
                            wait_reg(pe, ae, base + 32 * I + n + 1)
                            wait_reg(pe, am, base + 32 * I + n - 1)
                            for j in range(width_a(G, n // 2 % 8) // P):
                                ins = pe.transpose(bank(4 + n % 2)[:, j * P:(j + 1) * P],
                                                   A["sA"][:, n % 8, j * P:(j + 1) * P], ident[:, :])
                            ins.then_inc(atp, 1)
                        if s >= A_VALUES:
                            n = s - A_VALUES
                            e, hh = divmod(n, 2)
                            c, i = 2 * I + e // 8, e % 8
                            nb = width_a(G, i) // P
                            wait_reg(pe, am, base + 32 * I + n + 1)
                            if hh == 0:
                                wait_reg(pe, ao, tbase + 16 * I + e - 1)
                            for j in range(nb):
                                ins = pe.matmul(bank(6 + e % 2)[:, hh * HD:(hh + 1) * HD],
                                                A["ptA"][:, n % 8, j * P:(j + 1) * P],
                                                v_sb[:, i + 1 - nb + j, ds(c * P + hh * HD, HD)],
                                                start=(j == 0), stop=(j == nb - 1))
                            ins.then_inc(av, 1)

            for G in range(4):
                for kind in range(3):
                    block_(3 * G + kind)
                pe.wait_ge(v_ready, 9 * G + 9)
                pe.wait_ge(t_moved, 17 * G + 17)
                attention_a(G) if G else attention_b()

            for s, c in ((s_kt, 29), (s_qk, 29), (s_pv, 29), (s_va, 1), (s_vb, 1), (s_pb, 2), (s_nt, 1)):
                pe.sem_inc(s, c)
            with pe.Fori(0, DEC_B) as b:
                def keys_turn(T):
                    wait_reg(pe, sk_in[T % NKS], 16 * uses(NKS, T) * b + 16 * (T // NKS + 1))
                    wait_reg(pe, s_km, 29 * b + 29 + before(3, T))
                    if T == 2:
                        wait_reg(pe, s_om, 2 * b + 2)
                    for c in range(NC):
                        ins = pe.transpose(bank(x_bank_s(T))[:, c * P:(c + 1) * P],
                                           k_in[:, T % NKS, c * P:(c + 1) * P], ident[:, :])
                    ins.then_inc(s_kt, 1)

                def product(out, q, index, kh, kl, first, last):
                    qh, ql = q[0][index], q[1][index]
                    pe.matmul(out, qh, kh, start=first, stop=False, skip_group_check=True)
                    pe.matmul(out, qh, kl, start=False, stop=False, skip_group_check=True)
                    return pe.matmul(out, ql, kh, start=False, stop=last, skip_group_check=True)

                def score(T):
                    wait_reg(pe, s_km, 29 * b + 29 + T + 1)
                    if T < 13:
                        if T == 0:
                            q, at_, g = q_all, 1, 0
                        elif T < 5:
                            q, at_, g = q_g1, T - 1, 1
                        else:
                            q, at_, g = q_g2, T - 5, 2
                        col = g * (P + DEC_T)
                        out = bank(2)[0:NS, col:col + P]
                        first = T == 0
                    else:
                        j = T - 13
                        q, at_ = q_all, 0
                        out = bank(3 + (j // 4) % 2)[0:NS, (j % 4) * P:(j % 4 + 1) * P]
                        first = j % 4 == 0
                        if j in (0, 4):
                            wait_reg(pe, s_pbm, 2 * b + 2)
                        if j in (8, 12):
                            wait_reg(pe, s_tb, 4 * b + (1 if j == 8 else 2))
                    for c in range(NC):
                        ins = product(out, q, (slice(None), at_, c), kTs[0][:, T % 3, c, :], kTs[1][:, T % 3, c, :],
                                      first and c == 0, c == NC - 1)
                    ins.then_inc(s_qk, 1)

                def new_turn():
                    wait_reg(pe, sn_in, 64 * b + 64)
                    wait_reg(pe, s_pbm, 2 * b + 2)
                    wait_reg(pe, s_oc, 2 * b + 2)
                    for g in range(4):
                        for c in range(NC):
                            j = 4 * g + c
                            ins = pe.transpose(bank(5)[:, 384 + 8 * j:392 + 8 * j],
                                               kv_new[:, 0, g, c * P:(c + 1) * P],
                                               ident[NEW_AT:NEW_AT + DEC_T, NEW_AT:NEW_AT + DEC_T])
                    ins.then_inc(s_nt, 1)

                def new_score():
                    wait_reg(pe, s_nm, b + 1)
                    for g in range(4):
                        G = (g + 1) % 4
                        col = g * (P + DEC_T) + P if g < 3 else NEW_A
                        for c in range(NC):
                            product(bank(2)[0:NS, col:col + DEC_T], q_all, (slice(None), G, c),
                                    kTn[0][:, 4 * g + c, :], kTn[1][:, 4 * g + c, :], False, c == NC - 1)

                def value(T, out, pt):
                    s, per, k = lo_of(T)
                    wait_reg(pe, s, per * b + k + 1)
                    start = T in (0, 13)
                    pe.matmul(out, pt, v_hi[:, T % NVH, :], start=start, stop=False, skip_group_check=True)
                    pe.matmul(out[0:NS], pt[:, 0:NS], v_lo[:, T % NVS, :], start=False, stop=False,
                              skip_group_check=True).then_inc(s_pv, 1)

                def value_a(T):
                    value(T, bank(7), pT0[:, :] if T == 0 else (pT1[:, T - 1, :] if T < 5 else pT2[:, T - 5, :]))

                def twice_(j):
                    wait_reg(pe, s_scale, 2 * b + 2)
                    pe.matmul(bank(2)[:, SCALE_AT + j:SCALE_AT + j + 1], twice[:, :],
                              sc_s[:, 10 + 2 * j:11 + 2 * j], start=True, stop=True).then_inc(s_twice, 1)

                keys_turn(0)
                keys_turn(1)
                wait_reg(pe, sq_b, 2 * b + 2)
                wait_reg(pe, s_scale, 2 * b + 2)
                for T in range(NTS):
                    if T + 2 < NTS:
                        keys_turn(T + 2)
                    score(T)
                    if T == 3:
                        new_turn()
                    if T == 6:
                        new_score()
                    if T == 16:
                        wait_reg(pe, s_ea, b + 1)
                        for g in range(3):
                            col = g * (P + DEC_T)
                            pe.transpose(bank(5)[:, g * NS:(g + 1) * NS], s_a[:, col:col + P], ident[0:NS, 0:NS])
                            ins = pe.transpose(bank(5)[0:DEC_T, 192 + g * NS:192 + (g + 1) * NS],
                                               s_a[:, col + P:col + P + DEC_T], ident[0:NS, 0:NS])
                        ins.then_inc(s_pa, 1)
                    if T == 19:
                        wait_reg(pe, s_rec, 3 * b + 1)
                        twice_(0)
                    if T == PV_FROM:
                        wait_reg(pe, s_pam, b + 1)
                        wait_reg(pe, s_oc, 2 * b + 1)
                    if T in range(PV_FROM, PV_FROM + PV_EARLY):
                        value_a(T - PV_FROM)
                for T in range(PV_EARLY, 13):
                    value_a(T)
                wait_reg(pe, svn_in, 64 * b + 64)
                for g in range(3):
                    ins = pe.matmul(bank(7)[0:NS], pTn[:, g, :], kv_new[:, 1, g, :], start=False, stop=(g == 2),
                                    skip_group_check=True)
                ins.then_inc(s_va, 1)
                wait_reg(pe, s_eb, b + 1)
                for j in range(2):
                    for p in range(8):
                        pg = 8 * j + p
                        ins = pe.transpose(bank(3 + j)[:, p * NS:(p + 1) * NS], s_b[:, pg * P:(pg + 1) * P],
                                           ident[0:NS, 0:NS])
                    if j == 1:
                        ins = pe.transpose(bank(5)[0:DEC_T, 0:NS], s_b[:, PAST:KEYS_B], ident[0:NS, 0:NS])
                    ins.then_inc(s_pb, 1)
                for pg in range(N_PAGES):
                    if pg % 8 == 0:
                        wait_reg(pe, s_pbm, 2 * b + 2 + pg // 8 + 1)
                    value(13 + pg, bank(6), pTb[:, pg, :])
                    if pg == 7:
                        wait_reg(pe, s_om, 2 * b + 2 + 1)
                        pe.matmul(bank(7)[0:DEC_T], sel[:, :], om[:, 0, :], start=True, stop=True).then_inc(s_sel, 1)
                    if pg == 9:
                        wait_reg(pe, s_rec, 3 * b + 3)
                        twice_(1)
                pe.matmul(bank(6)[0:NS], pTn[:, 3, :], kv_new[:, 1, 3, :], start=False, stop=True,
                          skip_group_check=True).then_inc(s_vb, 1)
                wait_reg(pe, s_om, 2 * b + 2 + 2)
                pe.matmul(bank(5)[0:DEC_T], sel[:, :], om[:, 1, :], start=True, stop=True).then_inc(s_sel, 1)

            for u in range(FIRST_GATE, len(U)):
                block_(u)


def shape_constants():
    f = np.float32
    slopes_a = (2.0 ** (-8.0 * np.arange(1, 25) / 24)).astype(f).reshape(3, A_HEADS)
    slopes_b = (2.0 ** (-8.0 * np.arange(1, B_HEADS + 1) / B_HEADS)).astype(f)
    p = np.arange(P)[:, None]
    x = np.arange(2 * P)[None, :]
    bias_a = np.full((3, A_HEADS, P, 2 * P), MASKED, f)
    steps = p + P - x
    for g in range(2):
        ok = (steps >= 0) & (steps <= P)
        for h in range(A_HEADS):
            bias_a[g, h] = np.where(ok, slopes_a[g, h] * (steps * WINDOWS[g][1]).astype(f), f(MASKED))
    ok = (steps >= 0) & (steps % 2 == 0) & (x >= P)
    for h in range(A_HEADS):
        bias_a[2, h] = np.where(ok, slopes_a[2, h] * (steps * 8).astype(f), f(MASKED))
    dist = p - (np.arange(SEQ)[None, :] - (SEQ - P))
    bias_b = np.stack([np.where(dist >= 0, s * dist.astype(f), f(MASKED)) for s in slopes_b]).astype(f)
    c, t, hh = (a.reshape(-1) for a in np.meshgrid(np.arange(NC), np.arange(DEC_T), np.arange(2), indexing="ij"))
    bias_sa = np.full((NS, NEW_A), MASKED, f)
    bias_sb = np.full((NS, KEYS_B), MASKED, f)
    m = np.arange(P)[None, :]
    j = np.arange(DEC_T)[None, :]
    for g, (win, dil) in enumerate(WINDOWS):
        n = win // dil
        s = n + (t[:, None] // dil if dil < DEC_T else 0 * t[:, None]) - m
        slope = slopes_a[g][2 * c + hh][:, None]
        col = g * (P + DEC_T)
        bias_sa[:, col:col + P] = np.where(s <= n, slope * (s * dil).astype(f), f(MASKED))
        back = t[:, None] - j
        bias_sa[:, col + P:col + P + DEC_T] = np.where((back >= 0) & (back % dil == 0) & (back <= win),
                                                       slope * back.astype(f), f(MASKED))
    back = PAST + t[:, None] - np.arange(KEYS_B)[None, :]
    bias_sb[:] = np.where(back >= 0, slopes_b[c][:, None] * back.astype(f), f(MASKED))
    e = np.arange(CW)[None, :]
    mask = np.stack([e // HD == (2 * c + hh)[:, None], e // P == c[:, None]]).astype(f)
    sel = (t[:, None] == j).astype(f)
    coef = np.stack([hh == 0, hh == 1], axis=1).astype(f)
    return dict(ident=np.eye(P, dtype=f), bias_a=bias_a, bias_b=bias_b, bias_sa=bias_sa, bias_sb=bias_sb,
                mask=mask, sel=sel, coef=coef)


_INS = ["x_prompt", "x_sample", "cache_a0_kv", "cache_a1_kv", "cache_a2_kv", "cache_b_kv", "page_table", "norm_g",
        "w_in", "q_norm_a", "k_norm_a", "q_norm_b", "k_norm_b", "lambda_q1", "lambda_k1", "lambda_q2",
        "lambda_k2", "subln_g", "w_proj_a", "w_proj_b", "w_out"]
_OUTS = [(1, SEQ, D_MODEL), (DEC_B, DEC_T, D_MODEL),
         (1, 1, 128, 2, A_HEADS, HD), (1, 1, 512, 2, A_HEADS, HD), (1, 1, 1024, 2, A_HEADS, HD),
         (1, 1, SEQ, 2, B_HEADS, P),
         (1, DEC_B, 128, 2, A_HEADS, HD), (1, DEC_B, 512, 2, A_HEADS, HD), (1, DEC_B, 2048, 2, A_HEADS, HD),
         (1, DEC_B, DEC_T, 2, B_HEADS, P)]


def kernel(**inputs):
    import concourse.bacc as bacc
    from concourse.bass_utils import run_bass_kernel_spmd

    nc = bacc.Bacc("TRN2", target_bir_lowering=False, num_devices=1)
    arrays, aps = {}, {}
    for name, a in [(n, inputs[n]) for n in _INS] + list(shape_constants().items()):
        a = np.ascontiguousarray(a)
        arrays[f"in_{name}"] = a
        aps[name] = nc.dram_tensor(f"in_{name}", a.shape, mybir.dt.from_np(a.dtype), kind="ExternalInput").ap()
    outs = [nc.dram_tensor(f"out_{i}", shape, F32, kind="ExternalOutput").ap() for i, shape in enumerate(_OUTS)]
    i = aps
    build_step(nc, i["x_prompt"], i["x_sample"], [i["cache_a0_kv"], i["cache_a1_kv"], i["cache_a2_kv"]],
               i["cache_b_kv"], i["page_table"], i["norm_g"], i["w_in"], i["q_norm_a"], i["k_norm_a"],
               i["q_norm_b"], i["k_norm_b"], i["lambda_q1"], i["lambda_k1"], i["lambda_q2"], i["lambda_k2"],
               i["subln_g"], i["w_proj_a"], i["w_proj_b"], i["w_out"], i["ident"], i["bias_a"], i["bias_b"],
               i["bias_sa"], i["bias_sb"], i["mask"], i["sel"], i["coef"],
               outs[0], outs[1], outs[2:5], outs[5], outs[6:9], outs[9])
    r = run_bass_kernel_spmd(nc, [arrays], core_ids=[0])
    return tuple(r.results[0][f"out_{k}"] for k in range(len(_OUTS)))
```
